# Optimizing a Trainium2 kernel written in Bass

```python
import math
import jax, jax.numpy as jnp
from jax import lax
import numpy as np

D_MODEL = 1024
BATCH = 1
SEQ = 256
DEPTH = 2

HEAD_DIM = 64
FOX_HEADS = 4
DIL_HEADS = 4
FOX_W = FOX_HEADS * HEAD_DIM
DIL_W = DIL_HEADS * HEAD_DIM
SSD_HEADS = 8
SSD_HEAD_DIM = 64
SSD_INNER = SSD_HEADS * SSD_HEAD_DIM
SSD_GROUPS = 2
SSD_HPG = SSD_HEADS // SSD_GROUPS
SSD_STATE = 128
SSD_CONV = 4
SSD_CHUNK = 128
SSD_CONV_CH = SSD_INNER + 2 * SSD_GROUPS * SSD_STATE
MIX_WIDTH = FOX_W + DIL_W + SSD_INNER
PROJ_SIZES = (FOX_W, FOX_W, FOX_W, FOX_HEADS, DIL_W, DIL_W, DIL_W, SSD_INNER, SSD_CONV_CH, SSD_HEADS)
IN_PROJ = sum(PROJ_SIZES)
Q_BLOCK = 128
DIL_CONFIGS = ((128, 1), (512, 4), (2048, 16))
ROPE_THETA = 500000.0
ROPE_DIM = HEAD_DIM // 4
MEM_LEN = 256
XA_HEADS = 4
XA_HEAD_DIM = D_MODEL // XA_HEADS
N_GROUPS = 4
EXPERTS_PER_GROUP = 8
N_EXPERTS = N_GROUPS * EXPERTS_PER_GROUP
TOP_K = 2
EXPERT_FF = 512
MOE_BLOCK = 128
EPS = 1e-6

kernel_name = "hybrid_fox_dilated_ssd_hmoe"

def rmsnorm(x, g):
    xf = x.astype(jnp.float32)
    y = xf * lax.rsqrt(jnp.mean(xf * xf, axis=-1, keepdims=True) + EPS)
    return (y * g.astype(jnp.float32)).astype(x.dtype)

def rotary_partial(t, pos):
    half = ROPE_DIM // 2
    inv = jnp.power(ROPE_THETA, -2.0 * jnp.arange(half, dtype=jnp.float32) / ROPE_DIM)
    ang = pos.astype(jnp.float32)[:, None] * inv[None, :]
    cos = jnp.cos(ang).astype(t.dtype)
    sin = jnp.sin(ang).astype(t.dtype)
    t1, t2, rest = t[..., :half], t[..., half:ROPE_DIM], t[..., ROPE_DIM:]
    return jnp.concatenate([t1 * cos - t2 * sin, t2 * cos + t1 * sin, rest], axis=-1)

def fox_attention(q, k, v, log_f):
    B, H, S, hd = q.shape
    nb = S // Q_BLOCK
    c = jnp.cumsum(log_f, axis=-1)
    scale = hd ** -0.5
    qb = q.reshape(B, H, nb, Q_BLOCK, hd).transpose(2, 0, 1, 3, 4)
    cb = c.reshape(B, H, nb, Q_BLOCK).transpose(2, 0, 1, 3)
    kpos = jnp.arange(S)

    def block(args):
        qi, ci, bi = args
        s = jnp.einsum("bhqd,bhkd->bhqk", qi, k).astype(jnp.float32) * scale
        s = s + ci[..., :, None] - c[..., None, :]
        qpos = bi * Q_BLOCK + jnp.arange(Q_BLOCK)
        s = jnp.where(kpos[None, :] <= qpos[:, None], s, -jnp.inf)
        p = jax.nn.softmax(s, axis=-1)
        return jnp.einsum("bhqk,bhkd->bhqd", p.astype(v.dtype), v)

    o = lax.map(block, (qb, cb, jnp.arange(nb)))
    return o.transpose(1, 2, 0, 3, 4).reshape(B, H, S, hd)

def dilated_attention(q, k, v):
    B, H, S, hd = q.shape
    scale = hd ** -0.5
    outs, maxes, dens = [], [], []
    for window, dil in DIL_CONFIGS:
        steps = window // dil
        L = S // dil
        nb = -(-L // steps)
        Lp = nb * steps

        def to_res(t):
            t = t.reshape(B, H, L, dil, hd).transpose(0, 1, 3, 2, 4)
            t = jnp.pad(t, ((0, 0), (0, 0), (0, 0), (0, Lp - L), (0, 0)))
            return t.reshape(B, H, dil, nb, steps, hd)

        def band(t):
            prev = jnp.pad(t, ((0, 0), (0, 0), (0, 0), (1, 0), (0, 0), (0, 0)))[:, :, :, :-1]
            return jnp.concatenate([prev, t], axis=4)

        def from_res(t):
            X = t.shape[-1]
            t = t.reshape(B, H, dil, Lp, X)[:, :, :, :L]
            return t.transpose(0, 1, 3, 2, 4).reshape(B, H, S, X)

        qr = to_res(q)
        kb = band(to_res(k))
        vb = band(to_res(v))
        s = jnp.einsum("bhrnqd,bhrnkd->bhrnqk", qr, kb).astype(jnp.float32) * scale
        qi = jnp.arange(steps)[:, None] + steps
        kj = jnp.arange(2 * steps)[None, :]
        dist = qi - kj
        blk = jnp.arange(nb)[:, None, None]
        valid = (dist >= 0) & (dist <= steps) & (blk * steps + kj[None] - steps >= 0)
        s = jnp.where(valid, s, -jnp.inf)
        m = jnp.max(s, axis=-1, keepdims=True)
        e = jnp.exp(s - m)
        den = jnp.sum(e, axis=-1, keepdims=True)
        o = jnp.einsum("bhrnqk,bhrnkd->bhrnqd", (e / den).astype(v.dtype), vb)
        outs.append(from_res(o).astype(jnp.float32))
        maxes.append(from_res(m))
        dens.append(from_res(den))
    ms = jnp.stack(maxes)
    ds = jnp.stack(dens)
    os_ = jnp.stack(outs)
    w = jnp.exp(ms - jnp.max(ms, axis=0, keepdims=True)) * ds
    o = jnp.sum(w * os_, axis=0) / jnp.sum(w, axis=0)
    return o.astype(q.dtype)

def ssd_mixer(z, xbc, dt_raw, conv_w, conv_b, dt_bias, A_log, D_skip, norm_g):
    B, S, _ = z.shape
    G, R, P, N, Q = SSD_GROUPS, SSD_HPG, SSD_HEAD_DIM, SSD_STATE, SSD_CHUNK
    nc = S // Q
    conv = lax.conv_general_dilated(
        xbc, conv_w.reshape(SSD_CONV, 1, SSD_CONV_CH).astype(xbc.dtype),
        window_strides=(1,), padding=((SSD_CONV - 1, 0),),
        dimension_numbers=("NWC", "WIO", "NWC"), feature_group_count=SSD_CONV_CH)
    xbc = jax.nn.silu(conv + conv_b)
    xs = xbc[..., :SSD_INNER].reshape(B, S, G, R, P)
    Bm = xbc[..., SSD_INNER:SSD_INNER + G * N].reshape(B, nc, Q, G, N)
    Cm = xbc[..., SSD_INNER + G * N:].reshape(B, nc, Q, G, N)
    dt = jax.nn.softplus(dt_raw.astype(jnp.float32) + dt_bias.astype(jnp.float32))
    A = -jnp.exp(A_log.astype(jnp.float32))
    dA = (dt * A).reshape(B, nc, Q, G, R).transpose(0, 3, 4, 1, 2)
    Xc = (xs * dt.reshape(B, S, G, R)[..., None]).reshape(B, nc, Q, G, R, P)
    A_cs = jnp.cumsum(dA, axis=-1)
    tri = jnp.tril(jnp.ones((Q, Q), dtype=bool))
    Lmat = jnp.exp(jnp.where(tri, A_cs[..., :, None] - A_cs[..., None, :], -jnp.inf))
    CB = jnp.einsum("bclgn,bcsgn->bcgls", Cm, Bm)
    y_diag = jnp.einsum("bcgls,bgrcls,bcsgrp->bclgrp", CB, Lmat, Xc)
    decay_states = jnp.exp(A_cs[..., -1:] - A_cs)
    states = jnp.einsum("bclgn,bgrcl,bclgrp->bcgrpn", Bm, decay_states, Xc)
    chunk_decay = jnp.exp(A_cs[..., -1])

    def step(h, inp):
        st, dec = inp
        return dec[..., None, None] * h + st, h

    h0 = jnp.zeros((B, G, R, P, N), states.dtype)
    _, h_in = lax.scan(step, h0, (jnp.moveaxis(states, 1, 0), jnp.moveaxis(chunk_decay, -1, 0)))
    h_in = jnp.moveaxis(h_in, 0, 1)
    y_off = jnp.einsum("bclgn,bcgrpn,bgrcl->bclgrp", Cm, h_in, jnp.exp(A_cs))
    y = (y_diag + y_off).reshape(B, S, G, R, P) + xs * D_skip.reshape(G, R, 1)
    y = y.reshape(B, S, SSD_INNER).astype(z.dtype)
    return rmsnorm(y * jax.nn.silu(z), norm_g)

def memory_cross_attention(h, mem_n, wq, wkv, qn_g, kn_g, wo):
    B, S, _ = h.shape
    q = rmsnorm((h @ wq).reshape(B, S, XA_HEADS, XA_HEAD_DIM), qn_g)
    k, v = jnp.split(mem_n @ wkv, 2, axis=-1)
    k = rmsnorm(k.reshape(B, MEM_LEN, XA_HEADS, XA_HEAD_DIM), kn_g)
    v = v.reshape(B, MEM_LEN, XA_HEADS, XA_HEAD_DIM)
    s = jnp.einsum("bshd,bmhd->bhsm", q, k).astype(jnp.float32) * (XA_HEAD_DIM ** -0.5)
    p = jax.nn.softmax(s, axis=-1)
    o = jnp.einsum("bhsm,bmhd->bshd", p.astype(v.dtype), v).reshape(B, S, D_MODEL)
    return o @ wo

def hierarchical_moe(h, wg, bg, we, be, w1, w3, w2):
    B, S, D = h.shape
    T = B * S
    xt = h.reshape(T, D)
    g_logits = (xt @ wg).astype(jnp.float32) + bg
    g_prob = jax.nn.softmax(g_logits, axis=-1)
    g_sel = jnp.argmax(g_logits, axis=-1)
    g_gate = jnp.take_along_axis(g_prob, g_sel[:, None], axis=1)
    e_logits = ((xt @ we).astype(jnp.float32) + be).reshape(T, N_GROUPS, EXPERTS_PER_GROUP)
    e_in = jnp.take_along_axis(e_logits, g_sel[:, None, None], axis=1)[:, 0]
    top_v, top_i = lax.top_k(e_in, TOP_K)
    gates = (jax.nn.softmax(top_v, axis=-1) * g_gate).reshape(T * TOP_K)
    eid = (g_sel[:, None] * EXPERTS_PER_GROUP + top_i).reshape(T * TOP_K)
    tok = jnp.repeat(jnp.arange(T), TOP_K)
    n_assign = T * TOP_K
    order = jnp.argsort(eid)
    s_eid, s_tok, s_gate = eid[order], tok[order], gates[order]
    counts = jnp.bincount(eid, length=N_EXPERTS)
    padded = (counts + MOE_BLOCK - 1) // MOE_BLOCK * MOE_BLOCK
    starts = jnp.cumsum(counts) - counts
    ends_p = jnp.cumsum(padded)
    pstarts = ends_p - padded
    dest = pstarts[s_eid] + jnp.arange(n_assign) - starts[s_eid]
    nblk = (n_assign + MOE_BLOCK - 1) // MOE_BLOCK + N_EXPERTS
    buf = jnp.zeros((nblk * MOE_BLOCK, D), xt.dtype).at[dest].set(xt[s_tok])
    blk_expert = jnp.minimum(jnp.searchsorted(ends_p, jnp.arange(nblk) * MOE_BLOCK, side="right"), N_EXPERTS - 1)

    def run(args):
        xb, e = args
        return (jax.nn.silu(xb @ w1[e]) * (xb @ w3[e])) @ w2[e]

    ybuf = lax.map(run, (buf.reshape(nblk, MOE_BLOCK, D), blk_expert)).reshape(nblk * MOE_BLOCK, D)
    y = jnp.zeros((T, D), xt.dtype).at[s_tok].add(ybuf[dest] * s_gate[:, None].astype(xt.dtype))
    return y.reshape(B, S, D)

def setup_inputs(seed: int = 0) -> dict:
    key = jax.random.key(seed)
    ks = iter(jax.random.split(key, 48))
    L = DEPTH

    def nrm(shape, s):
        return jax.random.normal(next(ks), shape, jnp.float32) * s

    def gain(n):
        return 1.0 + nrm((L, n), 0.02)

    x = nrm((BATCH, SEQ, D_MODEL), 1.0)
    mem = nrm((BATCH, MEM_LEN, D_MODEL), 1.0)
    norm1_g = gain(D_MODEL)
    w_in = nrm((L, D_MODEL, IN_PROJ), D_MODEL ** -0.5)
    fox_fgate_b = jax.random.uniform(next(ks), (L, FOX_HEADS), jnp.float32, 1.0, 4.0)
    fox_qn_g = gain(HEAD_DIM)
    fox_kn_g = gain(HEAD_DIM)
    dil_qn_g = gain(HEAD_DIM)
    dil_kn_g = gain(HEAD_DIM)
    ssd_conv_w = nrm((L, SSD_CONV, SSD_CONV_CH), SSD_CONV ** -0.5)
    ssd_conv_b = nrm((L, SSD_CONV_CH), 0.01)
    dt0 = jnp.exp(jax.random.uniform(next(ks), (L, SSD_HEADS), jnp.float32)
                  * (math.log(0.1) - math.log(0.001)) + math.log(0.001))
    ssd_dt_bias = dt0 + jnp.log(-jnp.expm1(-dt0))
    ssd_A_log = jnp.log(jax.random.uniform(next(ks), (L, SSD_HEADS), jnp.float32, 1.0, 16.0))
    ssd_D = 1.0 + nrm((L, SSD_HEADS), 0.1)
    ssd_norm_g = gain(SSD_INNER)
    w_out = nrm((L, MIX_WIDTH, D_MODEL), MIX_WIDTH ** -0.5)
    norm2_g = gain(D_MODEL)
    mem_norm_g = gain(D_MODEL)
    xa_wq = nrm((L, D_MODEL, D_MODEL), D_MODEL ** -0.5)
    xa_wkv = nrm((L, D_MODEL, 2 * D_MODEL), D_MODEL ** -0.5)
    xa_qn_g = gain(XA_HEAD_DIM)
    xa_kn_g = gain(XA_HEAD_DIM)
    xa_wo = nrm((L, D_MODEL, D_MODEL), D_MODEL ** -0.5)
    norm3_g = gain(D_MODEL)
    router_wg = nrm((L, D_MODEL, N_GROUPS), D_MODEL ** -0.5)
    router_bg = nrm((L, N_GROUPS), 0.01)
    router_we = nrm((L, D_MODEL, N_EXPERTS), D_MODEL ** -0.5)
    router_be = nrm((L, N_EXPERTS), 0.01)
    exp_w1 = nrm((L, N_EXPERTS, D_MODEL, EXPERT_FF), D_MODEL ** -0.5)
    exp_w3 = nrm((L, N_EXPERTS, D_MODEL, EXPERT_FF), D_MODEL ** -0.5)
    exp_w2 = nrm((L, N_EXPERTS, EXPERT_FF, D_MODEL), EXPERT_FF ** -0.5)
    return {"x": x, "mem": mem, "norm1_g": norm1_g, "w_in": w_in, "fox_fgate_b": fox_fgate_b,
            "fox_qn_g": fox_qn_g, "fox_kn_g": fox_kn_g, "dil_qn_g": dil_qn_g, "dil_kn_g": dil_kn_g,
            "ssd_conv_w": ssd_conv_w, "ssd_conv_b": ssd_conv_b, "ssd_dt_bias": ssd_dt_bias,
            "ssd_A_log": ssd_A_log, "ssd_D": ssd_D, "ssd_norm_g": ssd_norm_g, "w_out": w_out,
            "norm2_g": norm2_g, "mem_norm_g": mem_norm_g, "xa_wq": xa_wq, "xa_wkv": xa_wkv,
            "xa_qn_g": xa_qn_g, "xa_kn_g": xa_kn_g, "xa_wo": xa_wo, "norm3_g": norm3_g,
            "router_wg": router_wg, "router_bg": router_bg, "router_we": router_we,
            "router_be": router_be, "exp_w1": exp_w1, "exp_w3": exp_w3, "exp_w2": exp_w2}

def reference(x, mem, norm1_g, w_in, fox_fgate_b, fox_qn_g, fox_kn_g, dil_qn_g, dil_kn_g,
              ssd_conv_w, ssd_conv_b, ssd_dt_bias, ssd_A_log, ssd_D, ssd_norm_g, w_out,
              norm2_g, mem_norm_g, xa_wq, xa_wkv, xa_qn_g, xa_kn_g, xa_wo, norm3_g,
              router_wg, router_bg, router_we, router_be, exp_w1, exp_w3, exp_w2):
    B, S, _ = x.shape
    pos = jnp.arange(S)
    split_idx = np.cumsum(PROJ_SIZES)[:-1].tolist()

    def heads(t, n):
        return t.reshape(B, S, n, -1).transpose(0, 2, 1, 3)

    for l in range(DEPTH):
        h = rmsnorm(x, norm1_g[l])
        (fq, fk, fv, ff, dq, dk, dv, z, xbc, dt_raw) = jnp.split(h @ w_in[l], split_idx, axis=-1)
        fq = rmsnorm(heads(fq, FOX_HEADS), fox_qn_g[l])
        fk = rmsnorm(heads(fk, FOX_HEADS), fox_kn_g[l])
        log_f = jax.nn.log_sigmoid(ff.astype(jnp.float32) + fox_fgate_b[l].astype(jnp.float32)).transpose(0, 2, 1)
        o_fox = fox_attention(fq, fk, heads(fv, FOX_HEADS), log_f)
        dq = rotary_partial(rmsnorm(heads(dq, DIL_HEADS), dil_qn_g[l]), pos)
        dk = rotary_partial(rmsnorm(heads(dk, DIL_HEADS), dil_kn_g[l]), pos)
        o_dil = dilated_attention(dq, dk, heads(dv, DIL_HEADS))
        o_ssd = ssd_mixer(z, xbc, dt_raw, ssd_conv_w[l], ssd_conv_b[l], ssd_dt_bias[l],
                          ssd_A_log[l], ssd_D[l], ssd_norm_g[l])
        mix = jnp.concatenate([o_fox.transpose(0, 2, 1, 3).reshape(B, S, FOX_W),
                               o_dil.transpose(0, 2, 1, 3).reshape(B, S, DIL_W),
                               o_ssd.astype(x.dtype)], axis=-1)
        x = x + mix @ w_out[l]
        h = rmsnorm(x, norm2_g[l])
        m = rmsnorm(mem, mem_norm_g[l])
        x = x + memory_cross_attention(h, m, xa_wq[l], xa_wkv[l], xa_qn_g[l], xa_kn_g[l], xa_wo[l])
        h = rmsnorm(x, norm3_g[l])
        x = x + hierarchical_moe(h, router_wg[l], router_bg[l], router_we[l], router_be[l],
                                 exp_w1[l], exp_w3[l], exp_w2[l])
    return x


_drawn_inputs = setup_inputs


def setup_inputs(seed=0):
    import zlib

    import numpy as np

    out = dict(_drawn_inputs(seed))
    spreads = {}
    factors = {'fox_qn_g': 5.749,
     'fox_kn_g': 4.611,
     'dil_qn_g': 5.934,
     'dil_kn_g': 4.333,
     'norm2_g': 3.494,
     'mem_norm_g': 4.693,
     'xa_qn_g': 8.0,
     'xa_kn_g': 8.0,
     'router_bg': 3.753,
     'router_be': 4.07}
    for name, (base, spread) in spreads.items():
        noise = np.random.default_rng([zlib.crc32(name.encode()), seed]).standard_normal(out[name].shape)
        drawn = base * np.exp(spread * noise) if base else spread * noise
        out[name] = __import__('jax').numpy.asarray(drawn.astype(out[name].dtype))
    for name, factor in factors.items():
        out[name] = (out[name] * factor).astype(out[name].dtype)
    return out
```

```python
from contextlib import ExitStack

import concourse.bass as bass
from concourse import mybir

F32 = mybir.dt.float32
I32 = mybir.dt.int32
ALU = mybir.AluOpType
ACT = mybir.ActivationFunctionType
AX = mybir.AxisListType

P = 128
DEPTH, S, D = 2, 256, 1024
NT = S // P
KC = D // P
HD, NH = 64, 4
SH, SP_, SI = 8, 64, 512
XC = 1024
XH, XD = 4, 256
NE, FF = 32, 512
QUAD = 4
CAP = P // QUAD
NQ = NE // QUAD
NG, EPG = 4, 8
EPS = 1e-6
BIG = 1e30
C_FQK, C_FV, C_DQK, C_DV, C_Z, C_XBC, C_DT = 0, 512, 772, 1284, 1540, 2052, 3076
T_FV, T_FF, T_DQK, T_DV, T_Z, T_DT, T_W = 512, 768, 772, 1284, 1540, 2052, 2060
ROWS = {}
_o = 0
for _n, _w in (("fox_qn_g", HD), ("fox_kn_g", HD), ("dil_qn_g", HD), ("dil_kn_g", HD), ("xa_qn_g", XD),
               ("xa_kn_g", XD), ("fox_fgate_b", NH), ("ssd_dt_bias", SH), ("ssd_A_log", SH), ("ssd_D", SH),
               ("router_bg", NG), ("router_be", NE)):
    ROWS[_n] = (_o, _w)
    _o += _w
ROWS_W = _o
CONST = {}
_o = 0
for _n, _w in (("ident", P), ("tri", 3 * P), ("causal", 2 * P), ("dilated", 3 * P), ("cos", NT * 8),
               ("sin", NT * 8), ("slots", CAP), ("caps", 8), ("down", NE), ("half", 16)):
    CONST[_n] = (_o, _w)
    _o += _w
CONST_W = _o

SLOTS = 6
UNIT = 4096
DENSE = ([("kv", i) for i in range(4)] + [("xbc", 0), ("xbc", 1), ("dt", 0), ("fqk", 0), ("fv", 0), ("dqk", 0),
         ("dv", 0), ("z", 0)] + [("w_out", 0), ("w_out", 1), ("wq", 0), ("wq", 1), ("wo", 0), ("wo", 1)])
DENSE_TURNS = len(DENSE) // SLOTS
assert DENSE_TURNS * SLOTS == len(DENSE)
MOE_UNITS = 12
MOE_TURNS = MOE_UNITS // SLOTS
IN_COLS = {"fqk": (C_FQK, 512), "fv": (C_FV, 260), "dqk": (C_DQK, 512), "dv": (C_DV, 256), "z": (C_Z, 512),
           "dt": (C_DT, 8)}
IN_DEST = {"fqk": 0, "fv": T_FV, "dqk": T_DQK, "dv": T_DV, "z": T_Z, "dt": T_DT}
IN_ORDER = ("dt", "fqk", "fv", "dqk", "dv", "z")

HEADS = [(fam, h) for fam in ("fox", "dil") for h in range(NH)]
L_AHEAD = 2


def list_jobs():
    jobs = [("params",)]
    jobs += [("memT", t, i) for t in range(NT) for i in range(2)]
    jobs += [("kv", n, t) for n in range(4) for t in range(NT)]
    jobs += [("kT", t, i) for t in range(NT) for i in range(2)]
    jobs += [("hT1", t, i) for t in range(NT) for i in range(2)]
    jobs += [("xbc", i) for i in range(4)]
    jobs += [("in", n, t) for n in IN_ORDER for t in range(NT)]
    jobs += [("cum",)]
    jobs += [("fT", t, i) for t in range(NT) for i in range(2)]
    jobs += [("dT", t) for t in range(NT)]
    for k in range(len(HEADS) + 1):
        if k < len(HEADS):
            jobs += [("s", HEADS[k], t) for t in range(NT)]
        if k:
            jobs += [("pT", HEADS[k - 1])]
            if k % 2 == 0:
                jobs += [("o", HEADS[k - 1])]
    jobs += [("xsT", t) for t in range(NT)] + [("cb", g) for g in range(2)]
    jobs += [("y", t) for t in range(NT)] + [("L", h) for h in range(SH)]
    jobs += [("ysT", t) for t in range(NT)]
    jobs += [("out1", n, t) for n in range(2) for t in range(NT)]
    jobs += [("hT2", t, i) for t in range(NT) for i in range(2)]
    jobs += [("q", n, t) for n in range(2) for t in range(NT)]
    jobs += [("qT", t, i) for t in range(NT) for i in range(2)]
    for h in range(XH + 1):
        if h < XH:
            jobs += [("xs", h, t) for t in range(NT)]
        if h:
            jobs += [("xpT", h - 1), ("xo", h - 1)]
    jobs += [("out2", n, t) for n in range(2) for t in range(NT)]
    jobs += [("hT3", t, i) for t in range(NT) for i in range(2)]
    return jobs + [("router",), ("rank",)]


NB = 8


def plan_banks():
    place, uses, n, held = {}, [0] * NB, 0, set()
    for job in list_jobs():
        while n % NB in held:
            n += 1
        b = n % NB
        place[job] = (b, uses[b])
        uses[b] += 1
        if job[0] == "y":
            held.add(b)
        if job == ("L", SH - 1):
            held.clear()
        n += 1
    return place, uses


PLACE, USES = plan_banks()
LAST_USE = {"kv": lambda i: ("kv", i, 1), "xbc": lambda i: ("xbc", 2 * i + 1), "w_out": lambda i: ("out1", i, 1),
            "wq": lambda i: ("q", i, 1), "wo": lambda i: ("out2", i, 1)}
N_PARAMS = 4 + 3 + len(ROWS) + 2
V_STEPS, A_STEPS, G_STEPS = 128, 2, 12
V_MOE = 4
G_X, G_MEM, G_2, G_3 = 0, 1, 2, 3


def last_use(unit):
    kind, i = unit
    return LAST_USE[kind](i) if kind in LAST_USE else ("in", kind, 1)


def trunk(nc, a, out):
    with ExitStack() as ctx:
        def sb(name, shape, dt=F32):
            return ctx.enter_context(nc.sbuf_tensor(name, shape, dt))

        per_layer = {}

        def sem(name, n=0):
            s = ctx.enter_context(nc.semaphore(name))
            per_layer[s] = n
            return s

        def at(s, l, n):
            return l * per_layer[s] + n

        ring = sb("ring", [P, SLOTS, UNIT])
        X = sb("X", [P, NT, D])
        H = sb("H", [P, NT, KC, P])
        HT = sb("HT", [P, KC, S])
        XBC = sb("XBC", [P, KC, S])
        proj = sb("proj", [P, NT * T_W])
        XBCp = sb("XBCp", [P, KC * (S + 3)])
        XS = sb("XS", [P, NT, SI])
        Y = sb("Y", [P, NT, SI])
        FQ = sb("FQ", [P, NT, 2 * NH, HD + 2])
        FQT = sb("FQT", [P, 2 * NH, S])
        DQT = sb("DQT", [P, 4, S])
        KT = sb("KT", [P, KC, S])
        VM = sb("VM", [P, NT, D])
        SCO = sb("SCO", [P, 2, NT, S])
        row = sb("row", [P, ROWS_W])
        con = sb("con", [P, CONST_W])
        g_ch = sb("g_ch", [P, 4, KC])
        p_rows = sb("p_rows", [44, P])
        p_ch = sb("p_ch", [P, 44])
        wr = sb("wr", [P, KC, NG + NE])
        ss = sb("ss", [P, 6])
        ssk = sb("ssk", [P, NT, XH])
        ssf = sb("ssf", [P, NT, 16])
        smax = sb("smax", [P, 2, NT])
        ssum = sb("ssum", [P, 2, NT])
        gate_in = sb("gate_in", [P, NT, 12])
        gate_e = sb("gate_e", [P, NT, 12])
        DL = sb("DL", [P, NT, 12])
        DTs = sb("DTs", [P, NT, SH])
        CUM = sb("CUM", [P, NT, 12])
        negA = sb("negA", [P, SH])
        rt = sb("rt", [P, NT, 8])
        rg = sb("rg", [P, NT, 4, NG])
        passes = sb("passes", [P, 2])
        passes_i = sb("passes_i", [P, DEPTH + 1], I32)
        over = sb("over", [P, 8])
        slot_no = sb("slot_no", [P, CAP])

        def view(buf, off, *shape):
            n = 1
            for x in shape:
                n *= x
            v = buf[:, off:off + n]
            if len(shape) == 1:
                return v
            names = "abcd"[:len(shape)]
            return v.rearrange(f"p ({' '.join(names)}) -> p {' '.join(names)}", **dict(zip(names, shape)))

        def ring_view(s, w):
            return view(ring[:, s, :], 0, KC, w)

        fqt_flat = FQT[:, :, :].rearrange("p a b -> p (a b)")
        pt = [proj[:, t * T_W:(t + 1) * T_W] for t in range(NT)]
        mem_raw = view(fqt_flat, 0, NT, D)
        K_tm = view(fqt_flat, 0, NT, D)
        MN = view(XBCp, 0, NT, KC, P)
        xin = view(XBCp, 0, KC, S + 3)
        MT = XBC[:, :, :]
        mixT = H[:, :, :, :].rearrange("p t c q -> p (t c q)").rearrange("p (c s) -> p c s", c=KC)
        Q_tm = view(proj, 0, NT, D)
        QT = HT[:, :, :]
        sq = view(SCO[:, :, :, :].rearrange("p a b c -> p (a b c)"), 0, 1024)
        rope = view(XS[:, :, :].rearrange("p a b -> p (a b)"), 0, 4, 2 * NH, 8)
        dqt_flat = DQT[:, :, :].rearrange("p a b -> p (a b)")
        lg = view(dqt_flat, 0, NT, NG + NE)
        first = view(dqt_flat, 128, NT, NE)
        em = view(dqt_flat, 192, NT, NE)
        oh = view(dqt_flat, 256, 2, NT, NE)
        gates = view(dqt_flat, 384, NT, NE)
        chosen = view(dqt_flat, 448, NT, NE)
        rank = view(dqt_flat, 512, NT, NE)
        ht_flat = HT[:, :, :].rearrange("p a b -> p (a b)")
        sig = view(ht_flat, 0, 2, S)
        ve = view(ht_flat, 512, 512)
        Ls = view(ht_flat, 1024, 2, 3 * P)
        Ms = view(fqt_flat, 0, 2, 3 * P)
        CB = view(fqt_flat, 1024, 2, 3 * P)
        Yf = Y[:, :, :].rearrange("p t n -> p (t n)")
        PT = view(Yf, 0, 2, 2 * S)
        junk = (sq, Yf)
        XG = view(proj, 0, KC, P)
        SEL = view(proj, 1024, NT, QUAD, CAP)
        SELG = view(proj, 1280, NT, QUAD, CAP)
        SELT = view(proj, 1536, S)
        HID = view(proj, 1792, 4, P)
        SIGM = view(proj, 2304, FF)
        HIDT = view(proj, 2816, 4, P)
        YS = XS[:, :, :].rearrange("p t n -> p (t n)")

        def c_(name, *shape):
            o, w = CONST[name]
            return view(con, o, *(shape or (w,)))

        def r_(name, *shape):
            o, w = ROWS[name]
            return view(row, o, *(shape or (w,)))

        def bc(ap, *shape):
            return ap.unsqueeze(len(ap.shape)).to_broadcast([P, *shape])

        ident, tri = c_("ident"), c_("tri")
        ones = tri[:, P:2 * P]

        bank = [ctx.enter_context(nc.psum_tensor(f"bank{b}", [P, 512], F32)) for b in range(NB)]
        B_GATH, B_SELT, B_UP, B_HIDT, B_DOWN, B_SCAT = (0, 1), 2, (3, 4), 5, (6, 7), (0, 1, 3, 4)

        bank_full = [sem(f"bank_full{b}", USES[b]) for b in range(NB)]
        bank_read = [sem(f"bank_read{b}", USES[b]) for b in range(NB)]
        landed = [sem(f"landed{s}") for s in range(SLOTS)]
        x_in, const_in = sem("x_in"), sem("const_in")
        params_in = sem("params_in", 16 * N_PARAMS)
        mem_in = sem("mem_in", 16)
        vector_layer = sem("vector_layer", 1)
        scalar_layer = sem("scalar_layer", 1)
        passes_known = sem("passes_known", 1)
        v_step = sem("v_step", V_STEPS)
        a_step = sem("a_step", A_STEPS)
        g_step = sem("g_step", G_STEPS)
        mem_ss, mem_rs = sem("mem_ss", 1), sem("mem_rs", 1)
        k_ss, k_rs = sem("k_ss", NT), sem("k_rs", NT)
        q_ss, q_rs = sem("q_ss", NT), sem("q_rs", NT)
        x_ss, x_rs = sem("x_ss", 3), sem("x_rs", 3)
        fd_sq = sem("fd_sq", NT)
        fd_ss, fd_rs = sem("fd_ss", NT), sem("fd_rs", NT)
        y_ss, y_rs = sem("y_ss", NT), sem("y_rs", NT)
        MN_ready = sem("MN_ready", 1)
        k_normed, q_normed = sem("k_normed", NT), sem("q_normed", NT)
        X_ready = sem("X_ready", 2)
        H_ready = sem("H_ready", 3 * NT)
        pads = sem("pads", 1)
        conv_done = sem("conv_done", KC)
        sig_exp = sem("sig_exp", KC)
        conv_gated = sem("conv_gated", KC)
        gate_abs, gate_ln = sem("gate_abs", 1), sem("gate_ln", 1)
        DL_ready = sem("DL_ready", 1)
        FQ_ready, DQ_ready = sem("FQ_ready", NT), sem("DQ_ready", NT)
        scores = sem("scores", 4 * NH)
        exps = sem("exps", 4 * NH)
        probs = sem("probs", 4 * NH)
        decays = sem("decays", SH)
        M_ready = sem("M_ready", SH)
        y_head = sem("y_head", SH - 1)
        z_exp = sem("z_exp", NT)
        Y_ready = sem("Y_ready", NT)
        xmax = sem("xmax", 2 * XH)
        xprobs = sem("xprobs", 2 * XH)
        g_shift, g_exp = sem("g_shift", 1), sem("g_exp", 1)
        e_shift, e_exp = sem("e_shift", 1), sem("e_exp", 1)
        chosen_ready = sem("chosen_ready", 1)
        units_used = sem("units_used")
        sel_ready, selg_ready = sem("sel_ready"), sem("selg_ready")
        gath_full, XG_ready = sem("gath_full"), sem("XG_ready")
        selt_full, SELT_ready = sem("selt_full"), sem("SELT_ready")
        up_exp, hid_ready = sem("up_exp"), sem("hid_ready")
        hidt_full, HIDT_ready = sem("hidt_full"), sem("HIDT_ready")
        YS_ready = sem("YS_ready")
        scat_full = sem("scat_full")
        v_moe = sem("v_moe")
        x_out = sem("x_out")
        waits_passed = sem("waits_passed")

        def bk(job):
            return bank[PLACE[job][0]]

        def full(job, l):
            b, k = PLACE[job]
            return bank_full[b], at(bank_full[b], l, k + 1)

        def free(job, l):
            b, k = PLACE[job]
            return bank_read[b], at(bank_read[b], l, k + 1)

        def copied(job, l):
            b, k = PLACE[job]
            return bank_read[b], at(bank_read[b], l, k + 2)

        def filled(job):
            return bank_full[PLACE[job][0]]

        def read(job):
            return bank_read[PLACE[job][0]]

        def alone(eng):
            eng.sem_inc(waits_passed, 1)

        def load_passes(eng, l):
            return eng.value_load(passes_i[0:1, bass.ds(l, 1)], min_val=0, max_val=8 * DEPTH)

        def moe_quads(eng, l, quad, head=None, new_pass=None):
            before = load_passes(eng, l)
            if head:
                head(0, before * NQ)
            with eng.Fori(1 if head else 0, NQ) as q:
                quad(q, before * NQ + q)
            eng.wait_ge(passes_known, at(passes_known, l, 2))
            alone(eng)
            more = eng.snap(load_passes(eng, l + 1) - before)
            with eng.If(more > 1):
                with eng.Fori(1, more) as ps:
                    if new_pass:
                        new_pass()
                    with eng.Fori(0, NQ) as q:
                        quad(q, (before + ps) * NQ + q)

        block = ctx.enter_context(nc.Block())

        @block.sync
        def _(sp):
            sp.dma_start(X[:, :, :], a["x"][0].rearrange("(t p) d -> p t d", p=P)).then_inc(x_in, 16)
            sp.dma_start(con[:, :], a["const"]).then_inc(const_in, 16)

            def dense(kind, i, l):
                name = {"kv": "xa_wkv", "wq": "xa_wq", "w_out": "w_out", "wo": "xa_wo"}.get(kind, "w_in")
                c0, w = IN_COLS.get(kind, (C_XBC if kind == "xbc" else 0, 512))
                rows = "a (c p) n -> p (a c) n" if kind in ("w_out", "wo") else "a (p c) n -> p (a c) n"
                v = a[name][bass.ds(l, 1)].rearrange(rows, c=KC)
                return w, v[:, :, c0 + i * 512:c0 + i * 512 + w]

            with sp.Fori(0, DEPTH) as l:
                sp.wait_ge(passes_known, at(passes_known, l, 1))
                quads_before = sp.snap(load_passes(sp, l) * NQ)
                for n, (kind, i) in enumerate(DENSE):
                    if n < SLOTS:
                        sp.wait_ge(units_used, quads_before * MOE_UNITS + SLOTS + n + 1)
                        alone(sp)
                    else:
                        sp.wait_ge(*full(last_use(DENSE[n - SLOTS]), l))
                        alone(sp)
                    w, src = dense(kind, i, l)
                    sp.dma_start(ring_view(n % SLOTS, w), src).then_inc(landed[n % SLOTS], 16)

                def quad(q, quads, head=False):
                    for n in range(MOE_UNITS):
                        name, i = ("exp_w1", "exp_w3", "exp_w2")[n // 4], n % 4
                        w = a[name][bass.ds(l, 1)].rearrange("a e k n -> (a e) k n")[bass.ds(q * QUAD, QUAD)]
                        if name == "exp_w2":
                            src = w.rearrange("e (p c) n -> p e c n", c=4)[:, :, i, :]
                        else:
                            src = w.rearrange("e (p c) n -> p e (c n)", c=KC)[:, :, i * 1024:(i + 1) * 1024]
                        if head and n < SLOTS:
                            sp.wait_ge(*full(last_use(DENSE[len(DENSE) - SLOTS + n]), l))
                            alone(sp)
                        sp.wait_ge(units_used, quads * MOE_UNITS + SLOTS + n + 1)
                        sp.dma_start(ring[:, n % SLOTS, :].rearrange("p (e n) -> p e n", e=QUAD), src
                                     ).then_inc(landed[n % SLOTS], 16)
                moe_quads(sp, l, quad, head=lambda q, quads: quad(q, quads, head=True))
            sp.wait_ge(vector_layer, DEPTH + 1)
            sp.dma_start(out[0].rearrange("(t p) d -> p t d", p=P), X[:, :, :]).then_inc(x_out, 16)
            sp.wait_ge(x_out, 16)

        @block.gpsimd
        def _(pool):
            pool.wait_ge(const_in, 16)
            with pool.Fori(0, DEPTH) as l:
                steps = [0]

                def rsqrt(ap, n):
                    alone(pool)
                    nc.gpsimd.tensor_scalar(ap, ap, 1.0 / n, EPS, ALU.mult, ALU.add).then_inc(g_step, 1)
                    steps[0] += 1
                    pool.wait_ge(g_step, at(g_step, l, steps[0]))
                    k = ap.free_size()
                    return nc.gpsimd.tensor_tensor(ap, ap, c_("half", 16)[:, 0:k], ALU.pow)

                def load(dst, src, done):
                    pool.dma_start(dst, src).then_inc(done, 16)

                pool.wait_ge(vector_layer, at(vector_layer, l, 1))
                pool.wait_ge(scalar_layer, at(scalar_layer, l, 1))
                alone(pool)

                def layer(name):
                    return a[name][bass.ds(l, 1)]

                load(mem_raw, a["mem"][0].rearrange("(t p) d -> p t d", p=P), mem_in)
                for i, n in enumerate(("norm1_g", "mem_norm_g", "norm2_g", "norm3_g")):
                    load(g_ch[:, i, :], layer(n).rearrange("a (p c) -> p (a c)", c=KC), params_in)
                load(p_rows[0:32, :], layer("ssd_conv_w").rearrange("a k (c p) -> (a k c) p", p=P), params_in)
                load(p_rows[32:40, :], layer("ssd_conv_b").rearrange("a (c p) -> (a c) p", p=P), params_in)
                load(p_rows[40:44, :], layer("ssd_norm_g").rearrange("a (c p) -> (a c) p", p=P), params_in)
                for n in ROWS:
                    load(r_(n), layer(n).to_broadcast([P, ROWS[n][1]]), params_in)
                load(wr[:, :, 0:NG], layer("router_wg").rearrange("a (p c) n -> p (a c) n", c=KC), params_in)
                load(wr[:, :, NG:], layer("router_we").rearrange("a (p c) n -> p (a c) n", c=KC), params_in)

                pool.wait_ge(mem_ss, at(mem_ss, l, 1))
                rsqrt(ss[:, 0:2], D).then_inc(mem_rs, 1)
                for t in range(NT):
                    pool.wait_ge(k_ss, at(k_ss, l, t + 1))
                    rsqrt(ssk[:, t, :], XD).then_inc(k_rs, 1)
                pool.wait_ge(x_ss, at(x_ss, l, 1))
                rsqrt(ss[:, 2:4], D).then_inc(x_rs, 1)
                for t in range(NT):
                    pool.wait_ge(fd_ss, at(fd_ss, l, t + 1))
                    rsqrt(ssf[:, t, :], HD).then_inc(fd_rs, 1)
                for t in range(NT):
                    pool.wait_ge(y_ss, at(y_ss, l, t + 1))
                    rsqrt(ss[:, 4 + t:5 + t], SI).then_inc(y_rs, 1)
                pool.wait_ge(x_ss, at(x_ss, l, 2))
                rsqrt(ss[:, 2:4], D).then_inc(x_rs, 1)
                for t in range(NT):
                    pool.wait_ge(q_ss, at(q_ss, l, t + 1))
                    rsqrt(ssk[:, t, :], XD).then_inc(q_rs, 1)
                pool.wait_ge(x_ss, at(x_ss, l, 3))
                rsqrt(ss[:, 2:4], D).then_inc(x_rs, 1)
                assert steps[0] == G_STEPS, steps

        @block.scalar
        def _(act):
            act.wait_ge(x_in, 16)
            with act.Fori(0, DEPTH) as l:
                steps = [0]

                def link(ins):
                    steps[0] += 1
                    ins.then_inc(a_step, 1)
                    act.wait_ge(a_step, at(a_step, l, steps[0]))

                def copy_out(job, dst, src):
                    act.wait_ge(*full(job, l))
                    nc.scalar.copy(dst, src).then_inc(read(job), 1)

                def norm_x(k, x_k):
                    if x_k:
                        act.wait_ge(X_ready, at(X_ready, l, x_k))
                    for t in range(NT):
                        last = nc.scalar.activation(junk[t], X[:, t, :], ACT.Square, accum_out=ss[:, 2 + t:3 + t])
                    last.then_inc(x_ss, 1)
                    act.wait_ge(x_rs, at(x_rs, l, k + 1))
                    nc.scalar.activation(H[:, 0], X[:, 0, :].rearrange("p (q c) -> p c q", c=KC), ACT.Copy,
                                         scale=ss[:, 2:3]).then_inc(H_ready, 1)

                act.wait_ge(vector_layer, at(vector_layer, l, 1))
                act.wait_ge(mem_in, at(mem_in, l, 16))
                for t in range(NT):
                    last = nc.scalar.activation(junk[t], mem_raw[:, t, :], ACT.Square, accum_out=ss[:, t:t + 1])
                last.then_inc(mem_ss, 1)
                act.wait_ge(mem_rs, at(mem_rs, l, 1))
                for t in range(NT):
                    last = nc.scalar.activation(MN[:, t], mem_raw[:, t, :].rearrange("p (q c) -> p c q", c=KC),
                                                ACT.Copy, scale=ss[:, t:t + 1])
                last.then_inc(MN_ready, 1)
                act.wait_ge(params_in, at(params_in, l, 16 * N_PARAMS))
                link(nc.scalar.activation(negA[:, :], r_("ssd_A_log"), ACT.Exp))
                for n in range(4):
                    for t in range(NT):
                        copy_out(("kv", n, t), (K_tm if n < 2 else VM)[:, t, n % 2 * 512:n % 2 * 512 + 512],
                                 bk(("kv", n, t))[:, :])
                for t in range(NT):
                    act.wait_ge(*copied(("kv", 0, t), l))
                    act.wait_ge(*copied(("kv", 1, t), l))
                    for h in range(XH):
                        part = slice(h * XD, (h + 1) * XD)
                        last = nc.scalar.activation(junk[t][:, part], K_tm[:, t, part], ACT.Square,
                                                    accum_out=ssk[:, t, h:h + 1])
                    last.then_inc(k_ss, 1)
                act.wait_ge(k_ss, at(k_ss, l, NT))
                norm_x(0, 0)
                act.wait_ge(pads, at(pads, l, 1))
                for i in range(4):
                    job = ("xbc", i)
                    copy_out(job, xin[:, 2 * i:2 * i + 2, 3:], bk(job)[:, :].rearrange("p (c s) -> p c s", c=2))
                for n in IN_ORDER:
                    for t in range(NT):
                        w = IN_COLS[n][1]
                        copy_out(("in", n, t), pt[t][:, IN_DEST[n]:IN_DEST[n] + w], bk(("in", n, t))[:, 0:w])
                    if n == "fv":
                        act.wait_ge(gate_abs, at(gate_abs, l, 1))
                        link(nc.scalar.activation(gate_e[:, :, :], gate_e[:, :, :], ACT.Exp))
                        nc.scalar.activation(gate_e[:, :, :], gate_e[:, :, :], ACT.Ln, bias=1.0).then_inc(gate_ln, 1)
                    if n == "dqk":
                        for t in range(NT):
                            dst = junk[t]
                            act.wait_ge(*copied(("in", "fqk", t), l))
                            act.wait_ge(*copied(("in", "dqk", t), l))
                            nc.scalar.activation(dst[:, 0:512], pt[t][:, 0:512], ACT.Square)
                            nc.scalar.activation(dst[:, 512:1024], pt[t][:, T_DQK:T_DQK + 512], ACT.Square
                                                 ).then_inc(fd_sq, 1)

                def exp_scores(k):
                    for t in range(NT):
                        act.wait_ge(scores, at(scores, l, 2 * k + t + 1))
                        w = (t + 1) * P
                        nc.scalar.activation(SCO[:, k % 2, t, 0:w], SCO[:, k % 2, t, 0:w], ACT.Exp,
                                             bias=smax[:, k % 2, t:t + 1], accum_out=ssum[:, k % 2, t:t + 1]
                                             ).then_inc(exps, 1)

                for t in range(NT):
                    for i in range(2):
                        job = ("fT", t, i)
                        copy_out(job, FQT[0:HD + 2, 4 * i:4 * i + 4, t * P:(t + 1) * P],
                                 bk(job)[0:HD + 2, :].rearrange("p (c s) -> p c s", c=4))
                for t in range(NT):
                    job = ("dT", t)
                    copy_out(job, DQT[:, :, t * P:(t + 1) * P], bk(job)[:, :].rearrange("p (c s) -> p c s", c=4))
                exp_scores(0)
                for k, head in enumerate(HEADS):
                    if k + 1 < len(HEADS):
                        exp_scores(k + 1)
                    act.wait_ge(conv_done, at(conv_done, l, k + 1))
                    nc.scalar.activation(sig[:, k % 2, :], XBC[:, k, :], ACT.Exp, scale=-1.0).then_inc(sig_exp, 1)
                    copy_out(("pT", head), PT[:, k % 2, 0:3 * P], bk(("pT", head))[:, 0:3 * P])
                    if k % 2:
                        copy_out(("o", head), mixT[:, k // 2, :], bk(("o", head))[:, 0:S])
                for t in range(NT):
                    copy_out(("xsT", t), XS[:, t, :], bk(("xsT", t))[:, :])
                for t in range(NT):
                    act.wait_ge(*copied(("in", "z", t), l))
                    nc.scalar.activation(sq[:, t * SI:(t + 1) * SI], pt[t][:, T_Z:T_Z + SI], ACT.Exp, scale=-1.0
                                         ).then_inc(z_exp, 1)
                for h in range(SH):
                    act.wait_ge(*copied(("L", h), l))
                    nc.scalar.activation(Ls[:, h % 2, :], Ls[:, h % 2, :], ACT.Exp).then_inc(decays, 1)
                norm_x(1, 1)
                for n in range(2):
                    for t in range(NT):
                        copy_out(("q", n, t), Q_tm[:, t, n * 512:(n + 1) * 512], bk(("q", n, t))[:, :])
                for t in range(NT):
                    act.wait_ge(*copied(("q", 0, t), l))
                    act.wait_ge(*copied(("q", 1, t), l))
                    for h in range(XH):
                        part = slice(h * XD, (h + 1) * XD)
                        last = nc.scalar.activation(junk[t][:, part], Q_tm[:, t, part], ACT.Square,
                                                    accum_out=ssk[:, t, h:h + 1])
                    last.then_inc(q_ss, 1)

                def exp_cross(h):
                    for t in range(NT):
                        act.wait_ge(xmax, at(xmax, l, 2 * h + t + 1))
                        nc.scalar.activation(SCO[:, h % 2, t, :], bk(("xs", h, t))[:, 0:S], ACT.Exp,
                                             bias=smax[:, h % 2, t:t + 1], scale=XD ** -0.5,
                                             accum_out=ssum[:, h % 2, t:t + 1]).then_inc(read(("xs", h, t)), 1)

                exp_cross(0)
                for h in range(XH):
                    if h + 1 < XH:
                        exp_cross(h + 1)
                    copy_out(("xpT", h), PT[:, h % 2, :], bk(("xpT", h))[:, :])
                    copy_out(("xo", h), mixT[:, 2 * h:2 * h + 2, :],
                             bk(("xo", h))[:, :].rearrange("p (c s) -> p c s", c=2))
                norm_x(2, 2)
                act.wait_ge(g_shift, at(g_shift, l, 1))
                nc.scalar.activation(rg[:, :, 1, :], rg[:, :, 1, :], ACT.Exp).then_inc(g_exp, 1)
                act.wait_ge(e_shift, at(e_shift, l, 1))
                nc.scalar.activation(rt[:, :, 4:5], rt[:, :, 4:5], ACT.Exp).then_inc(e_exp, 1)
                assert steps[0] == A_STEPS, ("A", steps)

                def quad(q, quads):
                    act.wait_ge(selt_full, quads + 1)
                    nc.scalar.copy(SELT, bank[B_SELT][:, 0:S]).then_inc(SELT_ready, 1)
                    act.wait_ge(units_used, quads * MOE_UNITS + MOE_UNITS + 4)
                    nc.scalar.activation(SIGM, bank[B_UP[0]][:, :], ACT.Exp, scale=-1.0).then_inc(up_exp, 1)
                    act.wait_ge(hidt_full, quads + 1)
                    nc.scalar.copy(HIDT, bank[B_HIDT][:, :].rearrange("p (c s) -> p c s", c=4)).then_inc(HIDT_ready, 1)
                    act.wait_ge(units_used, quads * MOE_UNITS + MOE_UNITS + 12)
                    for n in range(2):
                        last = nc.scalar.copy(YS[:, n * 512:(n + 1) * 512], bank[B_DOWN[n]][:, :])
                    last.then_inc(YS_ready, 1)
                moe_quads(act, l, quad)
                act.sem_inc(scalar_layer, 1)

        @block.vector
        def _(dve):
            v = nc.vector
            dve.wait_ge(const_in, 16)
            v.memset(passes[:, :], 0.0)
            v.memset(FQ[:, :, 0:NH, HD:HD + 1], 1.0)
            v.memset(FQ[:, :, NH:, HD + 1:HD + 2], 1.0)
            v.memset(passes_i[:, :], 0).then_inc(passes_known, 1)
            for b in range(NB):
                dve.sem_inc(bank_read[b], 1)
            dve.sem_inc(vector_layer, 1)
            dve.sem_inc(scalar_layer, 1)
            dve.sem_inc(units_used, MOE_UNITS)
            with dve.Fori(0, DEPTH) as l:
                steps = [0]

                def link(ins):
                    steps[0] += 1
                    ins.then_inc(v_step, 1)
                    dve.wait_ge(v_step, at(v_step, l, steps[0]))

                def gained(job, gain, dst):
                    dve.wait_ge(*full(job, l))
                    v.tensor_tensor(dst, bk(job)[:, :].rearrange("p (c s) -> p c s", c=4), bc(gain, 4, P), ALU.mult
                                    ).then_inc(read(job), 1)

                def copy4(job, dst):
                    dve.wait_ge(*full(job, l))
                    v.tensor_copy(dst, bk(job)[:, :].rearrange("p (c s) -> p c s", c=4)).then_inc(read(job), 1)

                def norm_x(k, gain, name):
                    dve.wait_ge(x_rs, at(x_rs, l, k + 1))
                    v.tensor_scalar(H[:, 1], X[:, 1, :].rearrange("p (q c) -> p c q", c=KC), ss[:, 3:4], None,
                                    ALU.mult).then_inc(H_ready, 1)
                    for t in range(NT):
                        for i in range(2):
                            gained((name, t, i), g_ch[:, gain, 4 * i:4 * i + 4],
                                   HT[:, 4 * i:4 * i + 4, t * P:(t + 1) * P])

                def head_norm(t, tm, gain, rs_sem, done):
                    dve.wait_ge(rs_sem, at(rs_sem, l, t + 1))
                    for h in range(XH):
                        part = tm[:, t, h * XD:(h + 1) * XD]
                        last = v.scalar_tensor_tensor(part, part, ssk[:, t, h:h + 1], r_(gain), ALU.mult, ALU.mult)
                    last.then_inc(done, 1)

                dve.wait_ge(params_in, at(params_in, l, 16 * N_PARAMS))
                dve.wait_ge(*full(("params",), l))
                v.tensor_copy(p_ch[:, :], bk(("params",))[:, 0:44]).then_inc(read(("params",)), 1)
                for t in range(NT):
                    for i in range(2):
                        gained(("memT", t, i), g_ch[:, G_MEM, 4 * i:4 * i + 4],
                               MT[:, 4 * i:4 * i + 4, t * P:(t + 1) * P])
                v.memset(xin[:, :, 0:3], 0.0).then_inc(pads, 1)
                for t in range(NT):
                    head_norm(t, K_tm, "xa_kn_g", k_rs, k_normed)
                for t in range(NT):
                    for i in range(2):
                        copy4(("kT", t, i), KT[:, 4 * i:4 * i + 4, t * P:(t + 1) * P])
                norm_x(0, G_X, "hT1")

                for t in range(NT):
                    dve.wait_ge(*copied(("in", "dt", t), l))
                    dve.wait_ge(*copied(("in", "fv", t), l))
                    v.tensor_tensor(gate_in[:, t, 0:NH], pt[t][:, T_FF:T_FF + NH], r_("fox_fgate_b"), ALU.add)
                    last = v.tensor_tensor(gate_in[:, t, NH:], pt[t][:, T_DT:T_DT + SH], r_("ssd_dt_bias"), ALU.add)
                link(last)
                link(v.tensor_scalar(gate_e[:, :, :], gate_in[:, :, :], -1.0, None, ALU.mult))
                v.tensor_tensor(gate_e[:, :, :], gate_e[:, :, :], gate_in[:, :, :], ALU.min).then_inc(gate_abs, 1)
                dve.wait_ge(gate_ln, at(gate_ln, l, 1))
                v.scalar_tensor_tensor(DL[:, :, 0:NH], gate_in[:, :, 0:NH], 0.0, gate_e[:, :, 0:NH], ALU.min,
                                       ALU.subtract)
                link(v.scalar_tensor_tensor(DTs[:, :, :], gate_in[:, :, NH:], 0.0, gate_e[:, :, NH:], ALU.max,
                                            ALU.add))
                v.scalar_tensor_tensor(DL[:, :, NH:], DTs[:, :, :], -1.0,
                                       negA[:, :].unsqueeze(1).to_broadcast([P, NT, SH]), ALU.mult, ALU.mult
                                       ).then_inc(DL_ready, 1)
                for t in range(NT):
                    dve.wait_ge(fd_sq, at(fd_sq, l, t + 1))
                    sqs = view(junk[t], 0, 16, HD)
                    v.tensor_reduce(ssf[:, t, :], sqs, AX.X, ALU.add).then_inc(fd_ss, 1)
                job = ("cum",)
                dve.wait_ge(*full(job, l))
                link(v.tensor_copy(CUM[:, :, :], bk(job)[:, 0:NT * 12].rearrange("p (t n) -> p t n", t=NT)))
                v.tensor_scalar(FQ[:, :, 0:NH, HD + 1], CUM[:, :, 0:NH], HD ** 0.5, None, ALU.mult)
                v.tensor_scalar(FQ[:, :, NH:, HD], CUM[:, :, 0:NH], -HD ** 0.5, None, ALU.mult
                                ).then_inc(read(job), 1)
                for t in range(NT):
                    dve.wait_ge(fd_rs, at(fd_rs, l, t + 1))
                    link(v.tensor_tensor(FQ[:, t, :, 0:HD], view(pt[t], 0, 2 * NH, HD), bc(ssf[:, t, 0:8], 8, HD),
                                         ALU.mult))
                    fq = FQ[:, t, :, 0:HD].rearrange("p (b h) d -> p b h d", b=2)
                    gain = r_("fox_qn_g", HD).shape and view(row, ROWS["fox_qn_g"][0], 2, HD)
                    v.tensor_tensor(fq, fq, gain.unsqueeze(2).to_broadcast([P, 2, NH, HD]), ALU.mult
                                    ).then_inc(FQ_ready, 1)
                for t in range(NT):
                    dq = view(pt[t], T_DQK, 2 * NH, HD)
                    link(v.tensor_tensor(dq, dq, bc(ssf[:, t, 8:16], 8, HD), ALU.mult))
                    d4 = view(pt[t], T_DQK, 2, NH, HD)
                    gain = view(row, ROWS["dil_qn_g"][0], 2, HD)
                    link(v.tensor_tensor(d4, d4, gain.unsqueeze(2).to_broadcast([P, 2, NH, HD]), ALU.mult))
                    cos = view(con, CONST["cos"][0] + 8 * t, 8).unsqueeze(1).to_broadcast([P, 8, 8])
                    sin = view(con, CONST["sin"][0] + 8 * t, 8).unsqueeze(1).to_broadcast([P, 8, 8])
                    v.tensor_tensor(rope[:, 0], dq[:, :, 0:8], cos, ALU.mult)
                    v.tensor_tensor(rope[:, 1], dq[:, :, 8:16], sin, ALU.mult)
                    v.tensor_tensor(rope[:, 2], dq[:, :, 8:16], cos, ALU.mult)
                    link(v.tensor_tensor(rope[:, 3], dq[:, :, 0:8], sin, ALU.mult))
                    v.tensor_tensor(dq[:, :, 0:8], rope[:, 0], rope[:, 1], ALU.subtract)
                    v.tensor_tensor(dq[:, :, 8:16], rope[:, 2], rope[:, 3], ALU.add).then_inc(DQ_ready, 1)

                def mask_scores(k):
                    fam = HEADS[k][0]
                    for t in range(NT):
                        w, job = (t + 1) * P, ("s", HEADS[k], t)
                        if fam == "fox":
                            mask = c_("causal")[:, S - w:S]
                        else:
                            mask = c_("dilated")[:, t * P:t * P + w]
                        dve.wait_ge(*full(job, l))
                        if k >= 2 and t == 0:
                            dve.wait_ge(*full(("pT", HEADS[k - 2]), l))
                        alone(dve)
                        v.tensor_tensor_reduce(out=SCO[:, k % 2, t, 0:w], in0=bk(job)[:, 0:w], in1=mask,
                                               scale=HD ** -0.5, scalar=-BIG, op0=ALU.add, op1=ALU.max,
                                               accum_out=smax[:, k % 2, t:t + 1]).then_inc(read(job), 1)
                        dve.wait_ge(*copied(job, l))
                        v.tensor_scalar(smax[:, k % 2, t:t + 1], smax[:, k % 2, t:t + 1], -1.0, None, ALU.mult
                                        ).then_inc(scores, 1)

                def normalize(k, summed, sem_out, widths):
                    for t in range(NT):
                        dve.wait_ge(*summed(t))
                        link(v.reciprocal(ssum[:, k % 2, t:t + 1], ssum[:, k % 2, t:t + 1]))
                        p = SCO[:, k % 2, t, 0:widths[t]]
                        v.tensor_scalar(p, p, ssum[:, k % 2, t:t + 1], None, ALU.mult).then_inc(sem_out, 1)

                def conv(c):
                    dve.wait_ge(*copied(("xbc", c // 2), l))
                    o = XBC[:, c, :]
                    link(v.tensor_scalar(o, xin[:, c, 0:S], p_ch[:, c:c + 1], p_ch[:, 32 + c:33 + c], ALU.mult,
                                         ALU.add))
                    for k in range(1, 3):
                        link(v.scalar_tensor_tensor(o, xin[:, c, k:k + S], p_ch[:, 8 * k + c:8 * k + c + 1], o,
                                                    ALU.mult, ALU.add))
                    v.scalar_tensor_tensor(o, xin[:, c, 3:3 + S], p_ch[:, 24 + c:25 + c], o, ALU.mult, ALU.add
                                           ).then_inc(conv_done, 1)

                def gate(c):
                    dve.wait_ge(sig_exp, at(sig_exp, l, c + 1))
                    s_ = sig[:, c % 2, :]
                    link(v.tensor_scalar(s_, s_, 1.0, None, ALU.add))
                    link(v.reciprocal(s_, s_))
                    v.tensor_tensor(XBC[:, c, :], XBC[:, c, :], s_, ALU.mult).then_inc(conv_gated, 1)

                mask_scores(0)
                for k in range(len(HEADS)):
                    conv(k)
                    if k + 1 < len(HEADS):
                        mask_scores(k + 1)
                    if k:
                        gate(k - 1)
                    normalize(k, lambda t: (exps, at(exps, l, 2 * k + t + 1)), probs, (P, 2 * P))
                gate(KC - 1)

                for g in range(2):
                    job = ("cb", g)
                    dve.wait_ge(*full(job, l))
                    v.tensor_tensor(CB[:, g, :], bk(job)[:, 0:3 * P], tri, ALU.mult).then_inc(read(job), 1)
                for g in range(2):
                    dve.wait_ge(*copied(("cb", g), l))

                def exponents(h):
                    job = ("L", h)
                    if h >= 2:
                        dve.wait_ge(M_ready, at(M_ready, l, h - 1))
                    dve.wait_ge(*full(job, l))
                    v.tensor_scalar(Ls[:, h % 2, 0:S], bk(job)[:, 0:S], CUM[:, 0, NH + h:NH + h + 1], 0.0,
                                    ALU.subtract, ALU.min)
                    v.tensor_scalar(Ls[:, h % 2, S:], bk(job)[:, P:S], CUM[:, 1, NH + h:NH + h + 1], 0.0,
                                    ALU.subtract, ALU.min).then_inc(read(job), 1)

                exponents(0)
                for h in range(SH):
                    if h + 1 < SH:
                        exponents(h + 1)
                    dve.wait_ge(decays, at(decays, l, h + 1))
                    if h >= 2:
                        dve.wait_ge(y_head, at(y_head, l, h - 1))
                    v.scalar_tensor_tensor(Ms[:, h % 2, 0:S], Ls[:, h % 2, 0:S], DTs[:, 0, h:h + 1],
                                           CB[:, h // 4, 0:S], ALU.mult, ALU.mult)
                    v.scalar_tensor_tensor(Ms[:, h % 2, S:], Ls[:, h % 2, S:], DTs[:, 1, h:h + 1],
                                           CB[:, h // 4, S:], ALU.mult, ALU.mult).then_inc(M_ready, 1)
                for t in range(NT):
                    dve.wait_ge(*copied(("xsT", t), l))
                    link(v.tensor_tensor(view(Y[:, t, :], 0, SH, SP_), view(XS[:, t, :], 0, SH, SP_),
                                         bc(r_("ssd_D"), SH, SP_), ALU.mult))
                    dve.wait_ge(*full(("y", t), l))
                    v.tensor_tensor(Y[:, t, :], Y[:, t, :], bk(("y", t))[:, :], ALU.add).then_inc(read(("y", t)), 1)
                    dve.wait_ge(z_exp, at(z_exp, l, t + 1))
                    e = sq[:, t * SI:(t + 1) * SI]
                    link(v.tensor_scalar(e, e, 1.0, None, ALU.add))
                    link(v.reciprocal(e, e))
                    link(v.tensor_tensor(e, e, pt[t][:, T_Z:T_Z + SI], ALU.mult))
                    link(v.tensor_tensor(Y[:, t, :], Y[:, t, :], e, ALU.mult))
                    v.tensor_tensor_reduce(out=ve[:, :], in0=Y[:, t, :], in1=Y[:, t, :], scale=1.0, scalar=0.0,
                                           op0=ALU.mult, op1=ALU.add, accum_out=ss[:, 4 + t:5 + t]).then_inc(y_ss, 1)
                for t in range(NT):
                    dve.wait_ge(y_rs, at(y_rs, l, t + 1))
                    v.tensor_scalar(Y[:, t, :], Y[:, t, :], ss[:, 4 + t:5 + t], None, ALU.mult).then_inc(Y_ready, 1)
                for t in range(NT):
                    gained(("ysT", t), p_ch[:, 40:44], mixT[:, 4:8, t * P:(t + 1) * P])

                def residual(name, bump):
                    for n in range(2):
                        for t in range(NT):
                            job = (name, n, t)
                            dve.wait_ge(*full(job, l))
                            x = X[:, t, n * 512:(n + 1) * 512]
                            v.tensor_tensor(x, x, bk(job)[:, :], ALU.add).then_inc(read(job), 1)
                    for n in range(2):
                        for t in range(NT):
                            dve.wait_ge(*copied((name, n, t), l))
                    dve.sem_inc(X_ready, 1)

                residual("out1", 1)
                norm_x(1, G_2, "hT2")
                for t in range(NT):
                    head_norm(t, Q_tm, "xa_qn_g", q_rs, q_normed)
                for t in range(NT):
                    for i in range(2):
                        copy4(("qT", t, i), QT[:, 4 * i:4 * i + 4, t * P:(t + 1) * P])

                def cross_max(h):
                    for t in range(NT):
                        job = ("xs", h, t)
                        dve.wait_ge(*full(job, l))
                        if h >= 2 and t == 0:
                            dve.wait_ge(*full(("xpT", h - 2), l))
                        m = smax[:, h % 2, t:t + 1]
                        link(v.tensor_reduce(m, bk(job)[:, 0:S], AX.X, ALU.max))
                        v.tensor_scalar(m, m, -XD ** -0.5, None, ALU.mult).then_inc(xmax, 1)

                cross_max(0)
                for h in range(XH):
                    if h + 1 < XH:
                        cross_max(h + 1)
                    normalize(h, lambda t: copied(("xs", h, t), l), xprobs, (S, S))
                residual("out2", 2)
                norm_x(2, G_3, "hT3")

                job = ("router",)
                dve.wait_ge(*full(job, l))
                bias = view(row, ROWS["router_bg"][0], NG + NE).unsqueeze(1).to_broadcast([P, NT, NG + NE])
                link(v.tensor_tensor(lg[:, :, :], bk(job)[:, 0:NT * (NG + NE)].rearrange("p (t n) -> p t n", t=NT),
                                     bias, ALU.add))

                def first_max(src, n, top, hot):
                    tmp = first[:, :, 0:n]
                    down = c_("down")[:, 0:n].unsqueeze(1).to_broadcast([P, NT, n])
                    link(v.tensor_reduce(top, src, AX.X, ALU.max))
                    link(v.tensor_tensor(tmp, src, top.to_broadcast([P, NT, n]), ALU.is_equal))
                    link(v.tensor_tensor(tmp, tmp, down, ALU.mult))
                    link(v.tensor_reduce(rt[:, :, 7:8], tmp, AX.X, ALU.max))
                    link(v.tensor_tensor(hot, tmp, rt[:, :, 7:8].to_broadcast([P, NT, n]), ALU.is_equal))

                gmax, m1, m2 = rt[:, :, 0:1], rt[:, :, 1:2], rt[:, :, 2:3]
                g_gate, e21, p1, p2 = rt[:, :, 3:4], rt[:, :, 4:5], rt[:, :, 5:6], rt[:, :, 6:7]
                first_max(lg[:, :, 0:NG], NG, gmax, rg[:, :, 0, :])
                v.tensor_tensor(rg[:, :, 1, :], lg[:, :, 0:NG], gmax.to_broadcast([P, NT, NG]), ALU.subtract
                                ).then_inc(g_shift, 1)
                link(v.tensor_scalar(rg[:, :, 2, :], rg[:, :, 0, :], 1.0, BIG, ALU.subtract, ALU.mult))
                link(v.tensor_tensor(em[:, :, :].rearrange("p t (g e) -> p t g e", g=NG),
                                     lg[:, :, NG:].rearrange("p t (g e) -> p t g e", g=NG),
                                     rg[:, :, 2, :].unsqueeze(3).to_broadcast([P, NT, NG, EPG]), ALU.add))
                first_max(em[:, :, :], NE, m1, oh[:, 0])
                link(v.scalar_tensor_tensor(em[:, :, :], oh[:, 0], -BIG, em[:, :, :], ALU.mult, ALU.add))
                first_max(em[:, :, :], NE, m2, oh[:, 1])
                v.tensor_tensor(e21, m2, m1, ALU.subtract).then_inc(e_shift, 1)
                v.tensor_tensor(chosen[:, :, :], oh[:, 0], oh[:, 1], ALU.add).then_inc(chosen_ready, 1)
                dve.wait_ge(g_exp, at(g_exp, l, 1))
                link(v.tensor_reduce(g_gate, rg[:, :, 1, :], AX.X, ALU.add))
                dve.wait_ge(e_exp, at(e_exp, l, 1))
                link(v.tensor_scalar(p1, e21, 1.0, None, ALU.add))
                link(v.tensor_tensor(p1, p1, g_gate, ALU.mult))
                link(v.reciprocal(p1, p1))
                link(v.tensor_tensor(p2, p1, e21, ALU.mult))
                link(v.tensor_tensor(gates[:, :, :], oh[:, 0], p1.to_broadcast([P, NT, NE]), ALU.mult))
                link(v.tensor_tensor(em[:, :, :], oh[:, 1], p2.to_broadcast([P, NT, NE]), ALU.mult))
                link(v.tensor_tensor(gates[:, :, :], gates[:, :, :], em[:, :, :], ALU.add))
                job = ("rank",)
                dve.wait_ge(*full(job, l))
                rk = bk(job)[:, 0:3 * NE].rearrange("p (t n) -> p t n", t=3)
                link(v.tensor_tensor(rank[:, :, :], chosen[:, :, :], rk[:, 0:NT, :], ALU.mult))
                link(v.tensor_scalar(rank[:, :, :], rank[:, :, :], 1.0, None, ALU.subtract))
                link(v.tensor_reduce(passes[:, 1:2], rk[:, NT, :], AX.X, ALU.max))
                link(v.tensor_tensor(over[:, :], passes[:, 1:2].to_broadcast([P, 8]), c_("caps"), ALU.is_gt))
                link(v.tensor_reduce(passes[:, 1:2], over[:, :], AX.X, ALU.add))
                link(v.tensor_tensor(passes[:, 0:1], passes[:, 0:1], passes[:, 1:2], ALU.add))
                v.tensor_copy(passes_i[:, bass.ds(l + 1, 1)], passes[:, 0:1]).then_inc(passes_known, 1)
                link(v.tensor_copy(slot_no[:, :], c_("slots")))
                dve.sem_inc(read(("router",)), 1)
                dve.sem_inc(read(("rank",)), 1)
                assert steps[0] == V_STEPS, ("V", steps)

                def quad(q, quads):
                    n_steps = [0]

                    def step(ins):
                        n_steps[0] += 1
                        ins.then_inc(v_moe, 1)
                        dve.wait_ge(v_moe, quads * V_MOE + n_steps[0])

                    mine = rank[:, :, bass.ds(q * QUAD, QUAD)].unsqueeze(3).to_broadcast([P, NT, QUAD, CAP])
                    places = slot_no[:, :].unsqueeze(1).unsqueeze(1).to_broadcast([P, NT, QUAD, CAP])
                    my_gates = gates[:, :, bass.ds(q * QUAD, QUAD)].unsqueeze(3).to_broadcast([P, NT, QUAD, CAP])
                    v.tensor_tensor(SEL, mine, places, ALU.is_equal).then_inc(sel_ready, 1)
                    dve.wait_ge(sel_ready, quads + 1)
                    v.tensor_tensor(SELG, SEL, my_gates, ALU.mult).then_inc(selg_ready, 1)
                    for i in range(2):
                        dve.wait_ge(gath_full, quads * 2 + i + 1)
                        v.tensor_tensor(XG[:, 4 * i:4 * i + 4, :],
                                        bank[B_GATH[i]][:, :].rearrange("p (c s) -> p c s", c=4),
                                        bc(g_ch[:, G_3, 4 * i:4 * i + 4], 4, P), ALU.mult).then_inc(XG_ready, 1)
                    dve.wait_ge(up_exp, quads + 1)
                    step(v.tensor_scalar(SIGM, SIGM, 1.0, None, ALU.add))
                    step(v.reciprocal(SIGM, SIGM))
                    step(v.tensor_tensor(SIGM, SIGM, bank[B_UP[0]][:, :], ALU.mult))
                    dve.wait_ge(units_used, quads * MOE_UNITS + MOE_UNITS + 8)
                    v.tensor_tensor(HID, SIGM.rearrange("p (q c) -> p c q", c=4),
                                    bank[B_UP[1]][:, :].rearrange("p (q c) -> p c q", c=4), ALU.mult
                                    ).then_inc(hid_ready, 1)
                    for i in range(4):
                        t, n = i // 2, i % 2
                        dve.wait_ge(scat_full, quads * 4 + i + 1)
                        x = X[:, t, n * 512:(n + 1) * 512]
                        last = v.tensor_tensor(x, x, bank[B_SCAT[i]][:, :], ALU.add)
                    step(last)
                    assert n_steps[0] == V_MOE

                def new_pass():
                    v.tensor_scalar(slot_no[:, :], slot_no[:, :], float(CAP), None, ALU.add)
                moe_quads(dve, l, quad, new_pass=new_pass)
                dve.sem_inc(vector_layer, 1)

        @block.tensor
        def _(pe):
            def mm(dst, lhsT, rhs, start=True, stop=True):
                return nc.tensor.matmul(dst, lhsT, rhs, start=start, stop=stop)

            pe.wait_ge(const_in, 16)
            with pe.Fori(0, DEPTH) as l:
                pe.wait_ge(passes_known, at(passes_known, l, 1))
                turn = pe.snap(load_passes(pe, l) * (NQ * MOE_TURNS) + l * DENSE_TURNS)
                pe.wait_ge(vector_layer, at(vector_layer, l, 1))

                def transposes(job, srcs, last_wait=lambda eng: None):
                    pe.wait_ge(*free(job, l))
                    last_wait(pe)
                    for i, src in enumerate(srcs):
                        last = nc.tensor.transpose(bk(job)[0:src.shape[1], i * P:i * P + src.shape[0]], src,
                                                   ident[0:src.shape[0], 0:src.shape[0]])
                    last.then_inc(filled(job), 1)

                def arrived(unit):
                    n = DENSE.index(unit)
                    pe.wait_ge(landed[n % SLOTS], (turn + n // SLOTS + 1) * 16)
                    return ring_view(n % SLOTS, IN_COLS.get(unit[0], (0, 512))[1])

                def token_major(unit, name, n, lhs):
                    w = arrived(unit)
                    for t in range(NT):
                        job = (name, n, t)
                        pe.wait_ge(*free(job, l))
                        for c in range(KC):
                            last = mm(bk(job)[:, 0:w.shape[2]], lhs[:, c, t * P:(t + 1) * P], w[:, c, :],
                                      start=c == 0, stop=c == KC - 1)
                        last.then_inc(filled(job), 1)

                def all_copied(name):
                    for t in range(NT):
                        for i in range(2):
                            pe.wait_ge(*copied((name, t, i), l))

                def transpose_h(k, name):
                    pe.wait_ge(H_ready, at(H_ready, l, NT * (k + 1)))
                    for t in range(NT):
                        for i in range(2):
                            transposes((name, t, i), [H[:, t, 4 * i + j, :] for j in range(4)])
                    all_copied(name)

                pe.wait_ge(params_in, at(params_in, l, 16 * N_PARAMS))
                transposes(("params",), [p_rows[:, :]], last_wait=alone)
                pe.wait_ge(MN_ready, at(MN_ready, l, 1))
                for t in range(NT):
                    for i in range(2):
                        transposes(("memT", t, i), [MN[:, t, 4 * i + j, :] for j in range(4)])
                all_copied("memT")
                for n in range(4):
                    token_major(("kv", n), "kv", n, MT)
                for t in range(NT):
                    pe.wait_ge(k_normed, at(k_normed, l, t + 1))
                    for i in range(2):
                        transposes(("kT", t, i), [K_tm[:, t, (4 * i + j) * P:(4 * i + j + 1) * P] for j in range(4)])
                transpose_h(0, "hT1")
                for i in range(4):
                    job = ("xbc", i)
                    w = arrived(("xbc", i // 2))
                    pe.wait_ge(*free(job, l))
                    for j in range(2):
                        c0 = (i % 2 * 2 + j) * P
                        for c in range(KC):
                            last = mm(bk(job)[:, j * S:(j + 1) * S], w[:, c, c0:c0 + P], HT[:, c, :],
                                      start=c == 0, stop=c == KC - 1)
                    last.then_inc(filled(job), 1)
                for n in IN_ORDER:
                    token_major((n, 0), "in", n, HT)

                job = ("cum",)
                pe.wait_ge(DL_ready, at(DL_ready, l, 1))
                pe.wait_ge(*free(job, l))
                mm(bk(job)[:, 0:12], tri[:, 0:P], DL[:, 0, :])
                mm(bk(job)[:, 12:24], ones, DL[:, 0, :], stop=False)
                mm(bk(job)[:, 12:24], tri[:, 0:P], DL[:, 1, :], start=False).then_inc(filled(job), 1)
                for t in range(NT):
                    pe.wait_ge(FQ_ready, at(FQ_ready, l, t + 1))
                    for i in range(2):
                        transposes(("fT", t, i), [FQ[:, t, 4 * i + j, :] for j in range(4)])
                for t in range(NT):
                    pe.wait_ge(DQ_ready, at(DQ_ready, l, t + 1))
                    transposes(("dT", t), [pt[t][:, T_DQK + j * P:T_DQK + (j + 1) * P] for j in range(4)])
                all_copied("fT")
                for t in range(NT):
                    pe.wait_ge(*copied(("dT", t), l))

                def score(k):
                    fam, h = HEADS[k]
                    for t in range(NT):
                        job, w = ("s", HEADS[k], t), (t + 1) * P
                        pe.wait_ge(*free(job, l))
                        if fam == "fox":
                            q, kk = FQT[0:HD + 2, h, t * P:(t + 1) * P], FQT[0:HD + 2, NH + h, 0:w]
                        else:
                            r = slice(HD * (h % 2), HD * (h % 2) + HD)
                            q, kk = DQT[r, h // 2, t * P:(t + 1) * P], DQT[r, 2 + h // 2, 0:w]
                        mm(bk(job)[:, 0:w], q, kk).then_inc(filled(job), 1)

                score(0)
                for k, (fam, h) in enumerate(HEADS):
                    if k + 1 < len(HEADS):
                        score(k + 1)
                    pe.wait_ge(probs, at(probs, l, 2 * k + 2))
                    transposes(("pT", (fam, h)), [SCO[:, k % 2, 0, 0:P], SCO[:, k % 2, 1, 0:P], SCO[:, k % 2, 1, P:S]])
                    if k % 2:
                        job = ("o", (fam, h))
                        pe.wait_ge(*free(job, l))
                        for k2 in (k - 1, k):
                            pe.wait_ge(*copied(("pT", HEADS[k2]), l))
                            r = slice(HD * (k2 % 2), HD * (k2 % 2) + HD)
                            v0 = (T_FV if fam == "fox" else T_DV) + HD * HEADS[k2][1]
                            mm(bk(job)[r, 0:S], pt[0][:, v0:v0 + HD], PT[:, k2 % 2, 0:S], stop=False)
                            last = mm(bk(job)[r, P:S], pt[1][:, v0:v0 + HD], PT[:, k2 % 2, S:3 * P], start=False)
                        last.then_inc(filled(job), 1)

                pe.wait_ge(conv_gated, at(conv_gated, l, KC))
                for t in range(NT):
                    transposes(("xsT", t), [XBC[:, c, t * P:(t + 1) * P] for c in range(4)])
                for g in range(2):
                    job, Bg, Cg = ("cb", g), XBC[:, 4 + g, :], XBC[:, 6 + g, :]
                    pe.wait_ge(*free(job, l))
                    mm(bk(job)[:, 0:S], Bg[:, 0:P], Cg)
                    mm(bk(job)[:, S:3 * P], Bg[:, P:S], Cg[:, P:S]).then_inc(filled(job), 1)

                def spread(h):
                    job = ("L", h)
                    pe.wait_ge(*free(job, l))
                    d = [DL[:, t, NH + h:NH + h + 1].to_broadcast([P, P]) for t in range(NT)]
                    mm(bk(job)[:, 0:S], d[0], tri[:, 0:S], stop=False)
                    mm(bk(job)[:, P:S], d[1], tri[:, 0:P], start=False).then_inc(filled(job), 1)

                for h in range(L_AHEAD):
                    spread(h)
                for t in range(NT):
                    pe.wait_ge(*copied(("xsT", t), l))
                    pe.wait_ge(*free(("y", t), l))
                for h in range(SH):
                    if h + L_AHEAD < SH:
                        spread(h + L_AHEAD)
                    pe.wait_ge(M_ready, at(M_ready, l, h + 1))
                    c = slice(SP_ * h, SP_ * (h + 1))
                    M = Ms[:, h % 2, :]
                    y0 = mm(bk(("y", 0))[:, c], M[:, 0:P], XS[:, 0, c])
                    if h == SH - 1:
                        y0.then_inc(filled(("y", 0)), 1)
                    mm(bk(("y", 1))[:, c], M[:, P:S], XS[:, 0, c], stop=False)
                    y1 = mm(bk(("y", 1))[:, c], M[:, S:], XS[:, 1, c], start=False)
                    y1.then_inc(filled(("y", 1)) if h == SH - 1 else y_head, 1)
                for t in range(NT):
                    pe.wait_ge(Y_ready, at(Y_ready, l, t + 1))
                    transposes(("ysT", t), [Y[:, t, j * P:(j + 1) * P] for j in range(4)])
                for t in range(NT):
                    pe.wait_ge(*copied(("ysT", t), l))
                for k in (1, 3, 5, 7):
                    pe.wait_ge(*copied(("o", HEADS[k]), l))
                for n in range(2):
                    token_major(("w_out", n), "out1", n, mixT)

                transpose_h(1, "hT2")
                for n in range(2):
                    token_major(("wq", n), "q", n, HT)
                for t in range(NT):
                    pe.wait_ge(q_normed, at(q_normed, l, t + 1))
                    for i in range(2):
                        transposes(("qT", t, i), [Q_tm[:, t, (4 * i + j) * P:(4 * i + j + 1) * P] for j in range(4)])
                all_copied("qT")
                all_copied("kT")

                def cross_score(h):
                    for t in range(NT):
                        job = ("xs", h, t)
                        pe.wait_ge(*free(job, l))
                        for c in (2 * h, 2 * h + 1):
                            last = mm(bk(job)[:, 0:S], QT[:, c, t * P:(t + 1) * P], KT[:, c, :],
                                      start=c == 2 * h, stop=c == 2 * h + 1)
                        last.then_inc(filled(job), 1)

                cross_score(0)
                for h in range(XH):
                    if h + 1 < XH:
                        cross_score(h + 1)
                    pe.wait_ge(xprobs, at(xprobs, l, 2 * h + 2))
                    transposes(("xpT", h), [SCO[:, h % 2, t, m * P:(m + 1) * P] for m in range(2) for t in range(NT)])
                    job = ("xo", h)
                    pe.wait_ge(*copied(("xpT", h), l))
                    pe.wait_ge(*free(job, l))
                    for j in range(2):
                        d0 = h * XD + j * P
                        for m in range(2):
                            last = mm(bk(job)[:, j * S:(j + 1) * S], VM[:, m, d0:d0 + P],
                                      PT[:, h % 2, m * S:(m + 1) * S], start=m == 0, stop=m == 1)
                    last.then_inc(filled(job), 1)
                for h in range(XH):
                    pe.wait_ge(*copied(("xo", h), l))
                for n in range(2):
                    token_major(("wo", n), "out2", n, mixT)

                transpose_h(2, "hT3")
                job, w = ("router",), NG + NE
                pe.wait_ge(*free(job, l))
                for t in range(NT):
                    for c in range(KC):
                        last = mm(bk(job)[:, t * w:(t + 1) * w], HT[:, c, t * P:(t + 1) * P], wr[:, c, :],
                                  start=c == 0, stop=c == KC - 1)
                last.then_inc(filled(job), 1)
                job = ("rank",)
                pe.wait_ge(chosen_ready, at(chosen_ready, l, 1))
                pe.wait_ge(*free(job, l))
                mm(bk(job)[:, 0:NE], tri[:, 0:P], chosen[:, 0, :])
                mm(bk(job)[:, NE:2 * NE], ones, chosen[:, 0, :], stop=False)
                mm(bk(job)[:, NE:2 * NE], tri[:, 0:P], chosen[:, 1, :], start=False)
                mm(bk(job)[:, 2 * NE:3 * NE], ones, chosen[:, 0, :], stop=False)
                mm(bk(job)[:, 2 * NE:3 * NE], ones, chosen[:, 1, :], start=False).then_inc(filled(job), 1)

                def quad(q, quads):
                    turns = (l + 1) * DENSE_TURNS + quads * MOE_TURNS

                    def landed_unit(n):
                        pe.wait_ge(landed[n % SLOTS], (turns + n // SLOTS + 1) * 16)
                        return ring[:, n % SLOTS, :].rearrange("p (e c n) -> p e c n", e=QUAD, n=512)

                    pe.wait_ge(sel_ready, quads + 1)
                    sel = SEL.rearrange("p t e s -> p t (e s)")
                    selg = SELG.rearrange("p t e s -> p t (e s)")
                    for i in range(2):
                        for j in range(4):
                            for t in range(NT):
                                last = mm(bank[B_GATH[i]][:, j * P:(j + 1) * P], H[:, t, 4 * i + j, :], sel[:, t, :],
                                          start=t == 0, stop=t == NT - 1)
                        last.then_inc(gath_full, 1)
                    pe.wait_ge(selg_ready, quads + 1)
                    for t in range(NT):
                        last = nc.tensor.transpose(bank[B_SELT][:, t * P:(t + 1) * P], selg[:, t, :], ident)
                    last.then_inc(selt_full, 1)
                    pe.wait_ge(XG_ready, quads * 2 + 2)
                    for n in range(8):
                        u = landed_unit(n)
                        for c in range(2):
                            k = n % 4 * 2 + c
                            for e in range(QUAD):
                                r = slice(CAP * e, CAP * (e + 1))
                                last = mm(bank[B_UP[n // 4]][r, :], XG[:, k, r], u[:, e, c, :],
                                          start=k == 0, stop=k == KC - 1)
                        last.then_inc(units_used, 1)
                    pe.wait_ge(hid_ready, quads + 1)
                    for j in range(4):
                        last = nc.tensor.transpose(bank[B_HIDT][:, j * P:(j + 1) * P], HID[:, j, :], ident)
                    last.then_inc(hidt_full, 1)
                    pe.wait_ge(HIDT_ready, quads + 1)
                    for n in range(4):
                        u = landed_unit(8 + n)
                        for c in range(2):
                            for e in range(QUAD):
                                r = slice(CAP * e, CAP * (e + 1))
                                last = mm(bank[B_DOWN[c]][r, :], HIDT[:, n, r], u[:, e, c, :],
                                          start=n == 0, stop=n == 3)
                        last.then_inc(units_used, 1)
                    pe.wait_ge(SELT_ready, quads + 1)
                    pe.wait_ge(YS_ready, quads + 1)
                    for i in range(4):
                        t, n = i // 2, i % 2
                        mm(bank[B_SCAT[i]][:, :], SELT[:, t * P:(t + 1) * P], YS[:, n * 512:(n + 1) * 512]
                           ).then_inc(scat_full, 1)
                moe_quads(pe, l, quad)


def constants():
    import numpy as np
    p = np.arange(P)[:, None]
    j = np.arange(P)[None, :]
    con = np.zeros((P, CONST_W), np.float32)

    def put(name, v):
        o, w = CONST[name]
        con[:, o:o + w] = v
    put("ident", p == j)
    tri = (p <= j).astype(np.float32)
    put("tri", np.concatenate([tri, np.ones((P, P)), tri], 1))
    put("causal", np.concatenate([np.zeros((P, P)), np.where(j <= p, 0.0, -BIG)], 1))
    dil = []
    for t in range(NT):
        d = (t * P + p) - np.arange((t + 1) * P)[None, :]
        m = sum(((d >= 0) & (d <= w) & (d % r == 0)).astype(np.float64) for w, r in ((128, 1), (512, 4), (2048, 16)))
        dil.append(np.where(m > 0, HD ** 0.5 * np.log(np.maximum(m, 1)), -BIG))
    put("dilated", np.concatenate(dil, 1))
    inv = np.power(np.float32(500000.0), -2.0 * np.arange(8, dtype=np.float32) / np.float32(16)).astype(np.float32)
    ang = np.arange(S, dtype=np.float32)[:, None] * inv[None, :]
    for name, f in (("cos", np.cos), ("sin", np.sin)):
        put(name, f(ang).astype(np.float32).reshape(NT, P, 8).transpose(1, 0, 2).reshape(P, NT * 8))
    put("slots", np.arange(CAP)[None, :])
    put("caps", (np.arange(8) * CAP)[None, :])
    put("down", (NE - np.arange(NE))[None, :])
    put("half", -0.5)
    return con


INPUTS = ["x", "mem", "norm1_g", "w_in", "fox_fgate_b", "fox_qn_g", "fox_kn_g", "dil_qn_g", "dil_kn_g",
          "ssd_conv_w", "ssd_conv_b", "ssd_dt_bias", "ssd_A_log", "ssd_D", "ssd_norm_g", "w_out", "norm2_g",
          "mem_norm_g", "xa_wq", "xa_wkv", "xa_qn_g", "xa_kn_g", "xa_wo", "norm3_g", "router_wg", "router_bg",
          "router_we", "router_be", "exp_w1", "exp_w3", "exp_w2"]


def kernel(**inputs):
    import numpy as np
    import concourse.bacc as bacc
    from concourse.bass_utils import run_bass_kernel_spmd

    nc = bacc.Bacc("TRN2", target_bir_lowering=False, num_devices=1)
    arrays = {n: np.ascontiguousarray(inputs[n]) for n in INPUTS}
    arrays["const"] = constants()
    aps = {n: nc.dram_tensor(n, v.shape, mybir.dt.from_np(v.dtype), kind="ExternalInput").ap()
           for n, v in arrays.items()}
    out = nc.dram_tensor("out", (1, S, D), F32, kind="ExternalOutput").ap()
    trunk(nc, aps, out)
    r = run_bass_kernel_spmd(nc, [arrays], core_ids=[0])
    return r.results[0]["out"]
```

```python
from contextlib import ExitStack

import concourse.bass as bass
from concourse import mybir

F32 = mybir.dt.float32
I32 = mybir.dt.int32
ALU = mybir.AluOpType
ACT = mybir.ActivationFunctionType
AX = mybir.AxisListType

P = 128
DEPTH, S, D = 2, 256, 1024
NT = S // P
KC = D // P
HD, NH = 64, 4
SH, SP_, SI = 8, 64, 512
XC = 1024
XH, XD = 4, 256
NE, FF = 32, 512
QUAD = 4
CAP = P // QUAD
NQ = NE // QUAD
NG, EPG = 4, 8
EPS = 1e-6
BIG = 1e30
C_FQK, C_FV, C_DQK, C_DV, C_Z, C_XBC, C_DT = 0, 512, 772, 1284, 1540, 2052, 3076
T_FV, T_FF, T_DQK, T_DV, T_Z, T_DT, T_W = 512, 768, 772, 1284, 1540, 2052, 2060
ROWS = {}
_o = 0
for _n, _w in (("fox_qn_g", HD), ("fox_kn_g", HD), ("dil_qn_g", HD), ("dil_kn_g", HD), ("xa_qn_g", XD),
               ("xa_kn_g", XD), ("fox_fgate_b", NH), ("ssd_dt_bias", SH), ("ssd_A_log", SH), ("ssd_D", SH),
               ("router_bg", NG), ("router_be", NE)):
    ROWS[_n] = (_o, _w)
    _o += _w
ROWS_W = _o
CONST = {}
_o = 0
for _n, _w in (("ident", P), ("tri", 3 * P), ("causal", 2 * P), ("dilated", 3 * P), ("cos", NT * 8),
               ("sin", NT * 8), ("slots", CAP), ("caps", 8), ("down", NE), ("half", 16)):
    CONST[_n] = (_o, _w)
    _o += _w
CONST_W = _o

SLOTS = 6
UNIT = 4096
DENSE = [("dt", 0), ("fv", 0), ("fqk", 0), ("xbc", 0), ("xbc", 1), ("dqk", 0), ("z", 0), ("dv", 0),
         ("kv", 0), ("kv", 1), ("kv", 2), ("kv", 3), ("w_out", 0), ("w_out", 1), ("wq", 0), ("wq", 1),
         ("wo", 0), ("wo", 1)]
DENSE_TURNS = len(DENSE) // SLOTS
assert DENSE_TURNS * SLOTS == len(DENSE)
MOE_UNITS = 12
MOE_TURNS = MOE_UNITS // SLOTS
IN_COLS = {"fqk": (C_FQK, 512), "fv": (C_FV, 260), "dqk": (C_DQK, 512), "dv": (C_DV, 256), "z": (C_Z, 512),
           "dt": (C_DT, 8)}
IN_DEST = {"fqk": 0, "fv": T_FV, "dqk": T_DQK, "dv": T_DV, "z": T_Z, "dt": T_DT}
IN_FIRST, IN_THEN = ("dt", "fv", "fqk"), ("dqk", "z", "dv")

HEADS = [(fam, h) for fam in ("fox", "dil") for h in range(NH)]
BETWEEN = [[("kv", 0, 0)], [("kv", 0, 1)], [("dT", 0), ("dT", 1), ("kT", 0, 0), ("kv", 1, 0)],
           [("kT", 0, 1), ("kv", 1, 1)], [("kT", 1, 0), ("kv", 2, 0)], [("kT", 1, 1), ("kv", 2, 1)],
           [("kv", 3, 0)], [], []]
CROSS = [(t, h) for t in range(NT) for h in range(XH)]
CROSS_BETWEEN = [[], [], [("qT", 1, 0), ("qT", 1, 1)], [], [], [("out2", 0, 0)], [("out2", 1, 0)], [], []]
L_AHEAD = 2


def list_jobs():
    def two(name, t):
        return [(name, t, 0), (name, t, 1)]

    jobs = two("hT1", 0) + two("hT1", 1)
    jobs += [("in", n, t) for n in IN_FIRST for t in range(NT)]
    jobs += [("params",)] + two("memT", 0) + two("memT", 1)
    jobs += [("xbc", i) for i in range(4)]
    jobs += [("cum",)] + two("fT", 0) + two("fT", 1)
    jobs += [("in", n, t) for n in IN_THEN for t in range(NT)]
    for k in range(len(HEADS) + 1):
        if k < len(HEADS):
            jobs += [("s", HEADS[k], t) for t in range(NT)]
        jobs += BETWEEN[k]
        if k:
            jobs += [("pT", HEADS[k - 1])]
            if k % 2 == 0:
                jobs += [("o", HEADS[k - 1])]
    jobs += [("xsT", t) for t in range(NT)] + [("cb", g) for g in range(2)]
    jobs += [("y", t) for t in range(NT)] + [("L", h) for h in range(SH)]
    jobs += [("kv", 3, 1)] + [("ysT", t) for t in range(NT)]
    jobs += [("out1", n, t) for t in range(NT) for n in range(2)]
    for t in range(NT):
        jobs += two("hT2", t) + [("q", 0, t), ("q", 1, t)]
    jobs += two("qT", 0)
    for j in range(len(CROSS) + 1):
        if j < len(CROSS):
            jobs += [("xs", *CROSS[j])]
        jobs += CROSS_BETWEEN[j]
        if j:
            jobs += [("xpT", *CROSS[j - 1]), ("xo", *CROSS[j - 1])]
    jobs += [("out2", 0, 1)] + two("hT3", 0) + [("out2", 1, 1)] + two("hT3", 1)
    return jobs + [("router",), ("rank",)]


NB = 8


def plan_banks():
    place, uses, n, held = {}, [0] * NB, 0, set()
    for job in list_jobs():
        while n % NB in held:
            n += 1
        b = n % NB
        place[job] = (b, uses[b])
        uses[b] += 1
        if job[0] == "y":
            held.add(b)
        if job == ("L", SH - 1):
            held.clear()
        n += 1
    return place, uses


PLACE, USES = plan_banks()
LAST_USE = {"kv": lambda i: ("kv", i, 1), "xbc": lambda i: ("xbc", 2 * i + 1), "w_out": lambda i: ("out1", i, 1),
            "wq": lambda i: ("q", i, 1), "wo": lambda i: ("out2", i, 1)}
N_PARAMS = 4
V_STEPS, A_STEPS, G_STEPS = 100, 2, 19
V_MOE = 2
G_X, G_MEM, G_2 = 0, 1, 2


def last_use(unit):
    kind, i = unit
    return LAST_USE[kind](i) if kind in LAST_USE else ("in", kind, 1)


def trunk(nc, a, out):
    with ExitStack() as ctx:
        def sb(name, shape, dt=F32):
            return ctx.enter_context(nc.sbuf_tensor(name, shape, dt))

        per_layer = {}

        def sem(name, n=0):
            s = ctx.enter_context(nc.semaphore(name))
            per_layer[s] = n
            return s

        def at(s, l, n):
            return l * per_layer[s] + n

        ring = sb("ring", [P, SLOTS, UNIT])
        X = sb("X", [P, NT, D])
        H = sb("H", [P, NT, KC, P])
        HT = sb("HT", [P, NT, KC, P])
        MT = sb("MT", [P, NT, KC, P])
        proj = sb("proj", [P, NT * T_W])
        XBCp = sb("XBCp", [P, KC * (S + 3)])
        XS = sb("XS", [P, NT, SI])
        Y = sb("Y", [P, NT, SI])
        FQ = sb("FQ", [P, NT, 2 * NH, HD + 2])
        FQT = sb("FQT", [P, 2 * NH, S])
        DQT = sb("DQT", [P, 4, S])
        KT = sb("KT", [P, KC, S])
        VM = sb("VM", [P, NT, D])
        SCO = sb("SCO", [P, 2, NT, S])
        row = sb("row", [P, ROWS_W])
        con = sb("con", [P, CONST_W])
        g_ch = sb("g_ch", [P, 3, KC])
        g3 = sb("g3", [P, DEPTH, KC])
        p_rows = sb("p_rows", [44, P])
        p_ch = sb("p_ch", [P, 44])
        wr = sb("wr", [P, KC, NG + NE])
        ss = sb("ss", [P, 6])
        ssk = sb("ssk", [P, NT, XH])
        ssm = sb("ssm", [P, NT])
        ssf = sb("ssf", [P, NT, 16])
        smax = sb("smax", [P, 2, NT])
        ssum = sb("ssum", [P, 2, NT])
        gate_in = sb("gate_in", [P, NT, 12])
        gate_e = sb("gate_e", [P, NT, 12])
        DL = sb("DL", [P, NT, 12])
        DTs = sb("DTs", [P, NT, SH])
        CUM = sb("CUM", [P, NT, 12])
        negA = sb("negA", [P, SH])
        rt = sb("rt", [P, NT, 8])
        rg = sb("rg", [P, NT, 4, NG])
        passes = sb("passes", [P, 2])
        passes_i = sb("passes_i", [P, DEPTH + 1], I32)
        over = sb("over", [P, 8])
        slot_no = sb("slot_no", [P, CAP])

        def view(buf, off, *shape):
            n = 1
            for x in shape:
                n *= x
            v = buf[:, off:off + n]
            if len(shape) == 1:
                return v
            names = "abcd"[:len(shape)]
            return v.rearrange(f"p ({' '.join(names)}) -> p {' '.join(names)}", **dict(zip(names, shape)))

        def ring_view(s, w):
            return view(ring[:, s, :], 0, KC, w)

        fqt_flat = FQT[:, :, :].rearrange("p a b -> p (a b)")
        pt = [proj[:, t * T_W:(t + 1) * T_W] for t in range(NT)]
        mem_raw = view(fqt_flat, 0, NT, D)
        MN = view(XBCp, 0, NT, KC, P)
        xin = view(XBCp, 0, KC, S + 3)
        xc = xin[:, :, 3:]
        mixT = H
        Q_tm = view(proj, 0, NT, D)
        QT = HT
        sq = view(SCO[:, :, :, :].rearrange("p a b c -> p (a b c)"), 0, 1024)
        fq_flat = FQ[:, :, :, :].rearrange("p a b c -> p (a b c)")
        cv = view(fq_flat, 0, 2, S)
        rope = view(fq_flat, 2 * S, 4, 2 * NH, 8)
        K_tm = XS
        dqt_flat = DQT[:, :, :].rearrange("p a b -> p (a b)")
        lg = view(dqt_flat, 0, NT, NG + NE)
        first = view(dqt_flat, 128, NT, NE)
        em = view(dqt_flat, 192, NT, NE)
        oh = view(dqt_flat, 256, 2, NT, NE)
        gates = view(dqt_flat, 384, NT, NE)
        chosen = view(dqt_flat, 448, NT, NE)
        rank = view(dqt_flat, 512, NT, NE)
        ht_flat = HT[:, :, :, :].rearrange("p t a b -> p (t a b)")
        sig = view(ht_flat, 0, 2, S)
        ve = view(ht_flat, 512, 512)
        Ls = view(ht_flat, 1024, 2, 3 * P)
        Ms = view(fqt_flat, 0, 2, 3 * P)
        CB = view(fqt_flat, 1024, 2, 3 * P)
        Yf = Y[:, :, :].rearrange("p t n -> p (t n)")
        PT = view(Yf, 0, 2, 2 * S)
        junk = (XS[:, :, :].rearrange("p t n -> p (t n)"), sq)
        XG = view(proj, 0, KC, P)
        SEL = view(proj, 1024, NT, QUAD, CAP)
        SELG = view(proj, 1280, NT, QUAD, CAP)
        SELT = view(proj, 1536, S)
        HID = view(proj, 1792, 4, P)
        SIGM = view(proj, 2304, FF)
        HIDT = view(proj, 2816, 4, P)
        YS = XS[:, :, :].rearrange("p t n -> p (t n)")

        def c_(name, *shape):
            o, w = CONST[name]
            return view(con, o, *(shape or (w,)))

        def r_(name, *shape):
            o, w = ROWS[name]
            return view(row, o, *(shape or (w,)))

        def bc(ap, *shape):
            return ap.unsqueeze(len(ap.shape)).to_broadcast([P, *shape])

        ident, tri = c_("ident"), c_("tri")
        ones = tri[:, P:2 * P]

        bank = [ctx.enter_context(nc.psum_tensor(f"bank{b}", [P, 512], F32)) for b in range(NB)]
        B_GATH, B_SELT, B_UP, B_HIDT, B_DOWN, B_SCAT = (0, 1), 2, (3, 4), 5, (6, 7), (0, 1, 3, 4)

        bank_full = [sem(f"bank_full{b}", USES[b]) for b in range(NB)]
        bank_read = [sem(f"bank_read{b}", USES[b]) for b in range(NB)]
        landed = [sem(f"landed{s}") for s in range(SLOTS)]
        x_in, const_in, g3_in = sem("x_in"), sem("const_in"), sem("g3_in")
        params_in = sem("params_in", 16 * N_PARAMS)
        mem_in = sem("mem_in", 16)
        vector_layer = sem("vector_layer", 1)
        passes_known = sem("passes_known", 1)
        v_step = sem("v_step", V_STEPS)
        a_step = sem("a_step", A_STEPS)
        g_step = sem("g_step", G_STEPS)
        mem_ss, mem_rs = sem("mem_ss", 1), sem("mem_rs", 1)
        k_ss, k_rs = sem("k_ss", 2 * NT), sem("k_rs", 2 * NT)
        q_ss, q_rs = sem("q_ss", NT), sem("q_rs", NT)
        x_ss, x_rs = sem("x_ss", 3 * NT), sem("x_rs", 3 * NT)
        fd_sq = sem("fd_sq", 2 * NT)
        fd_ss, fd_rs = sem("fd_ss", 2 * NT), sem("fd_rs", 2 * NT)
        y_ss, y_rs = sem("y_ss", NT), sem("y_rs", NT)
        MN_ready = sem("MN_ready", 1)
        k_normed, q_normed = sem("k_normed", 2 * NT), sem("q_normed", NT)
        X_ready = sem("X_ready", 2 * NT)
        H_ready = sem("H_ready", 3 * NT)
        pads = sem("pads", 1)
        conv_tap = sem("conv_tap", KC)
        conv_done = sem("conv_done", KC)
        conv_tanh = sem("conv_tanh", KC)
        conv_gated = sem("conv_gated", KC)
        gate_abs, gate_ln = sem("gate_abs", 1), sem("gate_ln", 1)
        DL_ready = sem("DL_ready", 1)
        FQ_ready, DQ_ready = sem("FQ_ready", NT), sem("DQ_ready", NT)
        scores = sem("scores", 4 * NH)
        exps = sem("exps", 4 * NH)
        probs = sem("probs", 4 * NH)
        decays = sem("decays", SH)
        M_ready = sem("M_ready", SH)
        y_head = sem("y_head", SH - 1)
        z_tanh = sem("z_tanh", NT)
        Y_ready = sem("Y_ready", NT)
        xmax = sem("xmax", 2 * XH)
        xprobs = sem("xprobs", 2 * XH)
        g_shift, g_exp = sem("g_shift", 1), sem("g_exp", 1)
        e_shift, e_exp = sem("e_shift", 1), sem("e_exp", 1)
        chosen_ready = sem("chosen_ready", 1)
        units_used = sem("units_used")
        sel_ready, selg_ready = sem("sel_ready"), sem("selg_ready")
        gath_full, XG_ready = sem("gath_full"), sem("XG_ready")
        selt_full, SELT_ready = sem("selt_full"), sem("SELT_ready")
        up_tanh, hid_ready = sem("up_tanh"), sem("hid_ready")
        hidt_full, HIDT_ready = sem("hidt_full"), sem("HIDT_ready")
        YS_ready = sem("YS_ready")
        scat_full = sem("scat_full")
        v_moe = sem("v_moe")
        x_out = sem("x_out")
        waits_passed = sem("waits_passed")

        def bk(job):
            return bank[PLACE[job][0]]

        def full(job, l):
            b, k = PLACE[job]
            return bank_full[b], at(bank_full[b], l, k + 1)

        def free(job, l):
            b, k = PLACE[job]
            return bank_read[b], at(bank_read[b], l, k + 1)

        def copied(job, l):
            b, k = PLACE[job]
            return bank_read[b], at(bank_read[b], l, k + 2)

        def filled(job):
            return bank_full[PLACE[job][0]]

        def read(job):
            return bank_read[PLACE[job][0]]

        def alone(eng):
            eng.sem_inc(waits_passed, 1)

        def load_passes(eng, l):
            return eng.value_load(passes_i[0:1, bass.ds(l, 1)], min_val=0, max_val=8 * DEPTH)

        def moe_quads(eng, l, quad, head=None, new_pass=None):
            before = load_passes(eng, l)
            if head:
                head(0, before * NQ)
            with eng.Fori(1 if head else 0, NQ) as q:
                quad(q, before * NQ + q)
            eng.wait_ge(passes_known, at(passes_known, l, 2))
            alone(eng)
            more = eng.snap(load_passes(eng, l + 1) - before)
            with eng.If(more > 1):
                with eng.Fori(1, more) as ps:
                    if new_pass:
                        new_pass()
                    with eng.Fori(0, NQ) as q:
                        quad(q, (before + ps) * NQ + q)

        block = ctx.enter_context(nc.Block())

        @block.sync
        def _(sp):
            sp.dma_start(X[:, :, :], a["x"][0].rearrange("(t p) d -> p t d", p=P)).then_inc(x_in, 16)
            sp.dma_start(con[:, :], a["const"]).then_inc(const_in, 16)
            sp.wait_ge(params_in, 16 * N_PARAMS)
            sp.wait_ge(mem_in, 16)

            def dense(kind, i, l):
                name = {"kv": "xa_wkv", "wq": "xa_wq", "w_out": "w_out", "wo": "xa_wo"}.get(kind, "w_in")
                c0, w = IN_COLS.get(kind, (C_XBC if kind == "xbc" else 0, 512))
                rows = "a (c p) n -> p (a c) n" if kind in ("w_out", "wo") else "a (p c) n -> p (a c) n"
                v = a[name][bass.ds(l, 1)].rearrange(rows, c=KC)
                return w, v[:, :, c0 + i * 512:c0 + i * 512 + w]

            with sp.Fori(0, DEPTH) as l:
                sp.wait_ge(passes_known, at(passes_known, l, 1))
                quads_before = sp.snap(load_passes(sp, l) * NQ)
                for n, (kind, i) in enumerate(DENSE):
                    if n < SLOTS:
                        sp.wait_ge(units_used, quads_before * MOE_UNITS + SLOTS + n + 1)
                        alone(sp)
                    else:
                        sp.wait_ge(*full(last_use(DENSE[n - SLOTS]), l))
                        alone(sp)
                    w, src = dense(kind, i, l)
                    sp.dma_start(ring_view(n % SLOTS, w), src).then_inc(landed[n % SLOTS], 16)

                def quad(q, quads, head=False):
                    for n in range(MOE_UNITS):
                        name, i = ("exp_w1", "exp_w3", "exp_w2")[n // 4], n % 4
                        w = a[name][bass.ds(l, 1)].rearrange("a e k n -> (a e) k n")[bass.ds(q * QUAD, QUAD)]
                        if name == "exp_w2":
                            src = w.rearrange("e (p c) n -> p e c n", c=4)[:, :, i, :]
                        else:
                            src = w.rearrange("e (p c) n -> p e (c n)", c=KC)[:, :, i * 1024:(i + 1) * 1024]
                        if head and n < SLOTS:
                            sp.wait_ge(*full(last_use(DENSE[len(DENSE) - SLOTS + n]), l))
                            alone(sp)
                        sp.wait_ge(units_used, quads * MOE_UNITS + SLOTS + n + 1)
                        sp.dma_start(ring[:, n % SLOTS, :].rearrange("p (e n) -> p e n", e=QUAD), src
                                     ).then_inc(landed[n % SLOTS], 16)
                moe_quads(sp, l, quad, head=lambda q, quads: quad(q, quads, head=True))
            sp.wait_ge(vector_layer, DEPTH + 1)
            sp.dma_start(out[0].rearrange("(t p) d -> p t d", p=P), X[:, :, :]).then_inc(x_out, 16)
            sp.wait_ge(x_out, 16)

        def small_loads(eng, l):
            def load(dst, src, done):
                eng.dma_start(dst, src).then_inc(done, 16)

            load(mem_raw, a["mem"][0].rearrange("(t p) d -> p t d", p=P), mem_in)
            load(g_ch[:, :, :], a["gains"][bass.ds(l, 1)].rearrange("a p (i c) -> (a p) i c", c=KC), params_in)
            load(p_rows[:, :], a["chan"][bass.ds(l, 1)].rearrange("a k p -> (a k) p"), params_in)
            load(row[:, :], a["rows"][bass.ds(l, 1)].to_broadcast([P, ROWS_W]), params_in)
            load(wr[:, :, :], a["router"][bass.ds(l, 1)].rearrange("a p (c n) -> (a p) c n", c=KC), params_in)

        @block.gpsimd
        def _(pool):
            pool.wait_ge(const_in, 16)
            with pool.Fori(0, DEPTH) as l:
                steps = [0]

                def rsqrt(ap, n, ready, k, done):
                    pool.wait_ge(ready, at(ready, l, k))
                    alone(pool)
                    nc.gpsimd.tensor_scalar(ap, ap, 1.0 / n, EPS, ALU.mult, ALU.add).then_inc(g_step, 1)
                    steps[0] += 1
                    pool.wait_ge(g_step, at(g_step, l, steps[0]))
                    nc.gpsimd.tensor_tensor(ap, ap, c_("half")[:, 0:ap.free_size()], ALU.pow).then_inc(done, 1)

                for t in range(NT):
                    rsqrt(ss[:, 2 + t:3 + t], D, x_ss, t + 1, x_rs)
                rsqrt(ss[:, 0:2], D, mem_ss, 1, mem_rs)
                for i in range(2):
                    for t in range(NT):
                        rsqrt(ssf[:, t, 8 * i:8 * i + 8], HD, fd_ss, NT * i + t + 1, fd_rs)
                for n in range(2):
                    for t in range(NT):
                        rsqrt(ssk[:, t, 2 * n:2 * n + 2], XD, k_ss, NT * n + t + 1, k_rs)
                for t in range(NT):
                    rsqrt(ss[:, 4 + t:5 + t], SI, y_ss, t + 1, y_rs)
                for t in range(NT):
                    rsqrt(ss[:, 2 + t:3 + t], D, x_ss, NT + t + 1, x_rs)
                for t in range(NT):
                    rsqrt(ssk[:, t, :], XD, q_ss, t + 1, q_rs)
                for t in range(NT):
                    rsqrt(ss[:, 2 + t:3 + t], D, x_ss, 2 * NT + t + 1, x_rs)
                assert steps[0] == G_STEPS, ("G", steps)

        @block.scalar
        def _(act):
            small_loads(act, 0)
            act.dma_start(g3[:, :, :], a["gain3"].rearrange("p (l c) -> p l c", c=KC)).then_inc(g3_in, 16)
            act.wait_ge(x_in, 16)
            with act.Fori(0, DEPTH) as l:
                steps = [0]

                def link(ins):
                    steps[0] += 1
                    ins.then_inc(a_step, 1)
                    act.wait_ge(a_step, at(a_step, l, steps[0]))

                def copy_out(job, dst, src):
                    act.wait_ge(*full(job, l))
                    nc.scalar.copy(dst, src).then_inc(read(job), 1)

                def square_x(k, t):
                    nc.scalar.activation(junk[t if k == 0 else 0], X[:, t, :], ACT.Square,
                                         accum_out=ss[:, 2 + t:3 + t]).then_inc(x_ss, 1)

                def norm_x(k, t):
                    act.wait_ge(x_rs, at(x_rs, l, NT * k + t + 1))
                    nc.scalar.activation(H[:, t], X[:, t, :].rearrange("p (q c) -> p c q", c=KC), ACT.Copy,
                                         scale=ss[:, 2 + t:3 + t]).then_inc(H_ready, 1)

                act.wait_ge(vector_layer, at(vector_layer, l, 1))
                for t in range(NT):
                    square_x(0, t)
                norm_x(0, 0)
                act.wait_ge(mem_in, at(mem_in, l, 16))
                act.wait_ge(x_ss, at(x_ss, l, NT))
                for t in range(NT):
                    last = nc.scalar.activation(junk[t], mem_raw[:, t, :], ACT.Square, accum_out=ss[:, t:t + 1])
                last.then_inc(mem_ss, 1)
                act.wait_ge(mem_rs, at(mem_rs, l, 1))
                for t in range(NT):
                    last = nc.scalar.activation(MN[:, t], mem_raw[:, t, :].rearrange("p (q c) -> p c q", c=KC),
                                                ACT.Copy, scale=ss[:, t:t + 1])
                last.then_inc(MN_ready, 1)
                act.wait_ge(params_in, at(params_in, l, 16 * N_PARAMS))
                link(nc.scalar.activation(negA[:, :], r_("ssd_A_log"), ACT.Exp))

                def copy_in(n):
                    for t in range(NT):
                        w = IN_COLS[n][1]
                        copy_out(("in", n, t), pt[t][:, IN_DEST[n]:IN_DEST[n] + w], bk(("in", n, t))[:, 0:w])

                def square_heads(n, buf):
                    for t in range(NT):
                        act.wait_ge(*copied(("in", n, t), l))
                        nc.scalar.activation(buf[:, t * 512:(t + 1) * 512], pt[t][:, IN_DEST[n]:IN_DEST[n] + 512],
                                             ACT.Square).then_inc(fd_sq, 1)

                copy_in("dt")
                copy_in("fv")
                act.wait_ge(gate_abs, at(gate_abs, l, 1))
                link(nc.scalar.activation(gate_e[:, :, :], gate_e[:, :, :], ACT.Exp))
                nc.scalar.activation(gate_e[:, :, :], gate_e[:, :, :], ACT.Ln, bias=1.0).then_inc(gate_ln, 1)
                copy_in("fqk")
                square_heads("fqk", Yf)
                act.wait_ge(pads, at(pads, l, 1))
                for i in range(4):
                    job = ("xbc", i)
                    copy_out(job, xin[:, 2 * i:2 * i + 2, 3:], bk(job)[:, :].rearrange("p (c s) -> p c s", c=2))
                for t in range(NT):
                    for i in range(2):
                        job = ("fT", t, i)
                        copy_out(job, FQT[0:HD + 2, 4 * i:4 * i + 4, t * P:(t + 1) * P],
                                 bk(job)[0:HD + 2, :].rearrange("p (c s) -> p c s", c=4))
                copy_in("dqk")
                square_heads("dqk", sq)
                copy_in("z")
                copy_in("dv")

                def exp_scores(k):
                    for t in range(NT):
                        act.wait_ge(scores, at(scores, l, 2 * k + t + 1))
                        w = (t + 1) * P
                        nc.scalar.activation(SCO[:, k % 2, t, 0:w], SCO[:, k % 2, t, 0:w], ACT.Exp,
                                             bias=smax[:, k % 2, t:t + 1], accum_out=ssum[:, k % 2, t:t + 1]
                                             ).then_inc(exps, 1)

                def take_kv(n, t):
                    job = ("kv", n, t)
                    if n >= 2:
                        return copy_out(job, VM[:, t, (n - 2) * 512:(n - 1) * 512], bk(job)[:, :])
                    if n == 1:
                        act.wait_ge(*full(("kT", 0, t), l))
                    copy_out(job, K_tm[:, t, :], bk(job)[:, :])
                    act.wait_ge(*copied(job, l))
                    for h in range(2):
                        part = slice(h * XD, (h + 1) * XD)
                        last = nc.scalar.activation(ve[:, part], K_tm[:, t, part], ACT.Square,
                                                    accum_out=ssk[:, t, 2 * n + h:2 * n + h + 1])
                    last.then_inc(k_ss, 1)

                for k in range(len(HEADS) + 1):
                    if k < KC:
                        if k >= 2:
                            act.wait_ge(conv_gated, at(conv_gated, l, k - 1))
                        else:
                            act.wait_ge(*full(("fT", 1, 1), l))
                            act.wait_ge(*copied(("params",), l))
                        act.wait_ge(*copied(("xbc", k // 2), l))
                        nc.scalar.activation(cv[:, k % 2, :], xin[:, k, 0:S], ACT.Identity,
                                             bias=p_ch[:, 32 + k:33 + k], scale=p_ch[:, k:k + 1]).then_inc(conv_tap, 1)
                    if k < len(HEADS):
                        exp_scores(k)
                        act.wait_ge(conv_done, at(conv_done, l, k + 1))
                        nc.scalar.activation(sig[:, k % 2, :], cv[:, k % 2, :], ACT.Tanh, scale=0.5
                                             ).then_inc(conv_tanh, 1)
                    for job in BETWEEN[k]:
                        if job[0] == "dT":
                            t = job[1]
                            copy_out(job, DQT[:, :, t * P:(t + 1) * P],
                                     bk(job)[:, :].rearrange("p (c s) -> p c s", c=4))
                        elif job[0] == "kv":
                            take_kv(*job[1:])
                    if k:
                        job = ("pT", HEADS[k - 1])
                        copy_out(job, PT[:, (k - 1) % 2, 0:3 * P], bk(job)[:, 0:3 * P])
                        if k % 2 == 0:
                            job = ("o", HEADS[k - 1])
                            copy_out(job, mixT[:, :, k // 2 - 1, :], bk(job)[:, 0:S].rearrange("p (t s) -> p t s", t=NT))
                for t in range(NT):
                    job = ("xsT", t)
                    act.wait_ge(*full(job, l))
                    nc.scalar.mul(XS[:, t, :], bk(job)[:, :], 0.5).then_inc(read(job), 1)
                for t in range(NT):
                    nc.scalar.activation(sq[:, t * SI:(t + 1) * SI], pt[t][:, T_Z:T_Z + SI], ACT.Tanh, scale=0.5
                                         ).then_inc(z_tanh, 1)
                for h in range(SH):
                    act.wait_ge(*copied(("L", h), l))
                    nc.scalar.activation(Ls[:, h % 2, :], Ls[:, h % 2, :], ACT.Exp).then_inc(decays, 1)
                take_kv(3, 1)

                for t in range(NT):
                    act.wait_ge(X_ready, at(X_ready, l, t + 1))
                    square_x(1, t)
                    norm_x(1, t)
                for t in range(NT):
                    for n in range(2):
                        copy_out(("q", n, t), Q_tm[:, t, n * 512:(n + 1) * 512], bk(("q", n, t))[:, :])
                    act.wait_ge(*copied(("q", 0, t), l))
                    act.wait_ge(*copied(("q", 1, t), l))
                    for h in range(XH):
                        part = slice(h * XD, (h + 1) * XD)
                        last = nc.scalar.activation(junk[0][:, part], Q_tm[:, t, part], ACT.Square,
                                                    accum_out=ssk[:, t, h:h + 1])
                    last.then_inc(q_ss, 1)
                for j in range(len(CROSS) + 1):
                    if j < len(CROSS):
                        job = ("xs", *CROSS[j])
                        act.wait_ge(xmax, at(xmax, l, j + 1))
                        nc.scalar.activation(SCO[:, j % 2, 0, :], bk(job)[:, 0:S], ACT.Exp,
                                             bias=smax[:, j % 2, 0:1], scale=XD ** -0.5,
                                             accum_out=ssum[:, j % 2, 0:1]).then_inc(read(job), 1)
                    if j:
                        t, h = CROSS[j - 1]
                        copy_out(("xpT", t, h), PT[:, (j - 1) % 2, 0:2 * P], bk(("xpT", t, h))[:, 0:2 * P])
                        copy_out(("xo", t, h), mixT[:, t, 2 * h:2 * h + 2, :],
                                 bk(("xo", t, h))[:, 0:2 * P].rearrange("p (c s) -> p c s", c=2))
                for t in range(NT):
                    act.wait_ge(X_ready, at(X_ready, l, NT + t + 1))
                    square_x(2, t)
                    norm_x(2, t)
                act.wait_ge(g_shift, at(g_shift, l, 1))
                nc.scalar.activation(rg[:, :, 1, :], rg[:, :, 1, :], ACT.Exp).then_inc(g_exp, 1)
                act.wait_ge(e_shift, at(e_shift, l, 1))
                nc.scalar.activation(rt[:, :, 4:5], rt[:, :, 4:5], ACT.Exp).then_inc(e_exp, 1)
                assert steps[0] == A_STEPS, ("A", steps)
                act.wait_ge(passes_known, at(passes_known, l, 2))
                alone(act)
                with act.If(l < DEPTH - 1):
                    small_loads(act, (l + 1).with_bounds(min_val=1, max_val=DEPTH - 1))

                def quad(q, quads):
                    act.wait_ge(selt_full, quads + 1)
                    nc.scalar.copy(SELT, bank[B_SELT][:, 0:S]).then_inc(SELT_ready, 1)
                    act.wait_ge(units_used, quads * MOE_UNITS + MOE_UNITS + 4)
                    nc.scalar.activation(SIGM, bank[B_UP[0]][:, :], ACT.Tanh, scale=0.5).then_inc(up_tanh, 1)
                    act.wait_ge(hidt_full, quads + 1)
                    nc.scalar.copy(HIDT, bank[B_HIDT][:, :].rearrange("p (c s) -> p c s", c=4)).then_inc(HIDT_ready, 1)
                    act.wait_ge(units_used, quads * MOE_UNITS + MOE_UNITS + 12)
                    for n in range(2):
                        last = nc.scalar.copy(YS[:, n * 512:(n + 1) * 512], bank[B_DOWN[n]][:, :])
                    last.then_inc(YS_ready, 1)
                moe_quads(act, l, quad)

        @block.vector
        def _(dve):
            v = nc.vector
            dve.wait_ge(const_in, 16)
            dve.wait_ge(g3_in, 16)
            v.memset(passes[:, :], 0.0)
            v.memset(passes_i[:, :], 0).then_inc(passes_known, 1)
            for b in range(NB):
                dve.sem_inc(bank_read[b], 1)
            dve.sem_inc(vector_layer, 1)
            dve.sem_inc(units_used, MOE_UNITS)
            with dve.Fori(0, DEPTH) as l:
                steps = [0]

                def link(ins):
                    steps[0] += 1
                    ins.then_inc(v_step, 1)
                    dve.wait_ge(v_step, at(v_step, l, steps[0]))

                def gained(job, gain, dst):
                    dve.wait_ge(*full(job, l))
                    v.tensor_tensor(dst, bk(job)[:, :].rearrange("p (c s) -> p c s", c=4), bc(gain, 4, P), ALU.mult
                                    ).then_inc(read(job), 1)

                def copy4(job, dst):
                    dve.wait_ge(*full(job, l))
                    v.tensor_copy(dst, bk(job)[:, :].rearrange("p (c s) -> p c s", c=4)).then_inc(read(job), 1)

                def transposed_x(name, gain, t):
                    for i in range(2):
                        gained((name, t, i), gain[:, 4 * i:4 * i + 4], HT[:, t, 4 * i:4 * i + 4, :])

                def times_gain(parts, rs, gain):
                    for h, part in enumerate(parts):
                        last = v.scalar_tensor_tensor(part, part, rs[:, h:h + 1], r_(gain), ALU.mult, ALU.mult)
                    return last

                dve.wait_ge(x_rs, at(x_rs, l, 2))
                v.tensor_scalar(H[:, 1], X[:, 1, :].rearrange("p (q c) -> p c q", c=KC), ss[:, 3:4], None, ALU.mult
                                ).then_inc(H_ready, 1)
                dve.wait_ge(params_in, at(params_in, l, 16 * N_PARAMS))
                for t in range(NT):
                    transposed_x("hT1", g_ch[:, G_X, :], t)

                for t in range(NT):
                    dve.wait_ge(*copied(("in", "dt", t), l))
                    dve.wait_ge(*copied(("in", "fv", t), l))
                    v.tensor_tensor(gate_in[:, t, 0:NH], pt[t][:, T_FF:T_FF + NH], r_("fox_fgate_b"), ALU.add)
                    last = v.tensor_tensor(gate_in[:, t, NH:], pt[t][:, T_DT:T_DT + SH], r_("ssd_dt_bias"), ALU.add)
                link(last)
                link(v.tensor_scalar(gate_e[:, :, :], gate_in[:, :, :], -1.0, None, ALU.mult))
                v.tensor_tensor(gate_e[:, :, :], gate_e[:, :, :], gate_in[:, :, :], ALU.min).then_inc(gate_abs, 1)
                dve.wait_ge(gate_ln, at(gate_ln, l, 1))
                v.scalar_tensor_tensor(DL[:, :, 0:NH], gate_in[:, :, 0:NH], 0.0, gate_e[:, :, 0:NH], ALU.min,
                                       ALU.subtract)
                link(v.scalar_tensor_tensor(DTs[:, :, :], gate_in[:, :, NH:], 0.0, gate_e[:, :, NH:], ALU.max,
                                            ALU.add))
                dve.wait_ge(a_step, at(a_step, l, 1))
                v.scalar_tensor_tensor(DL[:, :, NH:], DTs[:, :, :], -1.0,
                                       negA[:, :].unsqueeze(1).to_broadcast([P, NT, SH]), ALU.mult, ALU.mult
                                       ).then_inc(DL_ready, 1)
                dve.wait_ge(*full(("params",), l))
                v.tensor_copy(p_ch[:, :], bk(("params",))[:, 0:44]).then_inc(read(("params",)), 1)
                for t in range(NT):
                    for i in range(2):
                        gained(("memT", t, i), g_ch[:, G_MEM, 4 * i:4 * i + 4], MT[:, t, 4 * i:4 * i + 4, :])
                v.memset(xin[:, :, 0:3], 0.0).then_inc(pads, 1)

                def sum_squares(i, buf):
                    for t in range(NT):
                        dve.wait_ge(fd_sq, at(fd_sq, l, NT * i + t + 1))
                        v.tensor_reduce(ssf[:, t, 8 * i:8 * i + 8], view(buf, 512 * t, 8, HD), AX.X, ALU.add
                                        ).then_inc(fd_ss, 1)

                sum_squares(0, Yf)
                job = ("cum",)
                dve.wait_ge(*full(job, l))
                link(v.tensor_copy(CUM[:, :, :], bk(job)[:, 0:NT * 12].rearrange("p (t n) -> p t n", t=NT)))
                v.memset(FQ[:, :, 0:NH, HD:HD + 1], 1.0)
                v.memset(FQ[:, :, NH:, HD + 1:HD + 2], 1.0)
                v.tensor_scalar(FQ[:, :, 0:NH, HD + 1], CUM[:, :, 0:NH], HD ** 0.5, None, ALU.mult)
                v.tensor_scalar(FQ[:, :, NH:, HD], CUM[:, :, 0:NH], -HD ** 0.5, None, ALU.mult
                                ).then_inc(read(job), 1)
                for t in range(NT):
                    dve.wait_ge(fd_rs, at(fd_rs, l, t + 1))
                    link(v.tensor_tensor(FQ[:, t, :, 0:HD], view(pt[t], 0, 2 * NH, HD), bc(ssf[:, t, 0:8], 8, HD),
                                         ALU.mult))
                    fq = FQ[:, t, :, 0:HD].rearrange("p (b h) d -> p b h d", b=2)
                    gain = view(row, ROWS["fox_qn_g"][0], 2, HD)
                    v.tensor_tensor(fq, fq, gain.unsqueeze(2).to_broadcast([P, 2, NH, HD]), ALU.mult
                                    ).then_inc(FQ_ready, 1)

                def dilated_qk(t):
                    dve.wait_ge(fd_rs, at(fd_rs, l, NT + t + 1))
                    dq = view(pt[t], T_DQK, 2 * NH, HD)
                    link(v.tensor_tensor(dq, dq, bc(ssf[:, t, 8:16], 8, HD), ALU.mult))
                    d4 = view(pt[t], T_DQK, 2, NH, HD)
                    gain = view(row, ROWS["dil_qn_g"][0], 2, HD)
                    link(v.tensor_tensor(d4, d4, gain.unsqueeze(2).to_broadcast([P, 2, NH, HD]), ALU.mult))
                    cos = view(con, CONST["cos"][0] + 8 * t, 8).unsqueeze(1).to_broadcast([P, 8, 8])
                    sin = view(con, CONST["sin"][0] + 8 * t, 8).unsqueeze(1).to_broadcast([P, 8, 8])
                    v.tensor_tensor(rope[:, 0], dq[:, :, 0:8], cos, ALU.mult)
                    v.tensor_tensor(rope[:, 1], dq[:, :, 8:16], sin, ALU.mult)
                    v.tensor_tensor(rope[:, 2], dq[:, :, 8:16], cos, ALU.mult)
                    link(v.tensor_tensor(rope[:, 3], dq[:, :, 0:8], sin, ALU.mult))
                    v.tensor_tensor(dq[:, :, 0:8], rope[:, 0], rope[:, 1], ALU.subtract)
                    v.tensor_tensor(dq[:, :, 8:16], rope[:, 2], rope[:, 3], ALU.add).then_inc(DQ_ready, 1)

                def mask_scores(k):
                    fam = HEADS[k][0]
                    for t in range(NT):
                        w, job = (t + 1) * P, ("s", HEADS[k], t)
                        if fam == "fox":
                            mask = c_("causal")[:, S - w:S]
                        else:
                            mask = c_("dilated")[:, t * P:t * P + w]
                        dve.wait_ge(*full(job, l))
                        if k >= 2 and t == 0:
                            dve.wait_ge(*full(("pT", HEADS[k - 2]), l))
                        alone(dve)
                        v.tensor_tensor_reduce(out=SCO[:, k % 2, t, 0:w], in0=bk(job)[:, 0:w], in1=mask,
                                               scale=HD ** -0.5, scalar=-BIG, op0=ALU.add, op1=ALU.max,
                                               accum_out=smax[:, k % 2, t:t + 1]).then_inc(read(job), 1)
                        dve.wait_ge(*copied(job, l))
                        v.tensor_scalar(smax[:, k % 2, t:t + 1], smax[:, k % 2, t:t + 1], -1.0, None, ALU.mult
                                        ).then_inc(scores, 1)

                def normalize(p, total, done):
                    link(v.reciprocal(total, total))
                    v.tensor_scalar(p, p, total, None, ALU.mult).then_inc(done, 1)

                def conv(c):
                    dve.wait_ge(conv_tap, at(conv_tap, l, c + 1))
                    o = cv[:, c % 2, :]
                    for k in range(1, 4):
                        ins = v.scalar_tensor_tensor(o, xin[:, c, k:k + S], p_ch[:, 8 * k + c:8 * k + c + 1], o,
                                                     ALU.mult, ALU.add)
                        if k < 3:
                            link(ins)
                    ins.then_inc(conv_done, 1)

                def gate(c):
                    dve.wait_ge(conv_tanh, at(conv_tanh, l, c + 1))
                    v.scalar_tensor_tensor(xc[:, c, :], sig[:, c % 2, :], 1.0, cv[:, c % 2, :], ALU.add, ALU.mult
                                           ).then_inc(conv_gated, 1)

                for k in range(len(HEADS) + 1):
                    if k == 0:
                        sum_squares(1, sq)
                        dve.wait_ge(fd_ss, at(fd_ss, l, 2 * NT))
                    if k < len(HEADS):
                        mask_scores(k)
                        conv(k)
                    if k == 1:
                        for t in range(NT):
                            dilated_qk(t)
                    if k:
                        gate(k - 1)
                    for job in BETWEEN[k - 1] if k else ():
                        if job[0] == "kv" and job[1] < 2:
                            n, t = job[1:]
                            dve.wait_ge(k_rs, at(k_rs, l, NT * n + t + 1))
                            times_gain([K_tm[:, t, h * XD:(h + 1) * XD] for h in range(2)],
                                       ssk[:, t, 2 * n:2 * n + 2], "xa_kn_g").then_inc(k_normed, 1)
                    for job in BETWEEN[k]:
                        if job[0] == "kT":
                            n, t = job[1:]
                            copy4(job, KT[:, 4 * n:4 * n + 4, t * P:(t + 1) * P])
                    if k < len(HEADS):
                        for t in range(NT):
                            dve.wait_ge(exps, at(exps, l, 2 * k + t + 1))
                            normalize(SCO[:, k % 2, t, 0:(t + 1) * P], ssum[:, k % 2, t:t + 1], probs)

                for g in range(2):
                    job = ("cb", g)
                    dve.wait_ge(*full(job, l))
                    v.scalar_tensor_tensor(CB[:, g, :], bk(job)[:, 0:3 * P], 0.25, tri, ALU.mult, ALU.mult
                                           ).then_inc(read(job), 1)
                for g in range(2):
                    dve.wait_ge(*copied(("cb", g), l))

                def exponents(h):
                    job = ("L", h)
                    if h >= 2:
                        dve.wait_ge(M_ready, at(M_ready, l, h - 1))
                    dve.wait_ge(*full(job, l))
                    v.tensor_scalar(Ls[:, h % 2, 0:S], bk(job)[:, 0:S], CUM[:, 0, NH + h:NH + h + 1], 0.0,
                                    ALU.subtract, ALU.min)
                    v.tensor_scalar(Ls[:, h % 2, S:], bk(job)[:, P:S], CUM[:, 1, NH + h:NH + h + 1], 0.0,
                                    ALU.subtract, ALU.min).then_inc(read(job), 1)

                exponents(0)
                for h in range(SH):
                    if h + 1 < SH:
                        exponents(h + 1)
                    dve.wait_ge(decays, at(decays, l, h + 1))
                    if h >= 2:
                        dve.wait_ge(y_head, at(y_head, l, h - 1))
                    v.scalar_tensor_tensor(Ms[:, h % 2, 0:S], Ls[:, h % 2, 0:S], DTs[:, 0, h:h + 1],
                                           CB[:, h // 4, 0:S], ALU.mult, ALU.mult)
                    v.scalar_tensor_tensor(Ms[:, h % 2, S:], Ls[:, h % 2, S:], DTs[:, 1, h:h + 1],
                                           CB[:, h // 4, S:], ALU.mult, ALU.mult).then_inc(M_ready, 1)
                for t in range(NT):
                    dve.wait_ge(*copied(("xsT", t), l))
                    link(v.tensor_tensor(view(Y[:, t, :], 0, SH, SP_), view(XS[:, t, :], 0, SH, SP_),
                                         bc(r_("ssd_D"), SH, SP_), ALU.mult))
                    dve.wait_ge(*full(("y", t), l))
                    v.tensor_tensor(Y[:, t, :], Y[:, t, :], bk(("y", t))[:, :], ALU.add).then_inc(read(("y", t)), 1)
                    dve.wait_ge(z_tanh, at(z_tanh, l, t + 1))
                    e = sq[:, t * SI:(t + 1) * SI]
                    link(v.scalar_tensor_tensor(e, e, 1.0, pt[t][:, T_Z:T_Z + SI], ALU.add, ALU.mult))
                    link(v.scalar_tensor_tensor(Y[:, t, :], e, 0.5, Y[:, t, :], ALU.mult, ALU.mult))
                    v.tensor_tensor_reduce(out=ve[:, :], in0=Y[:, t, :], in1=Y[:, t, :], scale=1.0, scalar=0.0,
                                           op0=ALU.mult, op1=ALU.add, accum_out=ss[:, 4 + t:5 + t]).then_inc(y_ss, 1)
                for t in range(NT):
                    dve.wait_ge(y_rs, at(y_rs, l, t + 1))
                    v.tensor_scalar(Y[:, t, :], Y[:, t, :], ss[:, 4 + t:5 + t], None, ALU.mult).then_inc(Y_ready, 1)
                for t in range(NT):
                    gained(("ysT", t), p_ch[:, 40:44], mixT[:, t, 4:8, :])

                def residual(name, n, t):
                    job = (name, n, t)
                    dve.wait_ge(*full(job, l))
                    x = X[:, t, n * 512:(n + 1) * 512]
                    v.tensor_tensor(x, x, bk(job)[:, :], ALU.add).then_inc(read(job), 1)
                    if n == 1:
                        dve.wait_ge(*copied((name, 0, t), l))
                        dve.wait_ge(*copied((name, 1, t), l))
                        dve.sem_inc(X_ready, 1)

                for t in range(NT):
                    for n in range(2):
                        residual("out1", n, t)
                for t in range(NT):
                    transposed_x("hT2", g_ch[:, G_2, :], t)
                for t in range(NT):
                    dve.wait_ge(q_rs, at(q_rs, l, t + 1))
                    times_gain([Q_tm[:, t, h * XD:(h + 1) * XD] for h in range(XH)], ssk[:, t, :], "xa_qn_g"
                               ).then_inc(q_normed, 1)

                def transposed_q(t):
                    for i in range(2):
                        copy4(("qT", t, i), QT[:, t, 4 * i:4 * i + 4, :])

                transposed_q(0)
                for j in range(len(CROSS) + 1):
                    if j < len(CROSS):
                        job = ("xs", *CROSS[j])
                        dve.wait_ge(*full(job, l))
                        if j >= 2:
                            dve.wait_ge(*full(("xpT", *CROSS[j - 2]), l))
                        m = smax[:, j % 2, 0:1]
                        link(v.tensor_reduce(m, bk(job)[:, 0:S], AX.X, ALU.max))
                        v.tensor_scalar(m, m, -XD ** -0.5, None, ALU.mult).then_inc(xmax, 1)
                    if j == 2:
                        transposed_q(1)
                    if j < len(CROSS):
                        dve.wait_ge(*copied(job, l))
                        normalize(SCO[:, j % 2, 0, :], ssum[:, j % 2, 0:1], xprobs)
                    if j in (6, 7):
                        residual("out2", j - 6, 0)
                residual("out2", 0, 1)
                transposed_x("hT3", g3[:, bass.ds(l, 1), :].rearrange("p a c -> p (a c)"), 0)
                residual("out2", 1, 1)
                transposed_x("hT3", g3[:, bass.ds(l, 1), :].rearrange("p a c -> p (a c)"), 1)

                job = ("router",)
                dve.wait_ge(*full(job, l))
                bias = view(row, ROWS["router_bg"][0], NG + NE).unsqueeze(1).to_broadcast([P, NT, NG + NE])
                link(v.tensor_tensor(lg[:, :, :], bk(job)[:, 0:NT * (NG + NE)].rearrange("p (t n) -> p t n", t=NT),
                                     bias, ALU.add))

                def first_max(src, n, top, hot):
                    tmp = first[:, :, 0:n]
                    down = c_("down")[:, 0:n].unsqueeze(1).to_broadcast([P, NT, n])
                    link(v.tensor_reduce(top, src, AX.X, ALU.max))
                    link(v.tensor_tensor(tmp, src, top.to_broadcast([P, NT, n]), ALU.is_equal))
                    link(v.tensor_tensor(tmp, tmp, down, ALU.mult))
                    link(v.tensor_reduce(rt[:, :, 7:8], tmp, AX.X, ALU.max))
                    link(v.tensor_tensor(hot, tmp, rt[:, :, 7:8].to_broadcast([P, NT, n]), ALU.is_equal))

                gmax, m1, m2 = rt[:, :, 0:1], rt[:, :, 1:2], rt[:, :, 2:3]
                g_gate, e21, p1, p2 = rt[:, :, 3:4], rt[:, :, 4:5], rt[:, :, 5:6], rt[:, :, 6:7]
                first_max(lg[:, :, 0:NG], NG, gmax, rg[:, :, 0, :])
                v.tensor_tensor(rg[:, :, 1, :], lg[:, :, 0:NG], gmax.to_broadcast([P, NT, NG]), ALU.subtract
                                ).then_inc(g_shift, 1)
                link(v.tensor_scalar(rg[:, :, 2, :], rg[:, :, 0, :], 1.0, BIG, ALU.subtract, ALU.mult))
                link(v.tensor_tensor(em[:, :, :].rearrange("p t (g e) -> p t g e", g=NG),
                                     lg[:, :, NG:].rearrange("p t (g e) -> p t g e", g=NG),
                                     rg[:, :, 2, :].unsqueeze(3).to_broadcast([P, NT, NG, EPG]), ALU.add))
                first_max(em[:, :, :], NE, m1, oh[:, 0])
                link(v.scalar_tensor_tensor(em[:, :, :], oh[:, 0], -BIG, em[:, :, :], ALU.mult, ALU.add))
                first_max(em[:, :, :], NE, m2, oh[:, 1])
                v.tensor_tensor(e21, m2, m1, ALU.subtract).then_inc(e_shift, 1)
                v.tensor_tensor(chosen[:, :, :], oh[:, 0], oh[:, 1], ALU.add).then_inc(chosen_ready, 1)
                dve.wait_ge(g_exp, at(g_exp, l, 1))
                link(v.tensor_reduce(g_gate, rg[:, :, 1, :], AX.X, ALU.add))
                dve.wait_ge(e_exp, at(e_exp, l, 1))
                link(v.tensor_scalar(p1, e21, 1.0, None, ALU.add))
                link(v.tensor_tensor(p1, p1, g_gate, ALU.mult))
                link(v.reciprocal(p1, p1))
                link(v.tensor_tensor(p2, p1, e21, ALU.mult))
                link(v.tensor_tensor(gates[:, :, :], oh[:, 0], p1.to_broadcast([P, NT, NE]), ALU.mult))
                link(v.tensor_tensor(em[:, :, :], oh[:, 1], p2.to_broadcast([P, NT, NE]), ALU.mult))
                link(v.tensor_tensor(gates[:, :, :], gates[:, :, :], em[:, :, :], ALU.add))
                job = ("rank",)
                dve.wait_ge(*full(job, l))
                rk = bk(job)[:, 0:3 * NE].rearrange("p (t n) -> p t n", t=3)
                link(v.tensor_tensor(rank[:, :, :], chosen[:, :, :], rk[:, 0:NT, :], ALU.mult))
                link(v.tensor_scalar(rank[:, :, :], rank[:, :, :], 1.0, None, ALU.subtract))
                link(v.tensor_reduce(passes[:, 1:2], rk[:, NT, :], AX.X, ALU.max))
                link(v.tensor_tensor(over[:, :], passes[:, 1:2].to_broadcast([P, 8]), c_("caps"), ALU.is_gt))
                link(v.tensor_reduce(passes[:, 1:2], over[:, :], AX.X, ALU.add))
                link(v.tensor_tensor(passes[:, 0:1], passes[:, 0:1], passes[:, 1:2], ALU.add))
                v.tensor_copy(passes_i[:, bass.ds(l + 1, 1)], passes[:, 0:1]).then_inc(passes_known, 1)
                link(v.tensor_copy(slot_no[:, :], c_("slots")))
                dve.sem_inc(read(("router",)), 1)
                dve.sem_inc(read(("rank",)), 1)
                assert steps[0] == V_STEPS, ("V", steps)

                def quad(q, quads):
                    n_steps = [0]

                    def step(ins):
                        n_steps[0] += 1
                        ins.then_inc(v_moe, 1)
                        dve.wait_ge(v_moe, quads * V_MOE + n_steps[0])

                    mine = rank[:, :, bass.ds(q * QUAD, QUAD)].unsqueeze(3).to_broadcast([P, NT, QUAD, CAP])
                    places = slot_no[:, :].unsqueeze(1).unsqueeze(1).to_broadcast([P, NT, QUAD, CAP])
                    my_gates = gates[:, :, bass.ds(q * QUAD, QUAD)].unsqueeze(3).to_broadcast([P, NT, QUAD, CAP])
                    v.tensor_tensor(SEL, mine, places, ALU.is_equal).then_inc(sel_ready, 1)
                    dve.wait_ge(sel_ready, quads + 1)
                    v.tensor_tensor(SELG, SEL, my_gates, ALU.mult).then_inc(selg_ready, 1)
                    my_gain = g3[:, bass.ds(l, 1), :].rearrange("p a c -> p (a c)")
                    for i in range(2):
                        dve.wait_ge(gath_full, quads * 2 + i + 1)
                        v.tensor_tensor(XG[:, 4 * i:4 * i + 4, :],
                                        bank[B_GATH[i]][:, :].rearrange("p (c s) -> p c s", c=4),
                                        bc(my_gain[:, 4 * i:4 * i + 4], 4, P), ALU.mult).then_inc(XG_ready, 1)
                    dve.wait_ge(up_tanh, quads + 1)
                    step(v.scalar_tensor_tensor(SIGM, SIGM, 1.0, bank[B_UP[0]][:, :], ALU.add, ALU.mult))
                    dve.wait_ge(units_used, quads * MOE_UNITS + MOE_UNITS + 8)
                    v.scalar_tensor_tensor(HID, SIGM.rearrange("p (q c) -> p c q", c=4), 0.5,
                                           bank[B_UP[1]][:, :].rearrange("p (q c) -> p c q", c=4), ALU.mult, ALU.mult
                                           ).then_inc(hid_ready, 1)
                    for i in range(4):
                        t, n = i // 2, i % 2
                        dve.wait_ge(scat_full, quads * 4 + i + 1)
                        x = X[:, t, n * 512:(n + 1) * 512]
                        last = v.tensor_tensor(x, x, bank[B_SCAT[i]][:, :], ALU.add)
                    step(last)
                    assert n_steps[0] == V_MOE

                def new_pass():
                    v.tensor_scalar(slot_no[:, :], slot_no[:, :], float(CAP), None, ALU.add)
                moe_quads(dve, l, quad, new_pass=new_pass)
                dve.sem_inc(vector_layer, 1)

        @block.tensor
        def _(pe):
            def mm(dst, lhsT, rhs, start=True, stop=True):
                return nc.tensor.matmul(dst, lhsT, rhs, start=start, stop=stop)

            pe.wait_ge(const_in, 16)
            with pe.Fori(0, DEPTH) as l:
                pe.wait_ge(passes_known, at(passes_known, l, 1))
                turn = pe.snap(load_passes(pe, l) * (NQ * MOE_TURNS) + l * DENSE_TURNS)
                pe.wait_ge(vector_layer, at(vector_layer, l, 1))

                def transposes(job, srcs, last_wait=lambda eng: None):
                    pe.wait_ge(*free(job, l))
                    last_wait(pe)
                    for i, src in enumerate(srcs):
                        last = nc.tensor.transpose(bk(job)[0:src.shape[1], i * P:i * P + src.shape[0]], src,
                                                   ident[0:src.shape[0], 0:src.shape[0]])
                    last.then_inc(filled(job), 1)

                def arrived(unit):
                    n = DENSE.index(unit)
                    pe.wait_ge(landed[n % SLOTS], (turn + n // SLOTS + 1) * 16)
                    return ring_view(n % SLOTS, IN_COLS.get(unit[0], (0, 512))[1])

                def tile_job(job, unit, t, lhs):
                    w = arrived(unit)
                    pe.wait_ge(*free(job, l))
                    for c in range(KC):
                        last = mm(bk(job)[:, 0:w.shape[2]], lhs[:, t, c, :], w[:, c, :], start=c == 0, stop=c == KC - 1)
                    last.then_inc(filled(job), 1)

                def both_copied(name, t):
                    for i in range(2):
                        pe.wait_ge(*copied((name, t, i), l))

                def transpose_h(k, name, t):
                    pe.wait_ge(H_ready, at(H_ready, l, NT * k + (NT if k == 0 else t + 1)))
                    for i in range(2):
                        transposes((name, t, i), [H[:, t, 4 * i + j, :] for j in range(4)])

                for t in range(NT):
                    transpose_h(0, "hT1", t)
                for n in IN_FIRST:
                    for t in range(NT):
                        both_copied("hT1", t)
                        tile_job(("in", n, t), (n, 0), t, HT)
                pe.wait_ge(params_in, at(params_in, l, 16 * N_PARAMS))
                transposes(("params",), [p_rows[:, :]], last_wait=alone)
                pe.wait_ge(MN_ready, at(MN_ready, l, 1))
                for t in range(NT):
                    for i in range(2):
                        transposes(("memT", t, i), [MN[:, t, 4 * i + j, :] for j in range(4)])
                for i in range(4):
                    job = ("xbc", i)
                    w = arrived(("xbc", i // 2))
                    pe.wait_ge(*free(job, l))
                    for j in range(2):
                        c0 = (i % 2 * 2 + j) * P
                        for c in range(KC):
                            last = mm(bk(job)[:, j * S:(j + 1) * S], w[:, c, c0:c0 + P], HT[:, :, c, :],
                                      start=c == 0, stop=c == KC - 1)
                    last.then_inc(filled(job), 1)

                job = ("cum",)
                pe.wait_ge(DL_ready, at(DL_ready, l, 1))
                pe.wait_ge(*free(job, l))
                mm(bk(job)[:, 0:12], tri[:, 0:P], DL[:, 0, :])
                mm(bk(job)[:, 12:24], ones, DL[:, 0, :], stop=False)
                mm(bk(job)[:, 12:24], tri[:, 0:P], DL[:, 1, :], start=False).then_inc(filled(job), 1)
                for t in range(NT):
                    pe.wait_ge(FQ_ready, at(FQ_ready, l, t + 1))
                    for i in range(2):
                        transposes(("fT", t, i), [FQ[:, t, 4 * i + j, :] for j in range(4)])
                for n in IN_THEN:
                    for t in range(NT):
                        tile_job(("in", n, t), (n, 0), t, HT)
                for t in range(NT):
                    both_copied("fT", t)
                    both_copied("memT", t)

                def score(k):
                    fam, h = HEADS[k]
                    for t in range(NT):
                        job, w = ("s", HEADS[k], t), (t + 1) * P
                        pe.wait_ge(*free(job, l))
                        if fam == "fox":
                            q, kk = FQT[0:HD + 2, h, t * P:(t + 1) * P], FQT[0:HD + 2, NH + h, 0:w]
                        else:
                            r = slice(HD * (h % 2), HD * (h % 2) + HD)
                            q, kk = DQT[r, h // 2, t * P:(t + 1) * P], DQT[r, 2 + h // 2, 0:w]
                        mm(bk(job)[:, 0:w], q, kk).then_inc(filled(job), 1)

                for k in range(len(HEADS) + 1):
                    if k == NH:
                        for t in range(NT):
                            pe.wait_ge(*copied(("dT", t), l))
                    if k < len(HEADS):
                        score(k)
                    for job in BETWEEN[k]:
                        if job[0] == "kv":
                            tile_job(job, ("kv", job[1]), job[2], MT)
                        elif job[0] == "kT":
                            n, t = job[1:]
                            pe.wait_ge(k_normed, at(k_normed, l, NT * n + t + 1))
                            transposes(job, [K_tm[:, t, j * P:(j + 1) * P] for j in range(4)])
                        else:
                            t = job[1]
                            pe.wait_ge(DQ_ready, at(DQ_ready, l, t + 1))
                            transposes(job, [pt[t][:, T_DQK + j * P:T_DQK + (j + 1) * P] for j in range(4)])
                    if k == 0:
                        continue
                    b = (k - 1) % 2
                    pe.wait_ge(probs, at(probs, l, 2 * k))
                    transposes(("pT", HEADS[k - 1]), [SCO[:, b, 0, 0:P], SCO[:, b, 1, 0:P], SCO[:, b, 1, P:S]])
                    if k % 2 == 0:
                        job = ("o", HEADS[k - 1])
                        pe.wait_ge(*free(job, l))
                        for k2 in (k - 2, k - 1):
                            fam, h = HEADS[k2]
                            pe.wait_ge(*copied(("pT", HEADS[k2]), l))
                            r = slice(HD * (k2 % 2), HD * (k2 % 2) + HD)
                            v0 = (T_FV if fam == "fox" else T_DV) + HD * h
                            mm(bk(job)[r, 0:S], pt[0][:, v0:v0 + HD], PT[:, k2 % 2, 0:S], stop=False)
                            last = mm(bk(job)[r, P:S], pt[1][:, v0:v0 + HD], PT[:, k2 % 2, S:3 * P], start=False)
                        last.then_inc(filled(job), 1)

                pe.wait_ge(conv_gated, at(conv_gated, l, KC))
                for t in range(NT):
                    transposes(("xsT", t), [xc[:, c, t * P:(t + 1) * P] for c in range(4)])
                for g in range(2):
                    job, Bg, Cg = ("cb", g), xc[:, 4 + g, :], xc[:, 6 + g, :]
                    pe.wait_ge(*free(job, l))
                    mm(bk(job)[:, 0:S], Bg[:, 0:P], Cg)
                    mm(bk(job)[:, S:3 * P], Bg[:, P:S], Cg[:, P:S]).then_inc(filled(job), 1)

                def spread(h):
                    job = ("L", h)
                    pe.wait_ge(*free(job, l))
                    d = [DL[:, t, NH + h:NH + h + 1].to_broadcast([P, P]) for t in range(NT)]
                    mm(bk(job)[:, 0:S], d[0], tri[:, 0:S], stop=False)
                    mm(bk(job)[:, P:S], d[1], tri[:, 0:P], start=False).then_inc(filled(job), 1)

                for h in range(L_AHEAD):
                    spread(h)
                for t in range(NT):
                    pe.wait_ge(*copied(("xsT", t), l))
                    pe.wait_ge(*free(("y", t), l))
                for h in range(SH):
                    if h + L_AHEAD < SH:
                        spread(h + L_AHEAD)
                    pe.wait_ge(M_ready, at(M_ready, l, h + 1))
                    c = slice(SP_ * h, SP_ * (h + 1))
                    M = Ms[:, h % 2, :]
                    y0 = mm(bk(("y", 0))[:, c], M[:, 0:P], XS[:, 0, c])
                    if h == SH - 1:
                        y0.then_inc(filled(("y", 0)), 1)
                    mm(bk(("y", 1))[:, c], M[:, P:S], XS[:, 0, c], stop=False)
                    y1 = mm(bk(("y", 1))[:, c], M[:, S:], XS[:, 1, c], start=False)
                    y1.then_inc(filled(("y", 1)) if h == SH - 1 else y_head, 1)
                tile_job(("kv", 3, 1), ("kv", 3), 1, MT)
                for t in range(NT):
                    pe.wait_ge(Y_ready, at(Y_ready, l, t + 1))
                    transposes(("ysT", t), [Y[:, t, j * P:(j + 1) * P] for j in range(4)])
                for t in range(NT):
                    pe.wait_ge(*copied(("ysT", t), l))
                for k in (1, 3, 5, 7):
                    pe.wait_ge(*copied(("o", HEADS[k]), l))
                for t in range(NT):
                    for n in range(2):
                        tile_job(("out1", n, t), ("w_out", n), t, mixT)

                for t in range(NT):
                    transpose_h(1, "hT2", t)
                    both_copied("hT2", t)
                    for n in range(2):
                        tile_job(("q", n, t), ("wq", n), t, HT)

                def transpose_q(t):
                    pe.wait_ge(q_normed, at(q_normed, l, t + 1))
                    for i in range(2):
                        transposes(("qT", t, i), [Q_tm[:, t, (4 * i + j) * P:(4 * i + j + 1) * P] for j in range(4)])

                transpose_q(0)
                for n in range(2):
                    both_copied("kT", n)
                for j in range(len(CROSS) + 1):
                    if j < len(CROSS):
                        t, h = CROSS[j]
                        job = ("xs", t, h)
                        if h == 0:
                            both_copied("qT", t)
                        pe.wait_ge(*free(job, l))
                        for c in (2 * h, 2 * h + 1):
                            last = mm(bk(job)[:, 0:S], QT[:, t, c, :], KT[:, c, :], start=c == 2 * h,
                                      stop=c == 2 * h + 1)
                        last.then_inc(filled(job), 1)
                    if j == 2:
                        transpose_q(1)
                    if j == 5:
                        for h in range(XH):
                            pe.wait_ge(*copied(("xo", 0, h), l))
                    if j in (5, 6):
                        tile_job(("out2", j - 5, 0), ("wo", j - 5), 0, mixT)
                    if j == 0:
                        continue
                    t, h = CROSS[j - 1]
                    b = (j - 1) % 2
                    pe.wait_ge(xprobs, at(xprobs, l, j))
                    transposes(("xpT", t, h), [SCO[:, b, 0, m * P:(m + 1) * P] for m in range(2)])
                    job = ("xo", t, h)
                    pe.wait_ge(*copied(("xpT", t, h), l))
                    pe.wait_ge(*free(job, l))
                    for i in range(2):
                        d0 = h * XD + i * P
                        for m in range(2):
                            last = mm(bk(job)[:, i * P:(i + 1) * P], VM[:, m, d0:d0 + P],
                                      PT[:, b, m * P:(m + 1) * P], start=m == 0, stop=m == 1)
                    last.then_inc(filled(job), 1)
                for h in range(XH):
                    pe.wait_ge(*copied(("xo", 1, h), l))
                tile_job(("out2", 0, 1), ("wo", 0), 1, mixT)
                transpose_h(2, "hT3", 0)
                tile_job(("out2", 1, 1), ("wo", 1), 1, mixT)
                transpose_h(2, "hT3", 1)

                job, w = ("router",), NG + NE
                pe.wait_ge(*free(job, l))
                for t in range(NT):
                    both_copied("hT3", t)
                    for c in range(KC):
                        last = mm(bk(job)[:, t * w:(t + 1) * w], HT[:, t, c, :], wr[:, c, :],
                                  start=c == 0, stop=c == KC - 1)
                last.then_inc(filled(job), 1)
                job = ("rank",)
                pe.wait_ge(chosen_ready, at(chosen_ready, l, 1))
                pe.wait_ge(*free(job, l))
                mm(bk(job)[:, 0:NE], tri[:, 0:P], chosen[:, 0, :])
                mm(bk(job)[:, NE:2 * NE], ones, chosen[:, 0, :], stop=False)
                mm(bk(job)[:, NE:2 * NE], tri[:, 0:P], chosen[:, 1, :], start=False)
                mm(bk(job)[:, 2 * NE:3 * NE], ones, chosen[:, 0, :], stop=False)
                mm(bk(job)[:, 2 * NE:3 * NE], ones, chosen[:, 1, :], start=False).then_inc(filled(job), 1)

                def quad(q, quads):
                    turns = (l + 1) * DENSE_TURNS + quads * MOE_TURNS

                    def landed_unit(n):
                        pe.wait_ge(landed[n % SLOTS], (turns + n // SLOTS + 1) * 16)
                        return ring[:, n % SLOTS, :].rearrange("p (e c n) -> p e c n", e=QUAD, n=512)

                    pe.wait_ge(sel_ready, quads + 1)
                    sel = SEL.rearrange("p t e s -> p t (e s)")
                    selg = SELG.rearrange("p t e s -> p t (e s)")
                    for i in range(2):
                        for j in range(4):
                            for t in range(NT):
                                last = mm(bank[B_GATH[i]][:, j * P:(j + 1) * P], H[:, t, 4 * i + j, :], sel[:, t, :],
                                          start=t == 0, stop=t == NT - 1)
                        last.then_inc(gath_full, 1)
                    pe.wait_ge(selg_ready, quads + 1)
                    for t in range(NT):
                        last = nc.tensor.transpose(bank[B_SELT][:, t * P:(t + 1) * P], selg[:, t, :], ident)
                    last.then_inc(selt_full, 1)
                    pe.wait_ge(XG_ready, quads * 2 + 2)
                    for n in range(8):
                        u = landed_unit(n)
                        for c in range(2):
                            k = n % 4 * 2 + c
                            for e in range(QUAD):
                                r = slice(CAP * e, CAP * (e + 1))
                                last = mm(bank[B_UP[n // 4]][r, :], XG[:, k, r], u[:, e, c, :],
                                          start=k == 0, stop=k == KC - 1)
                        last.then_inc(units_used, 1)
                    pe.wait_ge(hid_ready, quads + 1)
                    for j in range(4):
                        last = nc.tensor.transpose(bank[B_HIDT][:, j * P:(j + 1) * P], HID[:, j, :], ident)
                    last.then_inc(hidt_full, 1)
                    pe.wait_ge(HIDT_ready, quads + 1)
                    for n in range(4):
                        u = landed_unit(8 + n)
                        for c in range(2):
                            for e in range(QUAD):
                                r = slice(CAP * e, CAP * (e + 1))
                                last = mm(bank[B_DOWN[c]][r, :], HIDT[:, n, r], u[:, e, c, :],
                                          start=n == 0, stop=n == 3)
                        last.then_inc(units_used, 1)
                    pe.wait_ge(SELT_ready, quads + 1)
                    pe.wait_ge(YS_ready, quads + 1)
                    for i in range(4):
                        t, n = i // 2, i % 2
                        mm(bank[B_SCAT[i]][:, :], SELT[:, t * P:(t + 1) * P], YS[:, n * 512:(n + 1) * 512]
                           ).then_inc(scat_full, 1)
                moe_quads(pe, l, quad)


def constants():
    import numpy as np
    p = np.arange(P)[:, None]
    j = np.arange(P)[None, :]
    con = np.zeros((P, CONST_W), np.float32)

    def put(name, v):
        o, w = CONST[name]
        con[:, o:o + w] = v
    put("ident", p == j)
    tri = (p <= j).astype(np.float32)
    put("tri", np.concatenate([tri, np.ones((P, P)), tri], 1))
    put("causal", np.concatenate([np.zeros((P, P)), np.where(j <= p, 0.0, -BIG)], 1))
    dil = []
    for t in range(NT):
        d = (t * P + p) - np.arange((t + 1) * P)[None, :]
        m = sum(((d >= 0) & (d <= w) & (d % r == 0)).astype(np.float64) for w, r in ((128, 1), (512, 4), (2048, 16)))
        dil.append(np.where(m > 0, HD ** 0.5 * np.log(np.maximum(m, 1)), -BIG))
    put("dilated", np.concatenate(dil, 1))
    inv = np.power(np.float32(500000.0), -2.0 * np.arange(8, dtype=np.float32) / np.float32(16)).astype(np.float32)
    ang = np.arange(S, dtype=np.float32)[:, None] * inv[None, :]
    for name, f in (("cos", np.cos), ("sin", np.sin)):
        put(name, f(ang).astype(np.float32).reshape(NT, P, 8).transpose(1, 0, 2).reshape(P, NT * 8))
    put("slots", np.arange(CAP)[None, :])
    put("caps", (np.arange(8) * CAP)[None, :])
    put("down", (NE - np.arange(NE))[None, :])
    put("half", -0.5)
    return con


WEIGHTS = ["x", "mem", "w_in", "w_out", "xa_wq", "xa_wkv", "xa_wo", "exp_w1", "exp_w3", "exp_w2"]


def lay_out(inputs):
    import numpy as np
    g = {n: np.asarray(v) for n, v in inputs.items()}
    arrays = {n: np.ascontiguousarray(g[n]) for n in WEIGHTS}
    arrays["rows"] = np.concatenate([g[n] for n in ROWS], axis=1)
    arrays["chan"] = np.concatenate([g["ssd_conv_w"].reshape(DEPTH, -1, P), g["ssd_conv_b"].reshape(DEPTH, -1, P),
                                     g["ssd_norm_g"].reshape(DEPTH, -1, P)], axis=1)
    gains = np.stack([g["norm1_g"], g["mem_norm_g"], g["norm2_g"]], axis=1).reshape(DEPTH, 3, P, KC)
    arrays["gains"] = np.ascontiguousarray(gains.transpose(0, 2, 1, 3)).reshape(DEPTH, P, 3 * KC)
    arrays["gain3"] = np.ascontiguousarray(g["norm3_g"].reshape(DEPTH, P, KC).transpose(1, 0, 2)).reshape(P, -1)
    arrays["router"] = np.concatenate([g["router_wg"], g["router_we"]], axis=2).reshape(DEPTH, P, -1)
    arrays["const"] = constants()
    return arrays


def kernel(**inputs):
    import concourse.bacc as bacc
    from concourse.bass_utils import run_bass_kernel_spmd

    nc = bacc.Bacc("TRN2", target_bir_lowering=False, num_devices=1)
    arrays = lay_out(inputs)
    aps = {n: nc.dram_tensor(n, v.shape, mybir.dt.from_np(v.dtype), kind="ExternalInput").ap()
           for n, v in arrays.items()}
    out = nc.dram_tensor("out", (1, S, D), F32, kind="ExternalOutput").ap()
    trunk(nc, aps, out)
    r = run_bass_kernel_spmd(nc, [arrays], core_ids=[0])
    return r.results[0]["out"]
```

```python
from contextlib import ExitStack

import concourse.bass as bass
from concourse import mybir

F32 = mybir.dt.float32
I32 = mybir.dt.int32
ALU = mybir.AluOpType
ACT = mybir.ActivationFunctionType
AX = mybir.AxisListType

P = 128
DEPTH, S, D = 2, 256, 1024
NT = S // P
KC = D // P
HD, NH = 64, 4
SH, SP_, SI = 8, 64, 512
XH, XD = 4, 256
NE, FF = 32, 512
QUAD = 4
CAP = P // QUAD
NQ = NE // QUAD
NG, EPG = 4, 8
EPS = 1e-6
BIG = 1e30
C_FQK, C_FV, C_DQK, C_DV, C_Z, C_XBC, C_DT = 0, 512, 772, 1284, 1540, 2052, 3076
T_FV, T_FF, T_DQK, T_DV, T_Z, T_W = 512, 768, 780, 1292, 1548, 2060
ROWS = {}
_o = 0
for _n, _w in (("fox_qn_g", HD), ("fox_kn_g", HD), ("dil_qn_g", HD), ("dil_kn_g", HD), ("xa_qn_g", XD),
               ("xa_kn_g", XD), ("fox_fgate_b", NH), ("ssd_dt_bias", SH), ("ssd_A_log", SH), ("ssd_D", SH),
               ("router_bg", NG), ("router_be", NE)):
    ROWS[_n] = (_o, _w)
    _o += _w
ROWS_W = _o
CONST = {}
_o = 0
for _n, _w in (("ident", P), ("tri", 3 * P), ("causal", 2 * P), ("dilated", 3 * P), ("cos", NT * 8),
               ("sin", NT * 8), ("slots", CAP), ("caps", 8), ("down", NE)):
    CONST[_n] = (_o, _w)
    _o += _w
CONST_W = _o

SLOTS = 6
UNIT = 4096
DENSE = [("fv", 0), ("fqk", 0), ("xbc", 0), ("xbc", 1), ("dqk", 0), ("z0", 0), ("z1", 0), ("dv", 0),
         ("kv", 0), ("kv", 1), ("kv", 2), ("kv", 3), ("w_out", 0), ("w_out", 1), ("wq", 0), ("wq", 1),
         ("wo", 0), ("wo", 1)]
DENSE_TURNS = len(DENSE) // SLOTS
assert DENSE_TURNS * SLOTS == len(DENSE)
MOE_UNITS = 12
MOE_TURNS = MOE_UNITS // SLOTS
SPARE_UNITS = (2, 3, 4, 5)
SHIFT = len(SPARE_UNITS)
HEAD_ORDER = (0, 1, 6, 7, 2, 3, 4, 8, 9, 5, 10, 11)


def moe_slot(n, head):
    if head and n < SLOTS:
        return None if n in SPARE_UNITS else n
    return (n - SHIFT) % SLOTS


LAST_IN_SLOT = [max(n for n in range(MOE_UNITS) if moe_slot(n, False) == s) for s in range(SLOTS)]
SHORT = [MOE_TURNS - sum(moe_slot(n, True) == s for n in range(MOE_UNITS)) for s in range(SLOTS)]


IN_COLS = {"fqk": (C_FQK, 512, 0), "fv": (C_FV, 268, T_FV), "dqk": (C_DQK, 512, T_DQK), "dv": (C_DV, 256, T_DV),
           "z0": (C_Z, 256, T_Z), "z1": (C_Z + 256, 256, T_Z + 256)}
W_FV = C_DQK - C_FV
PROJ_HT = NT * T_W + NT * KC * P
IN_FIRST, IN_THEN = ("fv", "fqk"), ("dqk", "z0", "z1", "dv")

HEADS = [(fam, h) for fam in ("fox", "dil") for h in range(NH)]
BETWEEN = [[("kv", 0, 0)], [("kv", 0, 1)], [("dT", 0), ("dT", 1), ("kT", 0, 0), ("kv", 1, 0)],
           [("kT", 0, 1), ("kv", 1, 1)], [("kT", 1, 0), ("kv", 2, 0)], [("kT", 1, 1), ("kv", 2, 1)],
           [("kv", 3, 0)], [], []]
CROSS = [(t, h) for t in range(NT) for h in range(XH)]
CROSS_BETWEEN = [[("q", 1, 1)], [], [], [("qT", 1, 0), ("qT", 1, 1)], [], [("out2", 0, 0)], [("out2", 1, 0)], [], []]
L_AHEAD = 2


def list_jobs():
    def two(name, t):
        return [(name, t, 0), (name, t, 1)]

    jobs = two("hT1", 0) + two("hT1", 1)
    jobs += [("in", n, t) for n in IN_FIRST for t in range(NT)]
    jobs += [("params",)] + two("memT", 0) + two("memT", 1)
    jobs += [("cum",)] + [("xbc", i) for i in range(4)]
    jobs += two("fT", 0) + two("fT", 1)
    jobs += [("in", n, t) for n in IN_THEN for t in range(NT)]
    for k in range(len(HEADS) + 1):
        if k < len(HEADS):
            jobs += [("s", HEADS[k], t) for t in range(NT)]
        jobs += BETWEEN[k]
        if k == len(HEADS):
            jobs += [("L", h) for h in range(L_AHEAD)]
        if k:
            jobs += [("pT", HEADS[k - 1])]
            if k % 2 == 0:
                jobs += [("o", HEADS[k - 1])]
    jobs += [("xsT", t) for t in range(NT)] + [("cb", g) for g in range(2)]
    jobs += [("y", t) for t in range(NT)] + [("L", h) for h in range(L_AHEAD, SH)]
    jobs += [("kv", 3, 1)] + [("ysT", t) for t in range(NT)]
    jobs += [("out1", 0, 0), ("out1", 1, 0), ("out1", 0, 1)] + two("hT2", 0) + [("out1", 1, 1)]
    jobs += [("q", 0, 0)] + two("hT2", 1) + [("q", 1, 0), ("q", 0, 1)] + two("qT", 0)
    for j in range(len(CROSS) + 1):
        if j < len(CROSS):
            jobs += [("xs", *CROSS[j])]
        jobs += CROSS_BETWEEN[j]
        if j:
            jobs += [("xpT", *CROSS[j - 1]), ("xo", *CROSS[j - 1])]
    jobs += [("out2", 0, 1)] + two("xT", 0) + [("out2", 1, 1), ("router",)] + two("xT", 1)
    return jobs + [("rank",), ("total",)]


NB = 8


def plan_banks():
    place, uses, n, held = {}, [0] * NB, 0, set()
    for job in list_jobs():
        while n % NB in held:
            n += 1
        b = n % NB
        place[job] = (b, uses[b])
        uses[b] += 1
        if job[0] == "y":
            held.add(b)
        if job == ("L", SH - 1):
            held.clear()
        n += 1
    return place, uses


PLACE, USES = plan_banks()
LAST_USE = {"kv": lambda i: ("kv", i, 1), "xbc": lambda i: ("xbc", 2 * i + 1), "w_out": lambda i: ("out1", i, 1),
            "wq": lambda i: ("q", i, 1), "wo": lambda i: ("out2", i, 1)}
N_PARAMS = 4
V_STEPS, A_STEPS, G_STEPS = 97, 2, 19
V_MOE = 1
G_X, G_MEM, G_2 = 0, 1, 2


def last_use(unit):
    kind, i = unit
    return LAST_USE[kind](i) if kind in LAST_USE else ("in", kind, 1)


def trunk(nc, a, out):
    with ExitStack() as ctx:
        def sb(name, shape, dt=F32):
            return ctx.enter_context(nc.sbuf_tensor(name, shape, dt))

        per_layer = {}

        def sem(name, n=0):
            s = ctx.enter_context(nc.semaphore(name))
            per_layer[s] = n
            return s

        def at(s, l, n):
            return l * per_layer[s] + n

        ring = sb("ring", [P, SLOTS, UNIT])
        X = sb("X", [P, NT, D])
        H = sb("H", [P, NT, KC, P])
        proj_ht = sb("proj_ht", [P, PROJ_HT])
        conv_mem = sb("conv_mem", [P, KC * (S + 3) + NT * KC * P])
        keys_values = sb("keys_values", [P, KC * S + NT * D])
        Y = sb("Y", [P, NT, SI])
        fox_ssd = sb("fox_ssd", [P, 2 * NH * S + NT * 2 * NH * (HD + 2) + NT * SI])
        DQT = sb("DQT", [P, 4, S])
        SCO = sb("SCO", [P, 2, NT, S])
        row = sb("row", [P, ROWS_W])
        con = sb("con", [P, CONST_W])
        g_ch = sb("g_ch", [P, 3, KC])
        g3 = sb("g3", [P, DEPTH, KC])
        p_rows = sb("p_rows", [44, P])
        p_ch = sb("p_ch", [P, 44])
        wr = sb("wr", [P, KC, NG + NE])
        ss = sb("ss", [P, 6])
        ssk = sb("ssk", [P, NT, XH])
        ssf = sb("ssf", [P, NT, 16])
        smax = sb("smax", [P, 2, NT])
        ssum = sb("ssum", [P, 2, NT])
        gate_in = sb("gate_in", [P, NT, 12])
        gate_e = sb("gate_e", [P, NT, 12])
        DL = sb("DL", [P, NT, 12])
        DTs = sb("DTs", [P, NT, SH])
        CUM = sb("CUM", [P, NT, 12])
        negA = sb("negA", [P, SH])
        rt = sb("rt", [P, NT, 8])
        rg = sb("rg", [P, NT, 4, NG])
        passes = sb("passes", [P, 2])
        half = sb("half", [P, 16])
        passes_i = sb("passes_i", [P, DEPTH + 1], I32)
        over = sb("over", [P, 8])
        slot_no = sb("slot_no", [P, CAP])

        def view(buf, off, *shape):
            n = 1
            for x in shape:
                n *= x
            v = buf[:, off:off + n]
            if len(shape) == 1:
                return v
            names = "abcd"[:len(shape)]
            return v.rearrange(f"p ({' '.join(names)}) -> p {' '.join(names)}", **dict(zip(names, shape)))

        proj, HT = view(proj_ht, 0, NT * T_W), view(proj_ht, NT * T_W, NT, KC, P)
        XBCp, MT = view(conv_mem, 0, KC * (S + 3)), view(conv_mem, KC * (S + 3), NT, KC, P)
        KT = view(keys_values, 0, KC, S)
        VM = view(keys_values, KC * S, NT, D)
        FQT = view(fox_ssd, 0, 2 * NH, S)
        FQ = view(fox_ssd, 2 * NH * S, NT, 2 * NH, HD + 2)
        XS = view(fox_ssd, 2 * NH * S + NT * 2 * NH * (HD + 2), NT, SI)
        spare = (conv_mem[:, 0:UNIT], fox_ssd[:, 0:UNIT], keys_values[:, :], proj_ht[:, PROJ_HT - UNIT:])

        def ring_view(s, w):
            return view(ring[:, s, :], 0, KC, w)

        fqt_flat = FQT[:, :, :].rearrange("p a b -> p (a b)")
        pt = [proj[:, t * T_W:(t + 1) * T_W] for t in range(NT)]
        mem_raw = view(fqt_flat, 0, NT, D)
        MN = view(XBCp, 0, NT, KC, P)
        xin = view(XBCp, 0, KC, S + 3)
        xc = xin[:, :, 3:]
        mixT = H
        Q_tm = view(proj, 0, NT, D)
        QT = HT
        sq = view(SCO[:, :, :, :].rearrange("p a b c -> p (a b c)"), 0, 1024)
        fq_flat = FQ[:, :, :, :].rearrange("p a b c -> p (a b c)")
        cv = view(fq_flat, 0, 2, S)
        rope = view(fq_flat, 2 * S, 4, 2 * NH, 8)
        K_tm = XS
        dqt_flat = DQT[:, :, :].rearrange("p a b -> p (a b)")
        lg = view(dqt_flat, 0, NT, NG + NE)
        ties = view(dqt_flat, 128, NT, NE)
        em = view(dqt_flat, 192, NT, NE)
        oh = view(dqt_flat, 256, 2, NT, NE)
        gates = view(dqt_flat, 384, NT, NE)
        chosen = view(dqt_flat, 448, NT, NE)
        chosen_flat = view(dqt_flat, 448, NT * NE)
        rank = view(dqt_flat, 512, NT, NE)
        ht_flat = view(proj_ht, NT * T_W, NT * KC * P)
        sig = view(ht_flat, 0, 2, S)
        ve = view(ht_flat, 512, 512)
        Ls = view(ht_flat, 1024, 2, 3 * P)
        Ms = view(fqt_flat, 0, 2, 3 * P)
        CB = view(fqt_flat, 1024, 2, 3 * P)
        Yf = Y[:, :, :].rearrange("p t n -> p (t n)")
        PT = view(Yf, 0, 2, 2 * S)
        XG = view(proj, 0, KC, P)
        SEL = view(proj, 1024, NT, QUAD, CAP)
        SELG = view(proj, 1280, NT, QUAD, CAP)
        SELT = view(proj, 1536, S)
        assert 1792 <= PROJ_HT - UNIT
        HID = view(sq, 0, 4, P)
        HIDT = view(sq, 512, 4, P)
        SIGM = view(Yf, 0, FF)
        YS = XS[:, :, :].rearrange("p t n -> p (t n)")

        def junk(k, t):
            if k == 0:
                return (Yf, sq)[t]
            return H[:, t, :, :].rearrange("p a b -> p (a b)")

        def c_(name, *shape):
            o, w = CONST[name]
            return view(con, o, *(shape or (w,)))

        def r_(name, *shape):
            o, w = ROWS[name]
            return view(row, o, *(shape or (w,)))

        def bc(ap, *shape):
            return ap.unsqueeze(len(ap.shape)).to_broadcast([P, *shape])

        ident, tri = c_("ident"), c_("tri")
        ones = tri[:, P:2 * P]

        bank = [ctx.enter_context(nc.psum_tensor(f"bank{b}", [P, 512], F32)) for b in range(NB)]
        B_GATH, B_SELT, B_UP, B_HIDT, B_DOWN, B_SCAT = (0, 1), 2, (3, 4), 5, (6, 7), (0, 1, 3, 4)

        bank_full = [sem(f"bank_full{b}", USES[b]) for b in range(NB)]
        bank_read = [sem(f"bank_read{b}", USES[b]) for b in range(NB)]
        landed = [sem(f"landed{s}") for s in range(SLOTS)]
        spare_in = [sem(f"spare_in{i}", 16) for i in range(SHIFT)]
        x_in = [sem(f"x_in{t}") for t in range(NT)]
        const_in, g3_in = sem("const_in"), sem("g3_in")
        dt_in = sem("dt_in", 16)
        params_in = sem("params_in", 16 * N_PARAMS)
        mem_in = sem("mem_in", 16)
        vector_layer = sem("vector_layer", 1)
        passes_known = sem("passes_known", 1)
        v_step = sem("v_step", V_STEPS)
        a_step = sem("a_step", A_STEPS)
        g_step = sem("g_step", G_STEPS)
        mem_ss, mem_rs = sem("mem_ss", 1), sem("mem_rs", 1)
        k_ss, k_rs = sem("k_ss", 2 * NT), sem("k_rs", 2 * NT)
        q_ss, q_rs = sem("q_ss", NT), sem("q_rs", NT)
        x_ss, x_rs = sem("x_ss", 3 * NT), sem("x_rs", 3 * NT)
        fd_sq = sem("fd_sq", 2 * NT)
        fd_ss, fd_rs = sem("fd_ss", 2 * NT), sem("fd_rs", 2 * NT)
        y_ss, y_rs = sem("y_ss", NT), sem("y_rs", NT)
        MN_ready = sem("MN_ready", 1)
        k_normed, q_normed = sem("k_normed", 2 * NT), sem("q_normed", NT)
        X_ready = sem("X_ready", 2 * NT)
        H_ready = sem("H_ready", 3 * NT)
        pads = sem("pads", 1)
        conv_tap = sem("conv_tap", KC)
        conv_done = sem("conv_done", KC)
        conv_tanh = sem("conv_tanh", KC)
        conv_gated = sem("conv_gated", KC)
        gate_abs, gate_ln = sem("gate_abs", 1), sem("gate_ln", 1)
        DL_ready = sem("DL_ready", 1)
        FQ_ready, DQ_ready = sem("FQ_ready", NT), sem("DQ_ready", NT)
        scores = sem("scores", 4 * NH)
        exps = sem("exps", 4 * NH)
        probs = sem("probs", 4 * NH)
        decays = sem("decays", SH)
        M_ready = sem("M_ready", SH)
        y_head = sem("y_head", SH - 1)
        z_tanh = sem("z_tanh", NT)
        Y_ready = sem("Y_ready", NT)
        xmax = sem("xmax", 2 * XH)
        xprobs = sem("xprobs", 2 * XH)
        g_shift, g_exp = sem("g_shift", 1), sem("g_exp", 1)
        e_shift, e_exp = sem("e_shift", 1), sem("e_exp", 1)
        chosen_ready = sem("chosen_ready", 1)
        units_used = sem("units_used")
        sel_ready, selg_ready = sem("sel_ready"), sem("selg_ready")
        gath_full, XG_ready = sem("gath_full"), sem("XG_ready")
        selt_full, SELT_ready = sem("selt_full"), sem("SELT_ready")
        up_tanh, hid_ready = sem("up_tanh"), sem("hid_ready")
        hidt_full, HIDT_ready = sem("hidt_full"), sem("HIDT_ready")
        YS_ready = sem("YS_ready")
        scat_full = sem("scat_full")
        places_set = sem("places_set")
        v_moe = sem("v_moe")
        x_added = sem("x_added")
        x_out = sem("x_out")
        half_set = sem("half_set")
        waits_passed = sem("waits_passed")

        def bk(job):
            return bank[PLACE[job][0]]

        def full(job, l):
            b, k = PLACE[job]
            return bank_full[b], at(bank_full[b], l, k + 1)

        def free(job, l):
            b, k = PLACE[job]
            return bank_read[b], at(bank_read[b], l, k + 1)

        def copied(job, l):
            b, k = PLACE[job]
            return bank_read[b], at(bank_read[b], l, k + 2)

        def filled(job):
            return bank_full[PLACE[job][0]]

        def read(job):
            return bank_read[PLACE[job][0]]

        def alone(eng):
            eng.sem_inc(waits_passed, 1)

        def load_passes(eng, l):
            return eng.value_load(passes_i[0:1, bass.ds(l, 1)], min_val=0, max_val=8 * DEPTH)

        def moe_quads(eng, l, quad, head=None, new_pass=None):
            before = load_passes(eng, l)
            if head:
                head(0, before * NQ)
                alone(eng)
            with eng.Fori(1 if head else 0, NQ) as q:
                quad(q, before * NQ + q)
            eng.wait_ge(passes_known, at(passes_known, l, 2))
            alone(eng)
            more = eng.snap(load_passes(eng, l + 1) - before)
            with eng.If(more > 1):
                with eng.Fori(1, more) as ps:
                    if new_pass:
                        new_pass(before + ps)
                    with eng.Fori(0, NQ) as q:
                        quad(q, (before + ps) * NQ + q)

        def landed_by(n, slot, head, l, quads):
            a_layer = DENSE_TURNS - SHORT[slot]
            layers = l * a_layer + DENSE_TURNS if head else (l + 1) * a_layer
            return layers + quads * MOE_TURNS + sum(moe_slot(m, head) == slot for m in range(n + 1))

        block = ctx.enter_context(nc.Block())

        @block.sync
        def _(sp):
            for t in range(NT):
                sp.dma_start(X[:, t, :], a["x"][0, t * P:(t + 1) * P, :]).then_inc(x_in[t], 16)
            sp.dma_start(con[:, :], a["const"]).then_inc(const_in, 16)

            def dense(kind, i, l):
                name = {"kv": "xa_wkv", "wq": "xa_wq", "w_out": "w_out", "wo": "xa_wo"}.get(kind, "w_in")
                c0, w, _ = IN_COLS.get(kind, (C_XBC if kind == "xbc" else 0, 512, 0))
                w = W_FV if kind == "fv" else w
                rows = "a (c p) n -> p (a c) n" if kind in ("w_out", "wo") else "a (p c) n -> p (a c) n"
                v = a[name][bass.ds(l, 1)].rearrange(rows, c=KC)
                return w, v[:, :, c0 + i * 512:c0 + i * 512 + w]

            with sp.Fori(0, DEPTH) as l:
                sp.wait_ge(passes_known, at(passes_known, l, 1))
                quads_before = sp.snap(load_passes(sp, l) * NQ)
                for n, (kind, i) in enumerate(DENSE):
                    if n < SLOTS:
                        sp.wait_ge(units_used, quads_before * MOE_UNITS + LAST_IN_SLOT[n] + 1)
                        alone(sp)
                    else:
                        sp.wait_ge(*full(last_use(DENSE[n - SLOTS]), l))
                        alone(sp)
                    w, src = dense(kind, i, l)
                    if kind == "fv":
                        place = ring_view(n % SLOTS, IN_COLS["fv"][1])
                        dt = a["w_in"][bass.ds(l, 1)].rearrange("a (p c) n -> p (a c) n", c=KC)[:, :, C_DT:C_DT + SH]
                        sp.dma_start(place[:, :, w:], dt).then_inc(dt_in, 16)
                    else:
                        place = ring_view(n % SLOTS, w)
                    sp.dma_start(place[:, :, 0:w], src).then_inc(landed[n % SLOTS], 16)

                def quad(q, quads, head=False):
                    for n in HEAD_ORDER if head else range(MOE_UNITS):
                        name, i = ("exp_w1", "exp_w3", "exp_w2")[n // 4], n % 4
                        w = a[name][bass.ds(l, 1)].rearrange("a e k n -> (a e) k n")[bass.ds(q * QUAD, QUAD)]
                        if name == "exp_w2":
                            src = w.rearrange("e (p c) n -> p e c n", c=4)[:, :, i, :]
                        else:
                            src = w.rearrange("e (p c) n -> p e (c n)", c=KC)[:, :, i * 1024:(i + 1) * 1024]
                        slot = moe_slot(n, head)
                        if slot is None:
                            i = SPARE_UNITS.index(n)
                            sp.wait_ge(*full((("kv", 3, 1), ("ysT", NT - 1), ("xo", 1, XH - 1), ("router",))[i], l))
                            alone(sp)
                            sp.dma_start(spare[i].rearrange("p (e n) -> p e n", e=QUAD), src).then_inc(spare_in[i], 16)
                            continue
                        if head and n < SLOTS + SHIFT:
                            sp.wait_ge(*full(last_use(DENSE[len(DENSE) - SLOTS + slot]), l))
                            alone(sp)
                        elif head:
                            sp.wait_ge(units_used, quads * MOE_UNITS + MOE_UNITS + slot + 1)
                        else:
                            sp.wait_ge(units_used, quads * MOE_UNITS + SLOTS + n + 1)
                        sp.dma_start(ring[:, slot, :].rearrange("p (e n) -> p e n", e=QUAD), src
                                     ).then_inc(landed[slot], 16)
                moe_quads(sp, l, quad, head=lambda q, quads: quad(q, quads, head=True))
            tiles_added = sp.snap(load_passes(sp, DEPTH) * (NQ * NT))
            for t in range(NT):
                sp.wait_ge(x_added, tiles_added + t + 3 - NT)
                alone(sp)
                sp.dma_start(out[0, t * P:(t + 1) * P, :], X[:, t, :]).then_inc(x_out, 16)
            sp.wait_ge(x_out, 16 * NT)

        def small_loads(eng, l):
            def load(dst, src, done):
                eng.dma_start(dst, src).then_inc(done, 16)

            load(g_ch[:, :, :], a["gains"][bass.ds(l, 1)].rearrange("a p (i c) -> (a p) i c", c=KC), params_in)
            load(p_rows[:, :], a["chan"][bass.ds(l, 1)].rearrange("a k p -> (a k) p"), params_in)
            load(row[:, :], a["rows"][bass.ds(l, 1)].to_broadcast([P, ROWS_W]), params_in)
            load(wr[:, :, :], a["router"][bass.ds(l, 1)].rearrange("a p (c n) -> (a p) c n", c=KC), params_in)

        def load_mem(eng):
            eng.dma_start(mem_raw, a["mem"][0].rearrange("(t p) d -> p t d", p=P)).then_inc(mem_in, 16)

        @block.gpsimd
        def _(pool):
            nc.gpsimd.memset(half[:, :], -0.5).then_inc(half_set, 1)
            pool.wait_ge(half_set, 1)
            with pool.Fori(0, DEPTH) as l:
                steps = [0]

                def rsqrt(ap, n, ready, k, done):
                    pool.wait_ge(ready, at(ready, l, k))
                    alone(pool)
                    nc.gpsimd.tensor_scalar(ap, ap, 1.0 / n, EPS, ALU.mult, ALU.add).then_inc(g_step, 1)
                    steps[0] += 1
                    pool.wait_ge(g_step, at(g_step, l, steps[0]))
                    nc.gpsimd.tensor_tensor(ap, ap, half[:, 0:ap.free_size()], ALU.pow).then_inc(done, 1)

                for t in range(NT):
                    rsqrt(ss[:, 2 + t:3 + t], D, x_ss, t + 1, x_rs)
                rsqrt(ss[:, 0:2], D, mem_ss, 1, mem_rs)
                for i in range(2):
                    for t in range(NT):
                        rsqrt(ssf[:, t, 8 * i:8 * i + 8], HD, fd_ss, NT * i + t + 1, fd_rs)
                for n in range(2):
                    for t in range(NT):
                        rsqrt(ssk[:, t, 2 * n:2 * n + 2], XD, k_ss, NT * n + t + 1, k_rs)
                for t in range(NT):
                    rsqrt(ss[:, 4 + t:5 + t], SI, y_ss, t + 1, y_rs)
                for t in range(NT):
                    rsqrt(ss[:, 2 + t:3 + t], D, x_ss, NT + t + 1, x_rs)
                for t in range(NT):
                    rsqrt(ssk[:, t, :], XD, q_ss, t + 1, q_rs)
                for t in range(NT):
                    rsqrt(ss[:, 2 + t:3 + t], D, x_ss, 2 * NT + t + 1, x_rs)
                assert steps[0] == G_STEPS, ("G", steps)

        @block.scalar
        def _(act):
            small_loads(act, 0)
            load_mem(act)
            act.dma_start(g3[:, :, :], a["gain3"].rearrange("p (l c) -> p l c", c=KC)).then_inc(g3_in, 16)
            act.wait_ge(half_set, 1)
            act.wait_ge(passes_known, 1)
            nc.scalar.activation(smax[:, 0, :], half[:, 0:NT], ACT.Square)
            with act.Fori(0, DEPTH) as l:
                steps = [0]

                def link(ins):
                    steps[0] += 1
                    ins.then_inc(a_step, 1)
                    act.wait_ge(a_step, at(a_step, l, steps[0]))

                def copy_out(job, dst, src):
                    act.wait_ge(*full(job, l))
                    nc.scalar.copy(dst, src).then_inc(read(job), 1)

                def square_x(k, t):
                    nc.scalar.activation(junk(k, t), X[:, t, :], ACT.Square,
                                         accum_out=ss[:, 2 + t:3 + t]).then_inc(x_ss, 1)

                def norm_x(k, t):
                    act.wait_ge(x_rs, at(x_rs, l, NT * k + t + 1))
                    nc.scalar.activation(H[:, t], X[:, t, :].rearrange("p (q c) -> p c q", c=KC), ACT.Copy,
                                         scale=ss[:, 2 + t:3 + t]).then_inc(H_ready, 1)

                tiles_added = act.snap(load_passes(act, l) * (NQ * NT))
                for t in range(NT):
                    act.wait_ge(x_in[t], 16)
                    act.wait_ge(x_added, tiles_added + t + 1)
                    square_x(0, t)
                norm_x(0, 0)
                act.wait_ge(mem_in, at(mem_in, l, 16))
                act.wait_ge(x_ss, at(x_ss, l, NT))
                for t in range(NT):
                    last = nc.scalar.activation(junk(0, t), mem_raw[:, t, :], ACT.Square, accum_out=ss[:, t:t + 1])
                last.then_inc(mem_ss, 1)
                act.wait_ge(mem_rs, at(mem_rs, l, 1))
                for t in range(NT):
                    last = nc.scalar.activation(MN[:, t], mem_raw[:, t, :].rearrange("p (q c) -> p c q", c=KC),
                                                ACT.Copy, scale=ss[:, t:t + 1])
                last.then_inc(MN_ready, 1)
                act.wait_ge(params_in, at(params_in, l, 16 * N_PARAMS))
                link(nc.scalar.activation(negA[:, :], r_("ssd_A_log"), ACT.Exp))

                def copy_in(n):
                    for t in range(NT):
                        _, w, dst = IN_COLS[n]
                        copy_out(("in", n, t), pt[t][:, dst:dst + w], bk(("in", n, t))[:, 0:w])

                def square_heads(n, buf):
                    for t in range(NT):
                        act.wait_ge(*copied(("in", n, t), l))
                        nc.scalar.activation(buf[:, t * 512:(t + 1) * 512], pt[t][:, IN_COLS[n][2]:IN_COLS[n][2] + 512],
                                             ACT.Square).then_inc(fd_sq, 1)

                copy_in("fv")
                act.wait_ge(gate_abs, at(gate_abs, l, 1))
                link(nc.scalar.activation(gate_e[:, :, :], gate_e[:, :, :], ACT.Exp))
                nc.scalar.activation(gate_e[:, :, :], gate_e[:, :, :], ACT.Ln, bias=1.0).then_inc(gate_ln, 1)
                copy_in("fqk")
                square_heads("fqk", Yf)
                act.wait_ge(pads, at(pads, l, 1))
                for i in range(4):
                    job = ("xbc", i)
                    copy_out(job, xin[:, 2 * i:2 * i + 2, 3:], bk(job)[:, :].rearrange("p (c s) -> p c s", c=2))
                for t in range(NT):
                    for i in range(2):
                        job = ("fT", t, i)
                        copy_out(job, FQT[0:HD + 2, 4 * i:4 * i + 4, t * P:(t + 1) * P],
                                 bk(job)[0:HD + 2, :].rearrange("p (c s) -> p c s", c=4))
                copy_in("dqk")
                square_heads("dqk", sq)
                copy_in("z0")
                copy_in("z1")
                copy_in("dv")

                def exp_scores(k):
                    for t in range(NT):
                        act.wait_ge(scores, at(scores, l, 2 * k + t + 1))
                        w = (t + 1) * P
                        nc.scalar.activation(SCO[:, k % 2, t, 0:w], SCO[:, k % 2, t, 0:w], ACT.Exp,
                                             bias=smax[:, k % 2, t:t + 1], accum_out=ssum[:, k % 2, t:t + 1]
                                             ).then_inc(exps, 1)

                def take_kv(n, t):
                    job = ("kv", n, t)
                    if n >= 2:
                        return copy_out(job, VM[:, t, (n - 2) * 512:(n - 1) * 512], bk(job)[:, :])
                    if n == 1:
                        act.wait_ge(*full(("kT", 0, t), l))
                    copy_out(job, K_tm[:, t, :], bk(job)[:, :])
                    act.wait_ge(*copied(job, l))
                    for h in range(2):
                        part = slice(h * XD, (h + 1) * XD)
                        last = nc.scalar.activation(ve[:, part], K_tm[:, t, part], ACT.Square,
                                                    accum_out=ssk[:, t, 2 * n + h:2 * n + h + 1])
                    last.then_inc(k_ss, 1)

                for k in range(len(HEADS) + 1):
                    if k < KC:
                        if k >= 2:
                            act.wait_ge(conv_gated, at(conv_gated, l, k - 1))
                        else:
                            act.wait_ge(*full(("fT", 1, 1), l))
                            act.wait_ge(*copied(("params",), l))
                        act.wait_ge(*copied(("xbc", k // 2), l))
                        nc.scalar.activation(cv[:, k % 2, :], xin[:, k, 0:S], ACT.Identity,
                                             bias=p_ch[:, 32 + k:33 + k], scale=p_ch[:, k:k + 1]).then_inc(conv_tap, 1)
                    if k < len(HEADS):
                        exp_scores(k)
                        act.wait_ge(conv_done, at(conv_done, l, k + 1))
                        nc.scalar.activation(sig[:, k % 2, :], cv[:, k % 2, :], ACT.Tanh, scale=0.5
                                             ).then_inc(conv_tanh, 1)
                    for job in BETWEEN[k]:
                        if job[0] == "dT":
                            t = job[1]
                            copy_out(job, DQT[:, :, t * P:(t + 1) * P],
                                     bk(job)[:, :].rearrange("p (c s) -> p c s", c=4))
                        elif job[0] == "kv":
                            take_kv(*job[1:])
                    if k:
                        job = ("pT", HEADS[k - 1])
                        copy_out(job, PT[:, (k - 1) % 2, 0:3 * P], bk(job)[:, 0:3 * P])
                        if k % 2 == 0:
                            job = ("o", HEADS[k - 1])
                            copy_out(job, mixT[:, :, k // 2 - 1, :], bk(job)[:, 0:S].rearrange("p (t s) -> p t s", t=NT))
                for h in range(SH):
                    if h == 1:
                        for t in range(NT):
                            job = ("xsT", t)
                            act.wait_ge(*full(job, l))
                            nc.scalar.mul(XS[:, t, :], bk(job)[:, :], 0.5).then_inc(read(job), 1)
                    if h in (2, 3):
                        t = h - 2
                        nc.scalar.activation(sq[:, t * SI:(t + 1) * SI], pt[t][:, T_Z:T_Z + SI], ACT.Tanh, scale=0.5
                                             ).then_inc(z_tanh, 1)
                    act.wait_ge(*copied(("L", h), l))
                    nc.scalar.activation(Ls[:, h % 2, :], Ls[:, h % 2, :], ACT.Exp).then_inc(decays, 1)
                take_kv(3, 1)

                for t in range(NT):
                    act.wait_ge(X_ready, at(X_ready, l, t + 1))
                    square_x(1, t)
                    norm_x(1, t)
                def copy_q(n, t):
                    copy_out(("q", n, t), Q_tm[:, t, n * 512:(n + 1) * 512], bk(("q", n, t))[:, :])

                def square_q(t):
                    act.wait_ge(*copied(("q", 0, t), l))
                    act.wait_ge(*copied(("q", 1, t), l))
                    for h in range(XH):
                        part = slice(h * XD, (h + 1) * XD)
                        last = nc.scalar.activation(junk(1, t)[:, part], Q_tm[:, t, part], ACT.Square,
                                                    accum_out=ssk[:, t, h:h + 1])
                    last.then_inc(q_ss, 1)

                copy_q(0, 0)
                copy_q(1, 0)
                square_q(0)
                copy_q(0, 1)
                for j in range(len(CROSS) + 1):
                    if j < len(CROSS):
                        job = ("xs", *CROSS[j])
                        act.wait_ge(xmax, at(xmax, l, j + 1))
                        nc.scalar.activation(SCO[:, j % 2, 0, :], bk(job)[:, 0:S], ACT.Exp,
                                             bias=smax[:, j % 2, 0:1], scale=XD ** -0.5,
                                             accum_out=ssum[:, j % 2, 0:1]).then_inc(read(job), 1)
                    if j == 0:
                        copy_q(1, 1)
                        square_q(1)
                    if j:
                        t, h = CROSS[j - 1]
                        copy_out(("xpT", t, h), PT[:, (j - 1) % 2, 0:2 * P], bk(("xpT", t, h))[:, 0:2 * P])
                        copy_out(("xo", t, h), mixT[:, t, 2 * h:2 * h + 2, :],
                                 bk(("xo", t, h))[:, 0:2 * P].rearrange("p (c s) -> p c s", c=2))
                for t in range(NT):
                    act.wait_ge(X_ready, at(X_ready, l, NT + t + 1))
                    square_x(2, t)
                    norm_x(2, t)
                act.wait_ge(g_shift, at(g_shift, l, 1))
                nc.scalar.activation(rg[:, :, 1, :], rg[:, :, 1, :], ACT.Exp).then_inc(g_exp, 1)
                act.wait_ge(e_shift, at(e_shift, l, 1))
                nc.scalar.activation(rt[:, :, 4:5], rt[:, :, 4:5], ACT.Exp).then_inc(e_exp, 1)
                assert steps[0] == A_STEPS, ("A", steps)
                act.wait_ge(passes_known, at(passes_known, l, 2))
                alone(act)
                with act.If(l < DEPTH - 1):
                    small_loads(act, (l + 1).with_bounds(min_val=1, max_val=DEPTH - 1))

                def quad(q, quads):
                    act.wait_ge(selt_full, quads + 1)
                    nc.scalar.copy(SELT, bank[B_SELT][:, 0:S]).then_inc(SELT_ready, 1)
                    act.wait_ge(units_used, quads * MOE_UNITS + MOE_UNITS + 4)
                    nc.scalar.activation(SIGM, bank[B_UP[0]][:, :], ACT.Tanh, scale=0.5).then_inc(up_tanh, 1)
                    act.wait_ge(hidt_full, quads + 1)
                    nc.scalar.copy(HIDT, bank[B_HIDT][:, :].rearrange("p (c s) -> p c s", c=4)).then_inc(HIDT_ready, 1)
                    act.wait_ge(units_used, quads * MOE_UNITS + MOE_UNITS + 12)
                    for n in range(2):
                        last = nc.scalar.copy(YS[:, n * 512:(n + 1) * 512], bank[B_DOWN[n]][:, :])
                    last.then_inc(YS_ready, 1)

                def first_quad(q, quads):
                    quad(q, quads)
                    with act.If(l < DEPTH - 1):
                        load_mem(act)
                moe_quads(act, l, quad, head=first_quad)

        @block.vector
        def _(dve):
            v = nc.vector
            v.memset(passes[:, :], 0.0)
            v.memset(passes_i[:, :], 0).then_inc(passes_known, 1)
            for b in range(NB):
                dve.sem_inc(bank_read[b], 1)
            dve.sem_inc(vector_layer, 1)
            dve.sem_inc(x_added, NT)
            dve.sem_inc(units_used, MOE_UNITS)
            dve.wait_ge(const_in, 16)
            with dve.Fori(0, DEPTH) as l:
                steps = [0]

                def link(ins):
                    steps[0] += 1
                    ins.then_inc(v_step, 1)
                    dve.wait_ge(v_step, at(v_step, l, steps[0]))

                def gained(job, gain, dst):
                    dve.wait_ge(*full(job, l))
                    v.tensor_tensor(dst, bk(job)[:, :].rearrange("p (c s) -> p c s", c=4), bc(gain, 4, P), ALU.mult
                                    ).then_inc(read(job), 1)

                def copy4(job, dst):
                    dve.wait_ge(*full(job, l))
                    v.tensor_copy(dst, bk(job)[:, :].rearrange("p (c s) -> p c s", c=4)).then_inc(read(job), 1)

                def transposed_x(name, gain, t):
                    for i in range(2):
                        gained((name, t, i), gain[:, 4 * i:4 * i + 4], HT[:, t, 4 * i:4 * i + 4, :])

                def times_gain(parts, rs, gain):
                    for h, part in enumerate(parts):
                        last = v.scalar_tensor_tensor(part, part, rs[:, h:h + 1], r_(gain), ALU.mult, ALU.mult)
                    return last

                dve.wait_ge(x_rs, at(x_rs, l, 2))
                v.tensor_scalar(H[:, 1], X[:, 1, :].rearrange("p (q c) -> p c q", c=KC), ss[:, 3:4], None, ALU.mult
                                ).then_inc(H_ready, 1)
                dve.wait_ge(params_in, at(params_in, l, 16 * N_PARAMS))
                for t in range(NT):
                    transposed_x("hT1", g_ch[:, G_X, :], t)

                for t in range(NT):
                    dve.wait_ge(*copied(("in", "fv", t), l))
                    last = v.tensor_tensor(gate_in[:, t, :], pt[t][:, T_FF:T_FF + 12],
                                           view(row, ROWS["fox_fgate_b"][0], 12), ALU.add)
                link(last)
                link(v.tensor_scalar(gate_e[:, :, :], gate_in[:, :, :], -1.0, None, ALU.mult))
                v.tensor_tensor(gate_e[:, :, :], gate_e[:, :, :], gate_in[:, :, :], ALU.min).then_inc(gate_abs, 1)
                dve.wait_ge(gate_ln, at(gate_ln, l, 1))
                v.scalar_tensor_tensor(DL[:, :, 0:NH], gate_in[:, :, 0:NH], 0.0, gate_e[:, :, 0:NH], ALU.min,
                                       ALU.subtract)
                link(v.scalar_tensor_tensor(DTs[:, :, :], gate_in[:, :, NH:], 0.0, gate_e[:, :, NH:], ALU.max,
                                            ALU.add))
                dve.wait_ge(a_step, at(a_step, l, 1))
                v.scalar_tensor_tensor(DL[:, :, NH:], DTs[:, :, :], -1.0,
                                       negA[:, :].unsqueeze(1).to_broadcast([P, NT, SH]), ALU.mult, ALU.mult
                                       ).then_inc(DL_ready, 1)
                dve.wait_ge(*full(("params",), l))
                v.tensor_copy(p_ch[:, :], bk(("params",))[:, 0:44]).then_inc(read(("params",)), 1)
                for t in range(NT):
                    for i in range(2):
                        gained(("memT", t, i), g_ch[:, G_MEM, 4 * i:4 * i + 4], MT[:, t, 4 * i:4 * i + 4, :])
                v.memset(xin[:, :, 0:3], 0.0).then_inc(pads, 1)

                def sum_squares(i, buf):
                    for t in range(NT):
                        dve.wait_ge(fd_sq, at(fd_sq, l, NT * i + t + 1))
                        v.tensor_reduce(ssf[:, t, 8 * i:8 * i + 8], view(buf, 512 * t, 8, HD), AX.X, ALU.add
                                        ).then_inc(fd_ss, 1)

                sum_squares(0, Yf)
                job = ("cum",)
                dve.wait_ge(*full(job, l))
                link(v.tensor_copy(CUM[:, :, :], bk(job)[:, 0:NT * 12].rearrange("p (t n) -> p t n", t=NT)))
                v.memset(FQ[:, :, 0:NH, HD:HD + 1], 1.0)
                v.memset(FQ[:, :, NH:, HD + 1:HD + 2], 1.0)
                v.tensor_scalar(FQ[:, :, 0:NH, HD + 1], CUM[:, :, 0:NH], HD ** 0.5, None, ALU.mult)
                v.tensor_scalar(FQ[:, :, NH:, HD], CUM[:, :, 0:NH], -HD ** 0.5, None, ALU.mult
                                ).then_inc(read(job), 1)
                for t in range(NT):
                    dve.wait_ge(fd_rs, at(fd_rs, l, t + 1))
                    link(v.tensor_tensor(FQ[:, t, :, 0:HD], view(pt[t], 0, 2 * NH, HD), bc(ssf[:, t, 0:8], 8, HD),
                                         ALU.mult))
                    fq = FQ[:, t, :, 0:HD].rearrange("p (b h) d -> p b h d", b=2)
                    gain = view(row, ROWS["fox_qn_g"][0], 2, HD)
                    v.tensor_tensor(fq, fq, gain.unsqueeze(2).to_broadcast([P, 2, NH, HD]), ALU.mult
                                    ).then_inc(FQ_ready, 1)

                def dilated_qk(t):
                    dve.wait_ge(fd_rs, at(fd_rs, l, NT + t + 1))
                    dq = view(pt[t], T_DQK, 2 * NH, HD)
                    link(v.tensor_tensor(dq, dq, bc(ssf[:, t, 8:16], 8, HD), ALU.mult))
                    d4 = view(pt[t], T_DQK, 2, NH, HD)
                    gain = view(row, ROWS["dil_qn_g"][0], 2, HD)
                    link(v.tensor_tensor(d4, d4, gain.unsqueeze(2).to_broadcast([P, 2, NH, HD]), ALU.mult))
                    cos = view(con, CONST["cos"][0] + 8 * t, 8).unsqueeze(1).to_broadcast([P, 8, 8])
                    sin = view(con, CONST["sin"][0] + 8 * t, 8).unsqueeze(1).to_broadcast([P, 8, 8])
                    v.tensor_tensor(rope[:, 0], dq[:, :, 0:8], cos, ALU.mult)
                    v.tensor_tensor(rope[:, 1], dq[:, :, 8:16], sin, ALU.mult)
                    v.tensor_tensor(rope[:, 2], dq[:, :, 8:16], cos, ALU.mult)
                    link(v.tensor_tensor(rope[:, 3], dq[:, :, 0:8], sin, ALU.mult))
                    v.tensor_tensor(dq[:, :, 0:8], rope[:, 0], rope[:, 1], ALU.subtract)
                    v.tensor_tensor(dq[:, :, 8:16], rope[:, 2], rope[:, 3], ALU.add).then_inc(DQ_ready, 1)

                def mask_scores(k):
                    fam = HEADS[k][0]
                    for t in range(NT):
                        w, job = (t + 1) * P, ("s", HEADS[k], t)
                        if fam == "fox":
                            mask = c_("causal")[:, S - w:S]
                        else:
                            mask = c_("dilated")[:, t * P:t * P + w]
                        dve.wait_ge(*full(job, l))
                        if k >= 2 and t == 0:
                            dve.wait_ge(*full(("pT", HEADS[k - 2]), l))
                        alone(dve)
                        v.tensor_tensor_reduce(out=SCO[:, k % 2, t, 0:w], in0=bk(job)[:, 0:w], in1=mask,
                                               scale=HD ** -0.5, scalar=-BIG, op0=ALU.add, op1=ALU.max,
                                               accum_out=smax[:, k % 2, t:t + 1]).then_inc(read(job), 1)
                        dve.wait_ge(*copied(job, l))
                        v.tensor_scalar(smax[:, k % 2, t:t + 1], smax[:, k % 2, t:t + 1], -1.0, None, ALU.mult
                                        ).then_inc(scores, 1)

                def normalize(p, total, done):
                    link(v.reciprocal(total, total))
                    v.tensor_scalar(p, p, total, None, ALU.mult).then_inc(done, 1)

                def conv(c):
                    dve.wait_ge(conv_tap, at(conv_tap, l, c + 1))
                    o = cv[:, c % 2, :]
                    for k in range(1, 4):
                        ins = v.scalar_tensor_tensor(o, xin[:, c, k:k + S], p_ch[:, 8 * k + c:8 * k + c + 1], o,
                                                     ALU.mult, ALU.add)
                        if k < 3:
                            link(ins)
                    ins.then_inc(conv_done, 1)

                def gate(c):
                    dve.wait_ge(conv_tanh, at(conv_tanh, l, c + 1))
                    v.scalar_tensor_tensor(xc[:, c, :], sig[:, c % 2, :], 1.0, cv[:, c % 2, :], ALU.add, ALU.mult
                                           ).then_inc(conv_gated, 1)

                for k in range(len(HEADS) + 1):
                    if k == 0:
                        sum_squares(1, sq)
                        dve.wait_ge(fd_ss, at(fd_ss, l, 2 * NT))
                    if k < len(HEADS):
                        mask_scores(k)
                        conv(k)
                    if k == 1:
                        for t in range(NT):
                            dilated_qk(t)
                    if k:
                        gate(k - 1)
                    for job in BETWEEN[k - 1] if k else ():
                        if job[0] == "kv" and job[1] < 2:
                            n, t = job[1:]
                            dve.wait_ge(k_rs, at(k_rs, l, NT * n + t + 1))
                            times_gain([K_tm[:, t, h * XD:(h + 1) * XD] for h in range(2)],
                                       ssk[:, t, 2 * n:2 * n + 2], "xa_kn_g").then_inc(k_normed, 1)
                    for job in BETWEEN[k]:
                        if job[0] == "kT":
                            n, t = job[1:]
                            copy4(job, KT[:, 4 * n:4 * n + 4, t * P:(t + 1) * P])
                    if k < len(HEADS):
                        for t in range(NT):
                            dve.wait_ge(exps, at(exps, l, 2 * k + t + 1))
                            normalize(SCO[:, k % 2, t, 0:(t + 1) * P], ssum[:, k % 2, t:t + 1], probs)

                def exponents(h):
                    job = ("L", h)
                    if h >= 2:
                        dve.wait_ge(M_ready, at(M_ready, l, h - 1))
                    dve.wait_ge(*full(job, l))
                    v.tensor_scalar(Ls[:, h % 2, 0:S], bk(job)[:, 0:S], CUM[:, 0, NH + h:NH + h + 1], 0.0,
                                    ALU.subtract, ALU.min)
                    v.tensor_scalar(Ls[:, h % 2, S:], bk(job)[:, P:S], CUM[:, 1, NH + h:NH + h + 1], 0.0,
                                    ALU.subtract, ALU.min).then_inc(read(job), 1)

                exponents(0)
                for g in range(2):
                    job = ("cb", g)
                    dve.wait_ge(*full(job, l))
                    v.scalar_tensor_tensor(CB[:, g, :], bk(job)[:, 0:3 * P], 0.25, tri, ALU.mult, ALU.mult
                                           ).then_inc(read(job), 1)
                for g in range(2):
                    dve.wait_ge(*copied(("cb", g), l))

                for h in range(SH):
                    if h + 1 < SH:
                        exponents(h + 1)
                    dve.wait_ge(decays, at(decays, l, h + 1))
                    if h >= 2:
                        dve.wait_ge(y_head, at(y_head, l, h - 1))
                    v.scalar_tensor_tensor(Ms[:, h % 2, 0:S], Ls[:, h % 2, 0:S], DTs[:, 0, h:h + 1],
                                           CB[:, h // 4, 0:S], ALU.mult, ALU.mult)
                    v.scalar_tensor_tensor(Ms[:, h % 2, S:], Ls[:, h % 2, S:], DTs[:, 1, h:h + 1],
                                           CB[:, h // 4, S:], ALU.mult, ALU.mult).then_inc(M_ready, 1)
                for t in range(NT):
                    dve.wait_ge(*copied(("xsT", t), l))
                    link(v.tensor_tensor(view(Y[:, t, :], 0, SH, SP_), view(XS[:, t, :], 0, SH, SP_),
                                         bc(r_("ssd_D"), SH, SP_), ALU.mult))
                    dve.wait_ge(*full(("y", t), l))
                    v.tensor_tensor(Y[:, t, :], Y[:, t, :], bk(("y", t))[:, :], ALU.add).then_inc(read(("y", t)), 1)
                    dve.wait_ge(z_tanh, at(z_tanh, l, t + 1))
                    e = sq[:, t * SI:(t + 1) * SI]
                    link(v.scalar_tensor_tensor(e, e, 1.0, pt[t][:, T_Z:T_Z + SI], ALU.add, ALU.mult))
                    link(v.scalar_tensor_tensor(Y[:, t, :], e, 0.5, Y[:, t, :], ALU.mult, ALU.mult))
                    v.tensor_tensor_reduce(out=ve[:, :], in0=Y[:, t, :], in1=Y[:, t, :], scale=1.0, scalar=0.0,
                                           op0=ALU.mult, op1=ALU.add, accum_out=ss[:, 4 + t:5 + t]).then_inc(y_ss, 1)
                for t in range(NT):
                    dve.wait_ge(y_rs, at(y_rs, l, t + 1))
                    v.tensor_scalar(Y[:, t, :], Y[:, t, :], ss[:, 4 + t:5 + t], None, ALU.mult).then_inc(Y_ready, 1)
                for t in range(NT):
                    gained(("ysT", t), p_ch[:, 40:44], mixT[:, t, 4:8, :])

                def residual(name, n, t):
                    job = (name, n, t)
                    dve.wait_ge(*full(job, l))
                    x = X[:, t, n * 512:(n + 1) * 512]
                    v.tensor_tensor(x, x, bk(job)[:, :], ALU.add).then_inc(read(job), 1)
                    if n == 1:
                        dve.wait_ge(*copied((name, 0, t), l))
                        dve.wait_ge(*copied((name, 1, t), l))
                        dve.sem_inc(X_ready, 1)

                residual("out1", 0, 0)
                residual("out1", 1, 0)
                residual("out1", 0, 1)
                transposed_x("hT2", g_ch[:, G_2, :], 0)
                residual("out1", 1, 1)
                transposed_x("hT2", g_ch[:, G_2, :], 1)

                def norm_q(t):
                    dve.wait_ge(q_rs, at(q_rs, l, t + 1))
                    times_gain([Q_tm[:, t, h * XD:(h + 1) * XD] for h in range(XH)], ssk[:, t, :], "xa_qn_g"
                               ).then_inc(q_normed, 1)

                def transposed_q(t):
                    for i in range(2):
                        copy4(("qT", t, i), QT[:, t, 4 * i:4 * i + 4, :])

                norm_q(0)
                transposed_q(0)
                for j in range(len(CROSS) + 1):
                    if j < len(CROSS):
                        job = ("xs", *CROSS[j])
                        dve.wait_ge(*full(job, l))
                        if j >= 2:
                            dve.wait_ge(*full(("xpT", *CROSS[j - 2]), l))
                        m = smax[:, j % 2, 0:1]
                        link(v.tensor_reduce(m, bk(job)[:, 0:S], AX.X, ALU.max))
                        v.tensor_scalar(m, m, -XD ** -0.5, None, ALU.mult).then_inc(xmax, 1)
                    if j == 2:
                        norm_q(1)
                    if j == 3:
                        transposed_q(1)
                    if j < len(CROSS):
                        dve.wait_ge(*copied(job, l))
                        normalize(SCO[:, j % 2, 0, :], ssum[:, j % 2, 0:1], xprobs)
                    if j in (6, 7):
                        residual("out2", j - 6, 0)
                dve.wait_ge(g3_in, 16)
                my_gain = g3[:, bass.ds(l, 1), :].rearrange("p a c -> p (a c)")
                residual("out2", 0, 1)
                transposed_x("xT", my_gain, 0)
                residual("out2", 1, 1)
                transposed_x("xT", my_gain, 1)

                job = ("router",)
                dve.wait_ge(*full(job, l))
                dve.wait_ge(x_rs, at(x_rs, l, 3 * NT))
                bias, w = view(row, ROWS["router_bg"][0], NG + NE), NG + NE
                for t in range(NT):
                    last = v.scalar_tensor_tensor(lg[:, t, :], bk(job)[:, t * w:(t + 1) * w], ss[:, 2 + t:3 + t], bias,
                                                  ALU.mult, ALU.add)
                link(last)
                dve.sem_inc(read(job), 1)

                def select(q):
                    mine = rank[:, :, bass.ds(q * QUAD, QUAD)].unsqueeze(3).to_broadcast([P, NT, QUAD, CAP])
                    places = slot_no[:, :].unsqueeze(1).unsqueeze(1).to_broadcast([P, NT, QUAD, CAP])
                    return v.tensor_tensor(SEL, mine, places, ALU.is_equal)

                def first_max(src, n, top, hot):
                    tmp = ties[:, :, 0:n]
                    link(v.tensor_reduce(top, src, AX.X, ALU.max))
                    for t in range(NT):
                        last = v.scalar_tensor_tensor(tmp[:, t], src[:, t], top[:, t], c_("down")[:, 0:n],
                                                      ALU.is_equal, ALU.mult)
                    link(last)
                    link(v.tensor_reduce(rt[:, :, 7:8], tmp, AX.X, ALU.max))
                    link(v.tensor_tensor(hot, tmp, rt[:, :, 7:8].to_broadcast([P, NT, n]), ALU.is_equal))

                gmax, m1, m2 = rt[:, :, 0:1], rt[:, :, 1:2], rt[:, :, 2:3]
                g_gate, e21, p1, p2 = rt[:, :, 3:4], rt[:, :, 4:5], rt[:, :, 5:6], rt[:, :, 6:7]
                first_max(lg[:, :, 0:NG], NG, gmax, rg[:, :, 0, :])
                v.tensor_tensor(rg[:, :, 1, :], lg[:, :, 0:NG], gmax.to_broadcast([P, NT, NG]), ALU.subtract
                                ).then_inc(g_shift, 1)
                link(v.tensor_scalar(rg[:, :, 2, :], rg[:, :, 0, :], 1.0, BIG, ALU.subtract, ALU.mult))
                link(v.tensor_tensor(em[:, :, :].rearrange("p t (g e) -> p t g e", g=NG),
                                     lg[:, :, NG:].rearrange("p t (g e) -> p t g e", g=NG),
                                     rg[:, :, 2, :].unsqueeze(3).to_broadcast([P, NT, NG, EPG]), ALU.add))
                first_max(em[:, :, :], NE, m1, oh[:, 0])
                link(v.scalar_tensor_tensor(em[:, :, :], oh[:, 0], -BIG, em[:, :, :], ALU.mult, ALU.add))
                first_max(em[:, :, :], NE, m2, oh[:, 1])
                v.tensor_tensor(e21, m2, m1, ALU.subtract).then_inc(e_shift, 1)
                v.tensor_tensor(chosen[:, :, :], oh[:, 0], oh[:, 1], ALU.add).then_inc(chosen_ready, 1)
                job = ("rank",)
                dve.wait_ge(*full(job, l))
                link(v.tensor_tensor(rank[:, :, :], chosen[:, :, :],
                                     bk(job)[:, 0:NT * NE].rearrange("p (t n) -> p t n", t=NT), ALU.mult))
                link(v.tensor_scalar(rank[:, :, :], rank[:, :, :], 1.0, None, ALU.subtract))
                link(v.tensor_copy(slot_no[:, :], c_("slots")))
                dve.sem_inc(places_set, 1)
                select(0).then_inc(sel_ready, 1)
                dve.sem_inc(read(("rank",)), 1)

                def gates_and_passes():
                    dve.wait_ge(g_exp, at(g_exp, l, 1))
                    link(v.tensor_reduce(g_gate, rg[:, :, 1, :], AX.X, ALU.add))
                    dve.wait_ge(e_exp, at(e_exp, l, 1))
                    link(v.tensor_scalar(p1, e21, 1.0, None, ALU.add))
                    link(v.tensor_tensor(p1, p1, g_gate, ALU.mult))
                    link(v.reciprocal(p1, p1))
                    link(v.tensor_tensor(p2, p1, e21, ALU.mult))
                    link(v.tensor_tensor(gates[:, :, :], oh[:, 0], p1.to_broadcast([P, NT, NE]), ALU.mult))
                    link(v.tensor_tensor(em[:, :, :], oh[:, 1], p2.to_broadcast([P, NT, NE]), ALU.mult))
                    link(v.tensor_tensor(gates[:, :, :], gates[:, :, :], em[:, :, :], ALU.add))
                    job = ("total",)
                    dve.wait_ge(*full(job, l))
                    link(v.tensor_reduce(passes[:, 1:2], bk(job)[:, 0:NE], AX.X, ALU.max))
                    link(v.tensor_tensor(over[:, :], passes[:, 1:2].to_broadcast([P, 8]), c_("caps"), ALU.is_gt))
                    link(v.tensor_reduce(passes[:, 1:2], over[:, :], AX.X, ALU.add))
                    link(v.tensor_tensor(passes[:, 0:1], passes[:, 0:1], passes[:, 1:2], ALU.add))
                    v.tensor_copy(passes_i[:, bass.ds(l + 1, 1)], passes[:, 0:1]).then_inc(passes_known, 1)
                    dve.sem_inc(read(("total",)), 1)
                    assert steps[0] == V_STEPS, ("V", steps)

                def quad(q, quads, first=False):
                    n_steps = [0]

                    def step(ins):
                        n_steps[0] += 1
                        ins.then_inc(v_moe, 1)
                        dve.wait_ge(v_moe, quads * V_MOE + n_steps[0])

                    my_gates = gates[:, :, bass.ds(q * QUAD, QUAD)].unsqueeze(3).to_broadcast([P, NT, QUAD, CAP])
                    if not first:
                        select(q).then_inc(sel_ready, 1)
                    dve.wait_ge(sel_ready, quads + 1)
                    for i in range(4):
                        dve.wait_ge(gath_full, quads * 4 + i + 1)
                        v.tensor_tensor(XG[:, 2 * i:2 * i + 2, :],
                                        view(bank[B_GATH[i % 2]], i // 2 * 2 * P, 2, P),
                                        bc(my_gain[:, 2 * i:2 * i + 2], 2, P), ALU.mult).then_inc(XG_ready, 1)
                    if first:
                        gates_and_passes()
                    v.tensor_tensor(SELG, SEL, my_gates, ALU.mult).then_inc(selg_ready, 1)
                    dve.wait_ge(up_tanh, quads + 1)
                    step(v.scalar_tensor_tensor(SIGM, SIGM, 1.0, bank[B_UP[0]][:, :], ALU.add, ALU.mult))
                    dve.wait_ge(units_used, quads * MOE_UNITS + MOE_UNITS + 8)
                    v.scalar_tensor_tensor(HID, SIGM.rearrange("p (q c) -> p c q", c=4), 0.5,
                                           bank[B_UP[1]][:, :].rearrange("p (q c) -> p c q", c=4), ALU.mult, ALU.mult
                                           ).then_inc(hid_ready, 1)
                    for i in range(4):
                        t, n = i // 2, i % 2
                        dve.wait_ge(scat_full, quads * 4 + i + 1)
                        x = X[:, t, n * 512:(n + 1) * 512]
                        last = v.tensor_tensor(x, x, bank[B_SCAT[i]][:, :], ALU.add)
                        if n == 1:
                            last.then_inc(x_added, 1)
                    dve.wait_ge(x_added, quads * NT + NT + NT)
                    assert n_steps[0] == V_MOE

                def new_pass(passes_before):
                    v.tensor_scalar(slot_no[:, :], slot_no[:, :], float(CAP), None, ALU.add).then_inc(places_set, 1)
                    dve.wait_ge(places_set, passes_before + 1)
                    alone(dve)
                moe_quads(dve, l, quad, head=lambda q, quads: quad(q, quads, first=True), new_pass=new_pass)
                dve.sem_inc(vector_layer, 1)

        @block.tensor
        def _(pe):
            def mm(dst, lhsT, rhs, start=True, stop=True):
                return nc.tensor.matmul(dst, lhsT, rhs, start=start, stop=stop)

            pe.wait_ge(const_in, 16)
            with pe.Fori(0, DEPTH) as l:
                pe.wait_ge(passes_known, at(passes_known, l, 1))
                moe_turns = load_passes(pe, l) * (NQ * MOE_TURNS)
                turn = [pe.snap(moe_turns + l * (DENSE_TURNS - short)) for short in range(2)]
                pe.wait_ge(vector_layer, at(vector_layer, l, 1))

                def transposes(job, srcs, last_wait=lambda eng: None):
                    pe.wait_ge(*free(job, l))
                    last_wait(pe)
                    for i, src in enumerate(srcs):
                        last = nc.tensor.transpose(bk(job)[0:src.shape[1], i * P:i * P + src.shape[0]], src,
                                                   ident[0:src.shape[0], 0:src.shape[0]])
                    last.then_inc(filled(job), 1)

                def arrived(unit):
                    n = DENSE.index(unit)
                    pe.wait_ge(landed[n % SLOTS], (turn[SHORT[n % SLOTS]] + n // SLOTS + 1) * 16)
                    if unit[0] == "fv":
                        pe.wait_ge(dt_in, at(dt_in, l, 16))
                    return ring_view(n % SLOTS, IN_COLS.get(unit[0], (0, 512))[1])

                def tile_job(job, unit, t, lhs):
                    w = arrived(unit)
                    pe.wait_ge(*free(job, l))
                    for c in range(KC):
                        last = mm(bk(job)[:, 0:w.shape[2]], lhs[:, t, c, :], w[:, c, :], start=c == 0, stop=c == KC - 1)
                    last.then_inc(filled(job), 1)

                def both_copied(name, t):
                    for i in range(2):
                        pe.wait_ge(*copied((name, t, i), l))

                def transpose_h(k, name, t):
                    pe.wait_ge(H_ready, at(H_ready, l, NT * k + (NT if k == 0 else t + 1)))
                    for i in range(2):
                        transposes((name, t, i), [H[:, t, 4 * i + j, :] for j in range(4)])

                for t in range(NT):
                    transpose_h(0, "hT1", t)
                for n in IN_FIRST:
                    for t in range(NT):
                        both_copied("hT1", t)
                        tile_job(("in", n, t), (n, 0), t, HT)
                pe.wait_ge(params_in, at(params_in, l, 16 * N_PARAMS))
                transposes(("params",), [p_rows[:, :]], last_wait=alone)
                pe.wait_ge(MN_ready, at(MN_ready, l, 1))
                for t in range(NT):
                    for i in range(2):
                        transposes(("memT", t, i), [MN[:, t, 4 * i + j, :] for j in range(4)])
                job = ("cum",)
                pe.wait_ge(DL_ready, at(DL_ready, l, 1))
                pe.wait_ge(*free(job, l))
                mm(bk(job)[:, 0:12], tri[:, 0:P], DL[:, 0, :])
                mm(bk(job)[:, 12:24], ones, DL[:, 0, :], stop=False)
                mm(bk(job)[:, 12:24], tri[:, 0:P], DL[:, 1, :], start=False).then_inc(filled(job), 1)
                for i in range(4):
                    job = ("xbc", i)
                    w = arrived(("xbc", i // 2))
                    pe.wait_ge(*free(job, l))
                    for j in range(2):
                        c0 = (i % 2 * 2 + j) * P
                        for c in range(KC):
                            last = mm(bk(job)[:, j * S:(j + 1) * S], w[:, c, c0:c0 + P], HT[:, :, c, :],
                                      start=c == 0, stop=c == KC - 1)
                    last.then_inc(filled(job), 1)

                for t in range(NT):
                    pe.wait_ge(FQ_ready, at(FQ_ready, l, t + 1))
                    for i in range(2):
                        transposes(("fT", t, i), [FQ[:, t, 4 * i + j, :] for j in range(4)])
                for n in IN_THEN:
                    for t in range(NT):
                        tile_job(("in", n, t), (n, 0), t, HT)
                for t in range(NT):
                    both_copied("fT", t)
                    both_copied("memT", t)

                def score(k):
                    fam, h = HEADS[k]
                    for t in range(NT):
                        job, w = ("s", HEADS[k], t), (t + 1) * P
                        pe.wait_ge(*free(job, l))
                        if fam == "fox":
                            q, kk = FQT[0:HD + 2, h, t * P:(t + 1) * P], FQT[0:HD + 2, NH + h, 0:w]
                        else:
                            r = slice(HD * (h % 2), HD * (h % 2) + HD)
                            q, kk = DQT[r, h // 2, t * P:(t + 1) * P], DQT[r, 2 + h // 2, 0:w]
                        mm(bk(job)[:, 0:w], q, kk).then_inc(filled(job), 1)

                def spread(h):
                    job = ("L", h)
                    pe.wait_ge(*free(job, l))
                    d = [DL[:, t, NH + h:NH + h + 1].to_broadcast([P, P]) for t in range(NT)]
                    mm(bk(job)[:, 0:S], d[0], tri[:, 0:S], stop=False)
                    mm(bk(job)[:, P:S], d[1], tri[:, 0:P], start=False).then_inc(filled(job), 1)

                for k in range(len(HEADS) + 1):
                    if k == NH:
                        for t in range(NT):
                            pe.wait_ge(*copied(("dT", t), l))
                    if k < len(HEADS):
                        score(k)
                    for job in BETWEEN[k]:
                        if job[0] == "kv":
                            tile_job(job, ("kv", job[1]), job[2], MT)
                        elif job[0] == "kT":
                            n, t = job[1:]
                            pe.wait_ge(k_normed, at(k_normed, l, NT * n + t + 1))
                            transposes(job, [K_tm[:, t, j * P:(j + 1) * P] for j in range(4)])
                        else:
                            t = job[1]
                            pe.wait_ge(DQ_ready, at(DQ_ready, l, t + 1))
                            transposes(job, [pt[t][:, T_DQK + j * P:T_DQK + (j + 1) * P] for j in range(4)])
                    if k == len(HEADS):
                        for h in range(L_AHEAD):
                            spread(h)
                    if k == 0:
                        continue
                    b = (k - 1) % 2
                    pe.wait_ge(probs, at(probs, l, 2 * k))
                    transposes(("pT", HEADS[k - 1]), [SCO[:, b, 0, 0:P], SCO[:, b, 1, 0:P], SCO[:, b, 1, P:S]])
                    if k % 2 == 0:
                        job = ("o", HEADS[k - 1])
                        pe.wait_ge(*free(job, l))
                        for k2 in (k - 2, k - 1):
                            fam, h = HEADS[k2]
                            pe.wait_ge(*copied(("pT", HEADS[k2]), l))
                            r = slice(HD * (k2 % 2), HD * (k2 % 2) + HD)
                            v0 = (T_FV if fam == "fox" else T_DV) + HD * h
                            mm(bk(job)[r, 0:S], pt[0][:, v0:v0 + HD], PT[:, k2 % 2, 0:S], stop=False)
                            last = mm(bk(job)[r, P:S], pt[1][:, v0:v0 + HD], PT[:, k2 % 2, S:3 * P], start=False)
                        last.then_inc(filled(job), 1)

                pe.wait_ge(conv_gated, at(conv_gated, l, KC))
                for t in range(NT):
                    transposes(("xsT", t), [xc[:, c, t * P:(t + 1) * P] for c in range(4)])
                for g in range(2):
                    job, Bg, Cg = ("cb", g), xc[:, 4 + g, :], xc[:, 6 + g, :]
                    pe.wait_ge(*free(job, l))
                    mm(bk(job)[:, 0:S], Bg[:, 0:P], Cg)
                    mm(bk(job)[:, S:3 * P], Bg[:, P:S], Cg[:, P:S]).then_inc(filled(job), 1)

                for t in range(NT):
                    pe.wait_ge(*copied(("xsT", t), l))
                    pe.wait_ge(*free(("y", t), l))
                for h in range(SH):
                    if h + L_AHEAD < SH:
                        spread(h + L_AHEAD)
                    pe.wait_ge(M_ready, at(M_ready, l, h + 1))
                    c = slice(SP_ * h, SP_ * (h + 1))
                    M = Ms[:, h % 2, :]
                    y0 = mm(bk(("y", 0))[:, c], M[:, 0:P], XS[:, 0, c])
                    if h == SH - 1:
                        y0.then_inc(filled(("y", 0)), 1)
                    mm(bk(("y", 1))[:, c], M[:, P:S], XS[:, 0, c], stop=False)
                    y1 = mm(bk(("y", 1))[:, c], M[:, S:], XS[:, 1, c], start=False)
                    y1.then_inc(filled(("y", 1)) if h == SH - 1 else y_head, 1)
                tile_job(("kv", 3, 1), ("kv", 3), 1, MT)
                for t in range(NT):
                    pe.wait_ge(Y_ready, at(Y_ready, l, t + 1))
                    transposes(("ysT", t), [Y[:, t, j * P:(j + 1) * P] for j in range(4)])
                for k in (1, 3, 5, 7):
                    pe.wait_ge(*copied(("o", HEADS[k]), l))
                pe.wait_ge(*copied(("ysT", 0), l))
                for n in range(2):
                    tile_job(("out1", n, 0), ("w_out", n), 0, mixT)
                pe.wait_ge(*copied(("ysT", 1), l))
                tile_job(("out1", 0, 1), ("w_out", 0), 1, mixT)
                transpose_h(1, "hT2", 0)
                tile_job(("out1", 1, 1), ("w_out", 1), 1, mixT)

                def transpose_q(t):
                    pe.wait_ge(q_normed, at(q_normed, l, t + 1))
                    for i in range(2):
                        transposes(("qT", t, i), [Q_tm[:, t, (4 * i + j) * P:(4 * i + j + 1) * P] for j in range(4)])

                both_copied("hT2", 0)
                tile_job(("q", 0, 0), ("wq", 0), 0, HT)
                transpose_h(1, "hT2", 1)
                tile_job(("q", 1, 0), ("wq", 1), 0, HT)
                both_copied("hT2", 1)
                tile_job(("q", 0, 1), ("wq", 0), 1, HT)
                transpose_q(0)
                for n in range(2):
                    both_copied("kT", n)
                for j in range(len(CROSS) + 1):
                    if j < len(CROSS):
                        t, h = CROSS[j]
                        job = ("xs", t, h)
                        if h == 0:
                            both_copied("qT", t)
                        pe.wait_ge(*free(job, l))
                        for c in (2 * h, 2 * h + 1):
                            last = mm(bk(job)[:, 0:S], QT[:, t, c, :], KT[:, c, :], start=c == 2 * h,
                                      stop=c == 2 * h + 1)
                        last.then_inc(filled(job), 1)
                    if j == 0:
                        tile_job(("q", 1, 1), ("wq", 1), 1, HT)
                    if j == 3:
                        transpose_q(1)
                    if j == 5:
                        for h in range(XH):
                            pe.wait_ge(*copied(("xo", 0, h), l))
                    if j in (5, 6):
                        tile_job(("out2", j - 5, 0), ("wo", j - 5), 0, mixT)
                    if j == 0:
                        continue
                    t, h = CROSS[j - 1]
                    b = (j - 1) % 2
                    pe.wait_ge(xprobs, at(xprobs, l, j))
                    transposes(("xpT", t, h), [SCO[:, b, 0, m * P:(m + 1) * P] for m in range(2)])
                    job = ("xo", t, h)
                    pe.wait_ge(*copied(("xpT", t, h), l))
                    pe.wait_ge(*free(job, l))
                    for i in range(2):
                        d0 = h * XD + i * P
                        for m in range(2):
                            last = mm(bk(job)[:, i * P:(i + 1) * P], VM[:, m, d0:d0 + P],
                                      PT[:, b, m * P:(m + 1) * P], start=m == 0, stop=m == 1)
                    last.then_inc(filled(job), 1)
                for h in range(XH):
                    pe.wait_ge(*copied(("xo", 1, h), l))

                def transpose_x(t):
                    pe.wait_ge(X_ready, at(X_ready, l, NT + t + 1))
                    dealt = X[:, t, :].rearrange("p (q c) -> p c q", c=KC)
                    for i in range(2):
                        transposes(("xT", t, i), [dealt[:, 4 * i + j, :] for j in range(4)])

                def logits(t):
                    both_copied("xT", t)
                    w = NG + NE
                    for c in range(KC):
                        last = mm(bk(("router",))[:, t * w:(t + 1) * w], HT[:, t, c, :], wr[:, c, :],
                                  start=c == 0, stop=c == KC - 1)
                    return last

                tile_job(("out2", 0, 1), ("wo", 0), 1, mixT)
                transpose_x(0)
                tile_job(("out2", 1, 1), ("wo", 1), 1, mixT)
                pe.wait_ge(*free(("router",), l))
                logits(0)
                transpose_x(1)
                logits(1).then_inc(filled(("router",)), 1)
                job = ("rank",)
                pe.wait_ge(chosen_ready, at(chosen_ready, l, 1))
                pe.wait_ge(*free(job, l))
                mm(bk(job)[:, 0:NT * NE], tri[:, 0:P], chosen_flat, stop=False)
                mm(bk(job)[:, NE:NT * NE], ones, chosen[:, 0, :], start=False).then_inc(filled(job), 1)
                job = ("total",)
                pe.wait_ge(*free(job, l))
                for t in range(NT):
                    last = mm(bk(job)[:, 0:NE], ones, chosen[:, t, :], start=t == 0, stop=t == NT - 1)
                last.then_inc(filled(job), 1)
                pe.wait_ge(H_ready, at(H_ready, l, 3 * NT))
                alone(pe)

                def quad(q, quads, head=False):

                    def landed_unit(n):
                        slot = moe_slot(n, head)
                        if slot is None:
                            i = SPARE_UNITS.index(n)
                            pe.wait_ge(spare_in[i], at(spare_in[i], l, 16))
                            return spare[i].rearrange("p (e c n) -> p e c n", e=QUAD, n=512)
                        pe.wait_ge(landed[slot], landed_by(n, slot, head, l, quads) * 16)
                        return ring[:, slot, :].rearrange("p (e c n) -> p e c n", e=QUAD, n=512)

                    pe.wait_ge(sel_ready, quads + 1)
                    sel = SEL.rearrange("p t e s -> p t (e s)")
                    selg = SELG.rearrange("p t e s -> p t (e s)")

                    def gather(piece):
                        for c in range(2):
                            col = (piece // 2 * 2 + c) * P
                            for t in range(NT):
                                last = mm(bank[B_GATH[piece % 2]][:, col:col + P], H[:, t, 2 * piece + c, :],
                                          sel[:, t, :], start=t == 0, stop=t == NT - 1)
                        last.then_inc(gath_full, 1)

                    gather(0)
                    gather(1)
                    for n in range(8):
                        if n < 4:
                            pe.wait_ge(XG_ready, quads * 4 + n + 1)
                        u = landed_unit(n)
                        for c in range(2):
                            k = n % 4 * 2 + c
                            for e in range(QUAD):
                                r = slice(CAP * e, CAP * (e + 1))
                                last = mm(bank[B_UP[n // 4]][r, :], XG[:, k, r], u[:, e, c, :],
                                          start=k == 0, stop=k == KC - 1)
                        last.then_inc(units_used, 1)
                        if n < 2:
                            gather(n + 2)
                        if n == 3:
                            pe.wait_ge(selg_ready, quads + 1)
                            for t in range(NT):
                                last = nc.tensor.transpose(bank[B_SELT][:, t * P:(t + 1) * P], selg[:, t, :], ident)
                            last.then_inc(selt_full, 1)
                    pe.wait_ge(hid_ready, quads + 1)
                    for j in range(4):
                        last = nc.tensor.transpose(bank[B_HIDT][:, j * P:(j + 1) * P], HID[:, j, :], ident)
                    last.then_inc(hidt_full, 1)
                    pe.wait_ge(HIDT_ready, quads + 1)
                    for n in range(4):
                        u = landed_unit(8 + n)
                        for c in range(2):
                            for e in range(QUAD):
                                r = slice(CAP * e, CAP * (e + 1))
                                last = mm(bank[B_DOWN[c]][r, :], HIDT[:, n, r], u[:, e, c, :],
                                          start=n == 0, stop=n == 3)
                        last.then_inc(units_used, 1)
                    pe.wait_ge(SELT_ready, quads + 1)
                    pe.wait_ge(YS_ready, quads + 1)
                    for i in range(4):
                        t, n = i // 2, i % 2
                        mm(bank[B_SCAT[i]][:, :], SELT[:, t * P:(t + 1) * P], YS[:, n * 512:(n + 1) * 512]
                           ).then_inc(scat_full, 1)
                moe_quads(pe, l, quad, head=lambda q, quads: quad(q, quads, head=True))


def constants():
    import numpy as np
    p = np.arange(P)[:, None]
    j = np.arange(P)[None, :]
    con = np.zeros((P, CONST_W), np.float32)

    def put(name, v):
        o, w = CONST[name]
        con[:, o:o + w] = v
    put("ident", p == j)
    tri = (p <= j).astype(np.float32)
    put("tri", np.concatenate([tri, np.ones((P, P)), tri], 1))
    put("causal", np.concatenate([np.zeros((P, P)), np.where(j <= p, 0.0, -BIG)], 1))
    dil = []
    for t in range(NT):
        d = (t * P + p) - np.arange((t + 1) * P)[None, :]
        m = sum(((d >= 0) & (d <= w) & (d % r == 0)).astype(np.float64) for w, r in ((128, 1), (512, 4), (2048, 16)))
        dil.append(np.where(m > 0, HD ** 0.5 * np.log(np.maximum(m, 1)), -BIG))
    put("dilated", np.concatenate(dil, 1))
    inv = np.power(np.float32(500000.0), -2.0 * np.arange(8, dtype=np.float32) / np.float32(16)).astype(np.float32)
    ang = np.arange(S, dtype=np.float32)[:, None] * inv[None, :]
    for name, f in (("cos", np.cos), ("sin", np.sin)):
        put(name, f(ang).astype(np.float32).reshape(NT, P, 8).transpose(1, 0, 2).reshape(P, NT * 8))
    put("slots", np.arange(CAP)[None, :])
    put("caps", (np.arange(8) * CAP)[None, :])
    put("down", (NE - np.arange(NE))[None, :])
    return con


WEIGHTS = ["x", "mem", "w_in", "w_out", "xa_wq", "xa_wkv", "xa_wo", "exp_w1", "exp_w3", "exp_w2"]


def lay_out(inputs):
    import numpy as np
    g = {n: np.asarray(v) for n, v in inputs.items()}
    arrays = {n: np.ascontiguousarray(g[n]) for n in WEIGHTS}
    arrays["rows"] = np.concatenate([g[n] for n in ROWS], axis=1)
    arrays["chan"] = np.concatenate([g["ssd_conv_w"].reshape(DEPTH, -1, P), g["ssd_conv_b"].reshape(DEPTH, -1, P),
                                     g["ssd_norm_g"].reshape(DEPTH, -1, P)], axis=1)
    gains = np.stack([g["norm1_g"], g["mem_norm_g"], g["norm2_g"]], axis=1).reshape(DEPTH, 3, P, KC)
    arrays["gains"] = np.ascontiguousarray(gains.transpose(0, 2, 1, 3)).reshape(DEPTH, P, 3 * KC)
    arrays["gain3"] = np.ascontiguousarray(g["norm3_g"].reshape(DEPTH, P, KC).transpose(1, 0, 2)).reshape(P, -1)
    arrays["router"] = np.concatenate([g["router_wg"], g["router_we"]], axis=2).reshape(DEPTH, P, -1)
    arrays["const"] = constants()
    return arrays


def kernel(**inputs):
    import concourse.bacc as bacc
    from concourse.bass_utils import run_bass_kernel_spmd

    nc = bacc.Bacc("TRN2", target_bir_lowering=False, num_devices=1)
    arrays = lay_out(inputs)
    aps = {n: nc.dram_tensor(n, v.shape, mybir.dt.from_np(v.dtype), kind="ExternalInput").ap()
           for n, v in arrays.items()}
    out = nc.dram_tensor("out", (1, S, D), F32, kind="ExternalOutput").ap()
    trunk(nc, aps, out)
    r = run_bass_kernel_spmd(nc, [arrays], core_ids=[0])
    return r.results[0]["out"]
```
